# Optimizing a Trainium2 kernel written in Bass

```python
import math
import jax, jax.numpy as jnp
from jax import lax
import numpy as np

D_MODEL = 1024
BATCH = 1
SEQ = 1024
DEPTH = 2

BLOCK = 128
A_WIDTH = D_MODEL // 2
A_HEAD_DIM = 64
A_HEADS = A_WIDTH // A_HEAD_DIM
A_KV_HEADS = A_HEADS // 4
WINDOW = 128
B_WIDTH = D_MODEL - A_WIDTH
SSM_GROUP = 16
SSM_GROUPS = B_WIDTH // SSM_GROUP
SSM_STATE = 64
DT_MIN = 0.001
DT_MAX = 0.1
C_WIDTH = D_MODEL
C_HEADS = A_HEADS
C_HEAD_DIM = C_WIDTH // C_HEADS
C_KV_HEADS = C_HEADS // 4
IDX_HEADS = 8
IDX_DIM = 64
TOPK_MAX = 256
NUM_BUCKETS = 32
REL_MAX_DIST = 1024
EPS = 1e-6
NEG_INF = -1e30

EVEN_SPLITS = (A_WIDTH, A_KV_HEADS * A_HEAD_DIM, A_KV_HEADS * A_HEAD_DIM, A_WIDTH, B_WIDTH, B_WIDTH)
ODD_SPLITS = (C_WIDTH, C_KV_HEADS * C_HEAD_DIM, C_KV_HEADS * C_HEAD_DIM, C_WIDTH,
              IDX_HEADS * IDX_DIM, IDX_DIM, IDX_HEADS)
N_EVEN = (DEPTH + 1) // 2
N_ODD = DEPTH // 2


def rms_norm(x, g):
    xf = x.astype(jnp.float32)
    y = xf * lax.rsqrt(jnp.mean(xf * xf, axis=-1, keepdims=True) + EPS)
    return (y * g.astype(jnp.float32)).astype(x.dtype)

def split_cols(z, sizes):
    idx = np.cumsum(sizes)[:-1].tolist()
    return jnp.split(z, idx, axis=-1)

def t5_bucket(dist):
    n = jnp.maximum(dist, 0)
    max_exact = NUM_BUCKETS // 2
    nf = jnp.maximum(n, 1).astype(jnp.float32)
    large = max_exact + (jnp.log(nf / max_exact) / math.log(REL_MAX_DIST / max_exact)
                         * (NUM_BUCKETS - max_exact)).astype(jnp.int32)
    large = jnp.minimum(large, NUM_BUCKETS - 1)
    return jnp.where(n < max_exact, n, large)

def swa_sink_attention(q, k, v, sinks, rel_bias):
    bsz, L, H, Dh = q.shape
    hkv = k.shape[2]
    G = H // hkv
    nb = L // BLOCK
    qb = q.reshape(bsz, nb, BLOCK, hkv, G, Dh)
    kb = k.reshape(bsz, nb, BLOCK, hkv, Dh)
    vb = v.reshape(bsz, nb, BLOCK, hkv, Dh)
    k_band = jnp.concatenate([jnp.concatenate([jnp.zeros_like(kb[:, :1]), kb[:, :-1]], axis=1), kb], axis=2)
    v_band = jnp.concatenate([jnp.concatenate([jnp.zeros_like(vb[:, :1]), vb[:, :-1]], axis=1), vb], axis=2)
    logits = jnp.einsum('bnqhgd,bnkhd->bnhgqk', qb, k_band).astype(jnp.float32) * (Dh ** -0.5)
    i = jnp.arange(BLOCK, dtype=jnp.int32)[:, None]
    j = jnp.arange(2 * BLOCK, dtype=jnp.int32)[None, :]
    d = i + BLOCK - j
    in_window = (d >= 0) & (d < WINDOW)
    first = (jnp.arange(nb) == 0)[:, None, None] & (j < BLOCK)[None]
    mask = in_window[None] & ~first
    bias = rel_bias[t5_bucket(d)].astype(jnp.float32)
    bias = bias.transpose(2, 0, 1).reshape(hkv, G, BLOCK, 2 * BLOCK)
    logits = jnp.where(mask[None, :, None, None], logits + bias, NEG_INF)
    sink = jnp.broadcast_to(sinks.astype(jnp.float32).reshape(1, 1, hkv, G, 1, 1), logits.shape[:-1] + (1,))
    p = jax.nn.softmax(jnp.concatenate([logits, sink], axis=-1), axis=-1)[..., :-1]
    out = jnp.einsum('bnhgqk,bnkhd->bnqhgd', p.astype(v.dtype), v_band)
    return out.reshape(bsz, L, H * Dh)

def ssm_combine(e1, e2):
    a1r, a1i, b1r, b1i = e1
    a2r, a2i, b2r, b2i = e2
    ar = a1r * a2r - a1i * a2i
    ai = a1r * a2i + a1i * a2r
    br = a2r * b1r - a2i * b1i + b2r
    bi = a2r * b1i + a2i * b1r + b2i
    return (ar, ai, br, bi)

def s5_mixer(u, log_dt, a_re, a_im, b_re, b_im, c_re, c_im, d_skip, glu_w, glu_b):
    bsz, L, W = u.shape
    G, P = a_re.shape
    ug = u.reshape(bsz, L, G, W // G)
    dt = jnp.exp(log_dt)[:, None]
    mag = jnp.exp(a_re * dt)
    ang = a_im * dt
    ab_re = mag * jnp.cos(ang)
    ab_im = mag * jnp.sin(ang)
    den = a_re * a_re + a_im * a_im
    n_re = ab_re - 1.0
    n_im = ab_im
    f_re = (n_re * a_re + n_im * a_im) / den
    f_im = (n_im * a_re - n_re * a_im) / den
    bb_re = f_re[..., None] * b_re - f_im[..., None] * b_im
    bb_im = f_re[..., None] * b_im + f_im[..., None] * b_re
    bu_re = jnp.einsum('blgh,gph->blgp', ug, bb_re)
    bu_im = jnp.einsum('blgh,gph->blgp', ug, bb_im)
    at_re = jnp.broadcast_to(ab_re[None, None], (1, L, G, P))
    at_im = jnp.broadcast_to(ab_im[None, None], (1, L, G, P))
    _, _, x_re, x_im = lax.associative_scan(ssm_combine, (at_re, at_im, bu_re, bu_im), axis=1)
    y = (jnp.einsum('blgp,ghp->blgh', x_re, c_re) - jnp.einsum('blgp,ghp->blgh', x_im, c_im)
         + d_skip * ug)
    y = jax.nn.gelu(y.reshape(bsz, L, W))
    h = y @ glu_w + glu_b
    return h[..., :W] * jax.nn.sigmoid(h[..., W:])

def dsa_attention(q, k, v, qi, ki, wi, rel_bias):
    bsz, L, H, Dh = q.shape
    hkv = k.shape[2]
    G = H // hkv
    nb = L // BLOCK
    topk = min(TOPK_MAX, L // 4)
    qb = q.reshape(bsz, nb, BLOCK, hkv, G, Dh).transpose(1, 0, 2, 3, 4, 5)
    qib = qi.reshape(bsz, nb, BLOCK, IDX_HEADS, IDX_DIM).transpose(1, 0, 2, 3, 4)
    wib = wi.reshape(bsz, nb, BLOCK, IDX_HEADS).transpose(1, 0, 2, 3)
    starts = jnp.arange(nb, dtype=jnp.int32) * BLOCK
    key_pos = jnp.arange(L, dtype=jnp.int32)

    def one_block(args):
        q_blk, qi_blk, w_blk, start = args
        t = start + jnp.arange(BLOCK, dtype=jnp.int32)
        rel = jax.nn.relu(jnp.einsum('bqhd,bsd->bqhs', qi_blk, ki).astype(jnp.float32) * (IDX_DIM ** -0.5))
        score = jnp.einsum('bqhs,bqh->bqs', rel, w_blk.astype(jnp.float32))
        score = jnp.where(key_pos[None, None, :] <= t[None, :, None], score, NEG_INF)
        _, idx = lax.top_k(score, topk)
        valid = idx <= t[None, :, None]
        k_sel = jax.vmap(lambda kk, ii: kk[ii])(k, idx)
        v_sel = jax.vmap(lambda vv, ii: vv[ii])(v, idx)
        logits = jnp.einsum('bqhgd,bqkhd->bqhgk', q_blk, k_sel).astype(jnp.float32) * (Dh ** -0.5)
        bias = rel_bias[t5_bucket(t[None, :, None] - idx)].astype(jnp.float32)
        bias = bias.reshape(bsz, BLOCK, topk, hkv, G).transpose(0, 1, 3, 4, 2)
        logits = jnp.where(valid[:, :, None, None, :], logits + bias, NEG_INF)
        p = jax.nn.softmax(logits, axis=-1).astype(v.dtype)
        return jnp.einsum('bqhgk,bqkhd->bqhgd', p, v_sel)

    out = lax.map(one_block, (qb, qib, wib, starts))
    return out.transpose(1, 0, 2, 3, 4, 5).reshape(bsz, L, H * Dh)

def even_layer(hn, rel_bias, w_in, w_out, q_g, k_g, sinks, log_dt, a_re, a_im, b_re, b_im,
               c_re, c_im, d_skip, glu_w, glu_b):
    bsz, L, _ = hn.shape
    q, k, v, gate_a, u, gate_b = split_cols(hn @ w_in, EVEN_SPLITS)
    q = rms_norm(q.reshape(bsz, L, A_HEADS, A_HEAD_DIM), q_g)
    k = rms_norm(k.reshape(bsz, L, A_KV_HEADS, A_HEAD_DIM), k_g)
    v = v.reshape(bsz, L, A_KV_HEADS, A_HEAD_DIM)
    att = swa_sink_attention(q, k, v, sinks, rel_bias) * jax.nn.silu(gate_a)
    ssm = s5_mixer(u, log_dt, a_re, a_im, b_re, b_im, c_re, c_im, d_skip, glu_w, glu_b) * jax.nn.silu(gate_b)
    return jnp.concatenate([att, ssm], axis=-1) @ w_out

def odd_layer(hn, rel_bias, w_in, w_out, q_g, k_g):
    bsz, L, _ = hn.shape
    q, k, v, gate, qi, ki, wi = split_cols(hn @ w_in, ODD_SPLITS)
    q = rms_norm(q.reshape(bsz, L, C_HEADS, C_HEAD_DIM), q_g)
    k = rms_norm(k.reshape(bsz, L, C_KV_HEADS, C_HEAD_DIM), k_g)
    v = v.reshape(bsz, L, C_KV_HEADS, C_HEAD_DIM)
    qi = qi.reshape(bsz, L, IDX_HEADS, IDX_DIM)
    wi = wi * (IDX_HEADS ** -0.5)
    att = dsa_attention(q, k, v, qi, ki, wi, rel_bias)
    return (att * jax.nn.silu(gate)) @ w_out

def first_inputs(seed: int = 0) -> dict:
    key = jax.random.key(seed)
    ks = jax.random.split(key, 24)
    f32 = jnp.float32

    def nrm(k, shape, s):
        return jax.random.normal(k, shape, f32) * s

    ev_in = sum(EVEN_SPLITS)
    od_in = sum(ODD_SPLITS)
    ssm_n = jnp.arange(SSM_STATE, dtype=f32)
    return {
        'x': nrm(ks[0], (BATCH, SEQ, D_MODEL), 1.0),
        'rel_bias': nrm(ks[1], (NUM_BUCKETS, A_HEADS), 0.5),
        'norm_g': 1.0 + nrm(ks[2], (DEPTH, D_MODEL), 0.02),
        'ev_w_in': nrm(ks[3], (N_EVEN, D_MODEL, ev_in), D_MODEL ** -0.5),
        'ev_w_out': nrm(ks[4], (N_EVEN, A_WIDTH + B_WIDTH, D_MODEL), (A_WIDTH + B_WIDTH) ** -0.5),
        'ev_q_norm_g': 1.0 + nrm(ks[5], (N_EVEN, A_HEAD_DIM), 0.02),
        'ev_k_norm_g': 1.0 + nrm(ks[6], (N_EVEN, A_HEAD_DIM), 0.02),
        'ev_sinks': nrm(ks[7], (N_EVEN, A_HEADS), 1.0),
        'ev_ssm_log_dt': jax.random.uniform(ks[8], (N_EVEN, SSM_GROUPS), f32, math.log(DT_MIN), math.log(DT_MAX)),
        'ev_ssm_a_re': -0.5 + nrm(ks[9], (N_EVEN, SSM_GROUPS, SSM_STATE), 0.01),
        'ev_ssm_a_im': jnp.pi * ssm_n + nrm(ks[10], (N_EVEN, SSM_GROUPS, SSM_STATE), 0.01),
        'ev_ssm_b_re': nrm(ks[11], (N_EVEN, SSM_GROUPS, SSM_STATE, SSM_GROUP), (2 * SSM_GROUP) ** -0.5),
        'ev_ssm_b_im': nrm(ks[12], (N_EVEN, SSM_GROUPS, SSM_STATE, SSM_GROUP), (2 * SSM_GROUP) ** -0.5),
        'ev_ssm_c_re': nrm(ks[13], (N_EVEN, SSM_GROUPS, SSM_GROUP, SSM_STATE), (2 * SSM_STATE) ** -0.5),
        'ev_ssm_c_im': nrm(ks[14], (N_EVEN, SSM_GROUPS, SSM_GROUP, SSM_STATE), (2 * SSM_STATE) ** -0.5),
        'ev_ssm_d': nrm(ks[15], (N_EVEN, SSM_GROUPS, SSM_GROUP), 1.0),
        'ev_glu_w': nrm(ks[16], (N_EVEN, B_WIDTH, 2 * B_WIDTH), B_WIDTH ** -0.5),
        'ev_glu_b': nrm(ks[17], (N_EVEN, 2 * B_WIDTH), 0.01),
        'od_w_in': nrm(ks[18], (N_ODD, D_MODEL, od_in), D_MODEL ** -0.5),
        'od_w_out': nrm(ks[19], (N_ODD, C_WIDTH, D_MODEL), C_WIDTH ** -0.5),
        'od_q_norm_g': 1.0 + nrm(ks[20], (N_ODD, C_HEAD_DIM), 0.02),
        'od_k_norm_g': 1.0 + nrm(ks[21], (N_ODD, C_HEAD_DIM), 0.02),
    }

def first_block(x, rel_bias, norm_g, ev_w_in, ev_w_out, ev_q_norm_g, ev_k_norm_g, ev_sinks,
              ev_ssm_log_dt, ev_ssm_a_re, ev_ssm_a_im, ev_ssm_b_re, ev_ssm_b_im, ev_ssm_c_re,
              ev_ssm_c_im, ev_ssm_d, ev_glu_w, ev_glu_b, od_w_in, od_w_out, od_q_norm_g, od_k_norm_g):
    h = x
    for layer in range(DEPTH):
        hn = rms_norm(h, norm_g[layer])
        j = layer // 2
        if layer % 2 == 0:
            out = even_layer(hn, rel_bias, ev_w_in[j], ev_w_out[j], ev_q_norm_g[j], ev_k_norm_g[j],
                             ev_sinks[j], ev_ssm_log_dt[j], ev_ssm_a_re[j], ev_ssm_a_im[j],
                             ev_ssm_b_re[j], ev_ssm_b_im[j], ev_ssm_c_re[j], ev_ssm_c_im[j],
                             ev_ssm_d[j], ev_glu_w[j], ev_glu_b[j])
        else:
            out = odd_layer(hn, rel_bias, od_w_in[j], od_w_out[j], od_q_norm_g[j], od_k_norm_g[j])
        h = h + out
    return h


DEPTH_2 = 1

D_PLE = 256
D_MIX = 2 * D_MODEL
D_SSM = D_MIX // 2
D_CONF = D_MIX - D_SSM
SSM_HEAD_DIM = 64
SSM_HEADS = D_SSM // SSM_HEAD_DIM
SSM_GROUPS_2 = 2
SSM_HPG = SSM_HEADS // SSM_GROUPS_2
SSM_STATE_2 = 128
SSM_CONV_K = 4
CHUNK = 128
CONF_K = 31
LN_EPS = 1e-5
RMS_EPS = 1e-5

COLS = (D_SSM,
        D_SSM,
        SSM_GROUPS_2 * SSM_STATE_2,
        SSM_GROUPS_2 * SSM_STATE_2,
        SSM_HEADS,
        2 * D_CONF,
        D_CONF)
D_IN_PROJ = sum(COLS)
SPLITS = tuple(int(s) for s in np.cumsum(COLS)[:-1])

DEEPNORM_ALPHA = (2.0 * DEPTH_2) ** 0.25
DEEPNORM_BETA = (8.0 * DEPTH_2) ** -0.25


def layer_norm(x, g, b):
    xf = x.astype(jnp.float32)
    mu = jnp.mean(xf, axis=-1, keepdims=True)
    var = jnp.mean(jnp.square(xf - mu), axis=-1, keepdims=True)
    return ((xf - mu) * lax.rsqrt(var + LN_EPS)).astype(x.dtype) * g + b

def causal_depthwise_conv(x, w, b):
    k = w.shape[0]
    xp = jnp.pad(x, ((0, 0), (k - 1, 0), (0, 0)))
    y = lax.conv_general_dilated(xp, w[:, None, :], window_strides=(1,), padding='VALID',
                                 dimension_numbers=('NWC', 'WIO', 'NWC'),
                                 feature_group_count=x.shape[-1])
    return y + b

def ssd_chunked(xh, dt, a, bm, cm):
    bsz, l, g, j, p = xh.shape
    n = bm.shape[-1]
    c = l // CHUNK
    xdt = (xh * dt[..., None]).reshape(bsz, c, CHUNK, g, j, p)
    adt = jnp.moveaxis((dt * a).reshape(bsz, c, CHUNK, g, j), 2, -1)
    a_cs = jnp.cumsum(adt, axis=-1)
    bc = bm.reshape(bsz, c, CHUNK, g, n)
    cc = cm.reshape(bsz, c, CHUNK, g, n)
    causal = jnp.tril(jnp.ones((CHUNK, CHUNK), dtype=bool))
    seg = a_cs[..., :, None] - a_cs[..., None, :]
    ldec = jnp.exp(jnp.where(causal, seg, -jnp.inf))
    cb = jnp.einsum('bclgn,bcsgn->bcgls', cc, bc)
    y_diag = jnp.einsum('bcgjls,bcsgjp->bclgjp', cb[:, :, :, None] * ldec, xdt)
    decay_states = jnp.exp(a_cs[..., -1:] - a_cs)
    states = jnp.einsum('bclgn,bcgjl,bclgjp->bcgjpn', bc, decay_states, xdt)
    chunk_decay = jnp.exp(a_cs[..., -1])

    def step(h, inp):
        s, d = inp
        return h * d[..., None, None] + s, h

    h0 = jnp.zeros((bsz, g, j, p, n), dtype=xdt.dtype)
    _, prev = lax.scan(step, h0, (jnp.moveaxis(states, 1, 0), jnp.moveaxis(chunk_decay, 1, 0)))
    prev = jnp.moveaxis(prev, 0, 1)
    y_off = jnp.einsum('bclgn,bcgjpn,bcgjl->bclgjp', cc, prev, jnp.exp(a_cs))
    return (y_diag + y_off).reshape(bsz, l, g, j, p)

def second_inputs(seed: int = 0) -> dict:
    key = jax.random.key(seed)
    ks = jax.random.split(key, 26)
    nrm = jax.random.normal
    f32 = jnp.float32
    x = nrm(ks[0], (BATCH, SEQ, D_MODEL), f32)
    p = nrm(ks[1], (DEPTH_2, BATCH, SEQ, D_PLE), f32)
    ln_emb_g = 1.0 + 0.02 * nrm(ks[2], (D_MODEL,), f32)
    ln_emb_b = 0.02 * nrm(ks[3], (D_MODEL,), f32)
    w_in = nrm(ks[4], (DEPTH_2, D_MODEL, D_IN_PROJ), f32) * D_MODEL ** -0.5
    d_xbc = D_SSM + 2 * SSM_GROUPS_2 * SSM_STATE_2
    ssm_conv_w = nrm(ks[5], (DEPTH_2, SSM_CONV_K, d_xbc), f32) * SSM_CONV_K ** -0.5
    ssm_conv_b = 0.02 * nrm(ks[6], (DEPTH_2, d_xbc), f32)
    dt0 = jnp.exp(jax.random.uniform(ks[7], (DEPTH_2, SSM_HEADS), f32, np.log(1e-3), np.log(1e-1)))
    dt_bias = dt0 + jnp.log(-jnp.expm1(-dt0))
    a_log = jnp.log(jax.random.uniform(ks[8], (DEPTH_2, SSM_HEADS), f32, 1.0, 16.0))
    d_skip = 1.0 + 0.1 * nrm(ks[9], (DEPTH_2, SSM_HEADS), f32)
    ssm_norm_g = 1.0 + 0.02 * nrm(ks[10], (DEPTH_2, D_SSM), f32)
    b_glu = 0.02 * nrm(ks[11], (DEPTH_2, 2 * D_CONF), f32)
    conf_conv_w = nrm(ks[12], (DEPTH_2, CONF_K, D_CONF), f32) * CONF_K ** -0.5
    conf_conv_b = 0.02 * nrm(ks[13], (DEPTH_2, D_CONF), f32)
    conf_ln_g = 1.0 + 0.02 * nrm(ks[14], (DEPTH_2, D_CONF), f32)
    conf_ln_b = 0.02 * nrm(ks[15], (DEPTH_2, D_CONF), f32)
    w_out = nrm(ks[16], (DEPTH_2, D_MIX, D_MODEL), f32) * (DEEPNORM_BETA * (2.0 / (D_MIX + D_MODEL)) ** 0.5)
    b_out = 0.02 * nrm(ks[17], (DEPTH_2, D_MODEL), f32)
    ln1_g = 1.0 + 0.02 * nrm(ks[18], (DEPTH_2, D_MODEL), f32)
    ln1_b = 0.02 * nrm(ks[19], (DEPTH_2, D_MODEL), f32)
    w_ple_gate = nrm(ks[20], (DEPTH_2, D_MODEL, D_MODEL), f32) * D_MODEL ** -0.5
    w_ple_proj = nrm(ks[21], (DEPTH_2, D_PLE, D_MODEL), f32) * (DEEPNORM_BETA * (2.0 / (D_PLE + D_MODEL)) ** 0.5)
    ln2_g = 1.0 + 0.02 * nrm(ks[22], (DEPTH_2, D_MODEL), f32)
    ln2_b = 0.02 * nrm(ks[23], (DEPTH_2, D_MODEL), f32)
    return {"x": x, "p": p, "ln_emb_g": ln_emb_g, "ln_emb_b": ln_emb_b, "w_in": w_in,
            "ssm_conv_w": ssm_conv_w, "ssm_conv_b": ssm_conv_b, "dt_bias": dt_bias,
            "a_log": a_log, "d_skip": d_skip, "ssm_norm_g": ssm_norm_g, "b_glu": b_glu,
            "conf_conv_w": conf_conv_w, "conf_conv_b": conf_conv_b, "conf_ln_g": conf_ln_g,
            "conf_ln_b": conf_ln_b, "w_out": w_out, "b_out": b_out, "ln1_g": ln1_g,
            "ln1_b": ln1_b, "w_ple_gate": w_ple_gate, "w_ple_proj": w_ple_proj,
            "ln2_g": ln2_g, "ln2_b": ln2_b}

def second_block(x, p, ln_emb_g, ln_emb_b, w_in, ssm_conv_w, ssm_conv_b, dt_bias, a_log,
              d_skip, ssm_norm_g, b_glu, conf_conv_w, conf_conv_b, conf_ln_g, conf_ln_b,
              w_out, b_out, ln1_g, ln1_b, w_ple_gate, w_ple_proj, ln2_g, ln2_b):
    bsz, l, _ = x.shape
    f32 = jnp.float32
    gn = SSM_GROUPS_2 * SSM_STATE_2
    h = layer_norm(x, ln_emb_g, ln_emb_b)
    for i in range(DEPTH_2):
        proj = jnp.einsum('bld,de->ble', h, w_in[i])
        xs, z, bm, cm, dt_raw, glu, cgate = jnp.split(proj, SPLITS, axis=-1)

        xbc = jnp.concatenate([xs, bm, cm], axis=-1)
        xbc = jax.nn.silu(causal_depthwise_conv(xbc, ssm_conv_w[i], ssm_conv_b[i]))
        xs_c = xbc[..., :D_SSM]
        bm_c = xbc[..., D_SSM:D_SSM + gn].reshape(bsz, l, SSM_GROUPS_2, SSM_STATE_2).astype(f32)
        cm_c = xbc[..., D_SSM + gn:].reshape(bsz, l, SSM_GROUPS_2, SSM_STATE_2).astype(f32)
        xh = xs_c.reshape(bsz, l, SSM_GROUPS_2, SSM_HPG, SSM_HEAD_DIM).astype(f32)
        dt = jax.nn.softplus((dt_raw + dt_bias[i]).astype(f32)).reshape(bsz, l, SSM_GROUPS_2, SSM_HPG)
        a = -jnp.exp(a_log[i].astype(f32)).reshape(SSM_GROUPS_2, SSM_HPG)
        y = ssd_chunked(xh, dt, a, bm_c, cm_c)
        y = y + d_skip[i].astype(f32).reshape(SSM_GROUPS_2, SSM_HPG)[:, :, None] * xh
        yz = y.reshape(bsz, l, SSM_GROUPS_2, D_SSM // SSM_GROUPS_2) * \
            jax.nn.silu(z.astype(f32)).reshape(bsz, l, SSM_GROUPS_2, D_SSM // SSM_GROUPS_2)
        yz = yz * lax.rsqrt(jnp.mean(jnp.square(yz), axis=-1, keepdims=True) + RMS_EPS)
        y_ssm = yz.reshape(bsz, l, D_SSM).astype(x.dtype) * ssm_norm_g[i]

        glu = glu + b_glu[i]
        u = glu[..., :D_CONF] * jax.nn.sigmoid(glu[..., D_CONF:])
        u = causal_depthwise_conv(u, conf_conv_w[i], conf_conv_b[i])
        u = jax.nn.silu(layer_norm(u, conf_ln_g[i], conf_ln_b[i]))
        y_conf = u * jax.nn.silu(cgate)

        mix = jnp.concatenate([y_ssm, y_conf], axis=-1)
        out = jnp.einsum('ble,ed->bld', mix, w_out[i]) + b_out[i]
        h = layer_norm(DEEPNORM_ALPHA * h + out, ln1_g[i], ln1_b[i])

        gate = jax.nn.sigmoid(jnp.einsum('bld,de->ble', h, w_ple_gate[i]))
        ple = jnp.einsum('blq,qd->bld', p[i], w_ple_proj[i])
        h = layer_norm(DEEPNORM_ALPHA * h + gate * ple, ln2_g[i], ln2_b[i])
    return h


_first_inputs = second_inputs


def second_inputs(seed=0):
    import zlib

    import numpy as np

    out = dict(_first_inputs(seed))
    spreads = {}
    factors = {'ssm_conv_b': 5.157,
     'ssm_norm_g': 8.0,
     'b_glu': 8.0,
     'conf_conv_b': 8.0,
     'conf_ln_g': 8.0,
     'conf_ln_b': 8.0,
     'b_out': 3.766,
     'ln1_g': 2.951,
     'ln1_b': 2.877,
     'ln2_g': 2.824,
     'ln2_b': 2.909}
    for name, (base, spread) in spreads.items():
        noise = np.random.default_rng([zlib.crc32(name.encode()), seed]).standard_normal(out[name].shape)
        drawn = base * np.exp(spread * noise) if base else spread * noise
        out[name] = __import__('jax').numpy.asarray(drawn.astype(out[name].dtype))
    for name, factor in factors.items():
        out[name] = (out[name] * factor).astype(out[name].dtype)
    return out


_narrow_inputs = second_inputs


def second_inputs(seed=0):

    out = dict(_narrow_inputs(seed))
    wider = {'ssm_norm_g': 3.89,
     'conf_ln_g': 8.64,
     'conf_ln_b': 8.62,
     'b_out': 3.76,
     'ln1_g': 3.28,
     'ln1_b': 3.28,
     'ln2_g': 3.18,
     'ln2_b': 3.18}
    for name, times in wider.items():
        mean = out[name].mean()
        out[name] = (mean + times * (out[name] - mean)).astype(out[name].dtype)
    return out


def setup_inputs(seed=0):
    out = dict(first_inputs(seed))
    for name, value in second_inputs(seed + 1).items():
        if name != "x":
            out[name + "_2"] = value
    return out


def reference(
    x, rel_bias, norm_g, ev_w_in, ev_w_out, ev_q_norm_g, ev_k_norm_g, ev_sinks, ev_ssm_log_dt,
    ev_ssm_a_re, ev_ssm_a_im, ev_ssm_b_re, ev_ssm_b_im, ev_ssm_c_re, ev_ssm_c_im, ev_ssm_d,
    ev_glu_w, ev_glu_b, od_w_in, od_w_out, od_q_norm_g, od_k_norm_g, p_2, ln_emb_g_2,
    ln_emb_b_2, w_in_2, ssm_conv_w_2, ssm_conv_b_2, dt_bias_2, a_log_2, d_skip_2, ssm_norm_g_2,
    b_glu_2, conf_conv_w_2, conf_conv_b_2, conf_ln_g_2, conf_ln_b_2, w_out_2, b_out_2, ln1_g_2,
    ln1_b_2, w_ple_gate_2, w_ple_proj_2, ln2_g_2, ln2_b_2,
):
    x = first_block(
        x, rel_bias, norm_g, ev_w_in, ev_w_out, ev_q_norm_g, ev_k_norm_g, ev_sinks,
        ev_ssm_log_dt, ev_ssm_a_re, ev_ssm_a_im, ev_ssm_b_re, ev_ssm_b_im, ev_ssm_c_re,
        ev_ssm_c_im, ev_ssm_d, ev_glu_w, ev_glu_b, od_w_in, od_w_out, od_q_norm_g, od_k_norm_g,
    )
    return second_block(
        x, p_2, ln_emb_g_2, ln_emb_b_2, w_in_2, ssm_conv_w_2, ssm_conv_b_2, dt_bias_2, a_log_2,
        d_skip_2, ssm_norm_g_2, b_glu_2, conf_conv_w_2, conf_conv_b_2, conf_ln_g_2, conf_ln_b_2,
        w_out_2, b_out_2, ln1_g_2, ln1_b_2, w_ple_gate_2, w_ple_proj_2, ln2_g_2, ln2_b_2,
    )


_drawn_inputs = setup_inputs


def setup_inputs(seed=0):
    import zlib

    import numpy as np

    out = dict(_drawn_inputs(seed))
    spreads = {}
    factors = {'norm_g': 3.657,
     'ev_q_norm_g': 8.0,
     'ev_k_norm_g': 8.0,
     'ev_sinks': 6.021,
     'ev_ssm_log_dt': 3.846,
     'ev_ssm_a_re': 8.0,
     'ev_ssm_a_im': 3.855,
     'ev_ssm_b_re': 5.034,
     'ev_ssm_b_im': 5.046,
     'ev_ssm_c_re': 5.084,
     'ev_ssm_c_im': 5.119,
     'ev_glu_b': 8.0,
     'od_q_norm_g': 8.0,
     'od_k_norm_g': 8.0}
    for name, (base, spread) in spreads.items():
        noise = np.random.default_rng([zlib.crc32(name.encode()), seed]).standard_normal(out[name].shape)
        drawn = base * np.exp(spread * noise) if base else spread * noise
        out[name] = __import__('jax').numpy.asarray(drawn.astype(out[name].dtype))
    for name, factor in factors.items():
        out[name] = (out[name] * factor).astype(out[name].dtype)
    return out
```

```python
import math

import numpy as np

import concourse.bass as bass
from concourse import mybir

F32 = mybir.dt.float32
BF16 = mybir.dt.bfloat16
ALU = mybir.AluOpType
ACT = mybir.ActivationFunctionType
AX = mybir.AxisListType

T = 1024
NB = 8
KB = 1024
NEG = -1e30
PI = math.pi
ALPHA = 2.0 ** 0.25


class Eng:

    def __init__(self, eng, sem, every):
        self.e, self.sem, self.n, self.seen = eng, sem, 0, {}
        every.append(self)

    def on(self, *toks):
        for t in toks:
            if t is None:
                continue
            if isinstance(t, list):
                self.on(*t)
                continue
            s, v = t
            if self.seen.get(s.name, 0) < v:
                self.e.wait_ge(s, v)
                self.seen[s.name] = v
        return self.e

    def did(self, ins):
        ins.then_inc(self.sem, 1)
        self.n += 1
        return (self.sem, self.n)

    def now(self):
        return (self.sem, self.n) if self.n else None


class Ring:

    def __init__(self, items):
        self.items, self.free, self.k = items, [[] for _ in items], -1

    def take(self):
        self.k = (self.k + 1) % len(self.items)
        f = self.free[self.k]
        assert f is not None, "buffer still out"
        self.free[self.k] = None
        return self.k, self.items[self.k], f

    def give(self, k, *toks):
        self.free[k] = list(toks)


class Dma:

    def __init__(self, sem):
        self.sem, self.n = sem, 0

    def start(self, eng, out, in_, *after):
        eng.on(*after).dma_start(out, in_).then_inc(self.sem, 16)
        self.n += 16
        return (self.sem, self.n)


def bc(ap, axis, n):
    u = ap.unsqueeze(axis)
    shape = list(u.shape)
    shape[axis] = n
    return u.to_broadcast(shape)


PANELS = [
    ("w_u", 8, 512), ("w_q", 8, 512), ("w_kv", 8, 256), ("w_ga", 8, 512), ("w_gb", 8, 512),
    ("w_glu", 4, 1024), ("w_eo0", 8, 512), ("w_eo1", 8, 512),
    ("w_qi", 8, 512), ("w_ki", 8, 136), ("w_okv", 8, 512), ("w_oq0", 8, 512), ("w_oq1", 8, 512),
    ("w_og0", 8, 512), ("w_og1", 8, 512), ("w_oo0", 8, 512), ("w_oo1", 8, 512),
    ("w_cf0", 8, 512), ("w_bc", 8, 512), ("w_cf1", 8, 512), ("w_xs0", 8, 512), ("w_cf2", 8, 512), ("w_xs1", 8, 512),
    ("w_cf3", 8, 512), ("w_dt", 8, 16), ("w_z0", 8, 512), ("w_z1", 8, 512),
    ("w_cg0", 8, 512), ("w_cg1", 8, 512),
    ("w_so00", 8, 512), ("w_so01", 8, 512), ("w_so10", 8, 512), ("w_so11", 8, 512),
    ("w_pg0", 8, 512), ("w_pg1", 8, 512), ("w_pp", 2, 1024),
]
EVEN_P = [p[0] for p in PANELS[:8]]
ODD_P = [p[0] for p in PANELS[8:17]]
SEC_P = [p[0] for p in PANELS[17:]]

SMALL = {
    "g_ev": 8, "g_od": 8, "qg_ev": 1, "kg_ev": 1, "sink": 8, "ldt": 32, "are": 32, "aim": 32,
    "dsk": 32, "glub": 8, "qg_od": 1, "kg_od": 1,
    "cxw": 48, "cxb": 12, "dtb": 16, "alog": 16, "sng": 8, "bglu": 16, "cfw": 248, "cfb": 8,
    "clg": 8, "clb": 8, "dk2": 16,
}
SM_OFF = {}
_o = 0
for _n, _c in SMALL.items():
    SM_OFF[_n] = _o
    _o += _c
SM_COLS = _o
STRIP_A = 383
STRIP_B = 1151


class K:

    def __init__(self, nc, d, panels):
        self.nc, self.d = nc, d
        ev = self.every = []
        self.V = Eng(nc.vector, nc.alloc_semaphore("s_dve"), ev)
        self.A = Eng(nc.scalar, nc.alloc_semaphore("s_act"), ev)
        self.P = Eng(nc.tensor, nc.alloc_semaphore("s_pe"), ev)
        self.G = Eng(nc.gpsimd, nc.alloc_semaphore("s_pool"), ev)
        self.S = Eng(nc.sync, nc.alloc_semaphore("s_sp"), ev)
        self.base = (nc.sbuf_base + 63) // 64 * 64
        self.end = nc.sbuf_usable_end
        self.nname = 0
        self.psum = nc.alloc_psum_tensor("psum", [128, 8, 512], F32)
        self.dsems = 0
        self.H0, self.X0, self.R0, self.C0 = 0, 32 * KB, 64 * KB, 112 * KB
        self.H = self.at(self.H0, [8, 1024])
        self.XT = self.at(self.X0, [8, 1024])
        self.ring = [self.at(self.R0 + 16 * KB * i, [4096]) for i in range(3)]
        o = self.C0
        self.ident = self.at(o, [128]); o += 512
        self.ones = self.at(o, [128]); o += 512
        self.tle = self.at(o, [128]); o += 512
        self.tgt = self.at(o, [128]); o += 512
        self.bones = self.at(o, [128]); o += 512
        self.flip = self.at(o, [128]); o += 512
        self.mhalf = self.at(o, [16]); o += 64
        self.epsc = self.at(o, [16]); o += 64
        self.tiny = self.at(o, [256]); o += 1024
        self.small = self.at(o, [SM_COLS]); o += (SM_COLS * 4 + 63) // 64 * 64
        self.PH0 = o
        self.slots = [None, None, None]
        self.slot_dma = [self.dma() for _ in range(3)]
        self.slot_free = [[], [], []]
        self.queue = list(panels)
        self.loaded = []
        for _ in range(3):
            self.prefetch()

    def at(self, off, shape, dt=F32):
        self.nname += 1
        size = 4 if dt == F32 else 2
        for s in shape:
            size *= s
        assert self.base + off + size <= self.end, (off, size, self.end - self.base)
        h = self.nc.alloc_sbuf_tensor_at(f"m{self.nname}", [128] + list(shape), dt, offset=self.base + off)
        return h[tuple(slice(None) for _ in range(len(shape) + 1))]

    def dma(self):
        self.dsems += 1
        return Dma(self.nc.alloc_semaphore(f"d{self.dsems}"))

    def bank(self, i, n=1):
        return self.psum[:, i, :] if n == 1 else self.psum[:, i:i + n, :].rearrange("p a b -> p (a b)")

    def sm(self, name, a=0, b=None):
        o = SM_OFF[name]
        return self.small[:, o + a:o + (SMALL[name] if b is None else b)]

    def prefetch(self):
        if not self.queue:
            return
        name = self.queue.pop(0)
        k, n = next((k, n) for m, k, n in PANELS if m == name)
        i = next(j for j in range(3) if self.slots[j] is None and self.slot_free[j] is not None)
        t = self.slot_dma[i].start(self.S, self.ring[i][:, 0:k * n], self.d[name], self.slot_free[i])
        self.slots[i] = name
        self.slot_free[i] = None
        self.loaded.append((name, i, t, self.ring[i][:, 0:k * n].rearrange("p (k n) -> p k n", k=k)))

    def panel(self, name):
        for nm, i, t, ap in self.loaded:
            if nm == name:
                return ap, t
        raise AssertionError(name)

    def done(self, name, *toks):
        for x in list(self.loaded):
            if x[0] == name:
                self.loaded.remove(x)
                self.slots[x[1]] = None
                self.slot_free[x[1]] = list(toks)
        self.prefetch()

    def mark(self):
        return [e.now() for e in self.every]

    def mm(self, out, lhsT, rhs, start, stop):
        return self.nc.tensor.matmul(out, lhsT, rhs, start=start, stop=stop, skip_group_check=True)

    def tr(self, out, in_):
        return self.nc.tensor.transpose(out, in_, self.ident[:, :])

    def setup(self):
        nc, G = self.nc, self.G
        self.t_small = self.dma().start(self.S, self.small[:, :], self.d["small"])
        a = [G.did(nc.gpsimd.memset(self.ident[:, :], 0.0)), G.did(nc.gpsimd.memset(self.ones[:, :], 1.0)),
             G.did(nc.gpsimd.memset(self.bones[:, :], 0.0)), G.did(nc.gpsimd.memset(self.mhalf[:, :], -0.5))]
        a.append(G.did(nc.gpsimd.memset(self.epsc[:, :], 1e-6)))
        G.on(*a)
        b = [G.did(nc.gpsimd.memset(self.bones[0:64, 0:64], 1.0)),
             G.did(nc.gpsimd.memset(self.bones[64:128, 64:128], 1.0))]
        aff = nc.gpsimd.affine_select
        G.on(*b)
        b.append(G.did(aff(out=self.ident[:, :], in_=self.ident[:, :], compare_op=ALU.not_equal, fill=1.0, base=0,
                           pattern=[[-1, 128]], channel_multiplier=1)))
        a2 = G.did(nc.gpsimd.memset(self.flip[:, :], 0.0))
        b.append(G.did(G.on(a2).affine_select(out=self.flip[:, :], in_=self.flip[:, :], compare_op=ALU.not_equal, fill=1.0,
                                              base=-127, pattern=[[1, 128]], channel_multiplier=1)))
        b.append(G.did(aff(out=self.tle[:, :], in_=self.ones[:, :], compare_op=ALU.is_ge, fill=0.0, base=0,
                           pattern=[[1, 128]], channel_multiplier=-1)))
        b.append(G.did(aff(out=self.tgt[:, :], in_=self.ones[:, :], compare_op=ALU.is_gt, fill=0.0, base=0,
                           pattern=[[-1, 128]], channel_multiplier=1)))
        self.t_const = b

    def transpose_to(self, src, dst, banks, ready, scale=None, only=range(8)):
        out = {}
        for half in range(2):
            for dt in only:
                k, bk, f = banks.take()
                self.P.on(f, self.t_const)
                for j in range(4):
                    b = 4 * half + j
                    self.P.on(ready[b])
                    ins = self.tr(self.bank(bk)[:, 128 * j:128 * j + 128], src[:, b, 128 * dt:128 * dt + 128])
                t = self.P.did(ins)
                o = dst[:, dt, 512 * half:512 * half + 512]
                if dt % 2:
                    if scale is None:
                        t2 = self.A.did(self.A.on(t).activation(o, self.bank(bk), ACT.Copy))
                    else:
                        t2 = self.A.did(self.A.on(t, self.t_small).activation(o, self.bank(bk), ACT.Copy, scale=scale[:, dt:dt + 1]))
                else:
                    if scale is None:
                        t2 = self.V.did(self.V.on(t).tensor_copy(o, self.bank(bk)))
                    else:
                        t2 = self.V.did(self.V.on(t, self.t_small).tensor_scalar(o, self.bank(bk), scale[:, dt:dt + 1], None, ALU.mult))
                banks.give(k, t2)
                out[(dt, half)] = t2
        return out

    def rms_rows(self, src, b, dst, ready, eps, junk, n=1024):
        c = self.tiny[:, 8 * b:8 * b + 1]
        e = self.tiny[:, 8 * b + 1:8 * b + 2]
        t = self.A.did(self.A.on(ready, self.wjunk).activation(junk, src, ACT.Square, accum_out=c))
        self.wjunk = t
        t = self.G.did(self.G.on(t, self.t_const).tensor_scalar(e, c, 1.0 / n, eps, ALU.mult, ALU.add))
        t = self.G.did(self.G.on(t).tensor_tensor(c, e, self.mhalf[:, 0:1], ALU.pow))
        return self.V.did(self.V.on(t, ready).tensor_scalar(dst, src, c, None, ALU.mult))

    def ln_rows(self, src, b, dst, ready, eps, gbc, bbc, tgb):
        V, G = self.V, self.G
        o = 24 * b
        st, mv, rs = self.tiny[:, o:o + 12], self.tiny[:, o + 12:o + 14], self.tiny[:, o + 14:o + 16]
        V.on(ready)
        ts = [V.did(V.e.bn_stats(st[:, 6 * i:6 * i + 6], src[:, 512 * i:512 * i + 512])) for i in range(2)]
        t = V.did(V.on(*ts).bn_aggr(mv, st))
        t1 = G.did(G.on(t, self.t_const).tensor_scalar(rs[:, 0:1], mv[:, 1:2], 1.0, eps, ALU.mult, ALU.add))
        t1 = G.did(G.on(t1).tensor_tensor(rs[:, 1:2], rs[:, 0:1], self.mhalf[:, 0:1], ALU.pow))
        t = V.did(V.on(t1).tensor_scalar(dst, src, mv[:, 0:1], rs[:, 1:2], ALU.subtract, ALU.mult))
        t = V.did(V.on(t, tgb).tensor_tensor(dst, dst, gbc, ALU.mult))
        return V.did(V.on(t).tensor_tensor(dst, dst, bbc, ALU.add))

    def proj_T(self, w, tw, col, m, banks, evac, xr=None, nk=8, X=None):
        X = self.XT if X is None else X
        last = None
        for half in range(2):
            k, bk, f = banks.take()
            self.P.on(f, tw, xr)
            for kk in range(nk):
                ins = self.mm(self.bank(bk)[0:m, :], w[:, kk, col:col + m], X[:, kk, 512 * half:512 * half + 512],
                              kk == 0, kk == nk - 1)
            last = self.P.did(ins)
            banks.give(k, *evac(half, self.bank(bk), last))
        return last

    def proj_N(self, w, tw, col, n, b, bk_ap, X=None, nk=8, start=True, stop=True):
        X = self.XT if X is None else X
        self.P.on(tw)
        for kk in range(nk):
            ins = self.mm(bk_ap, X[:, kk, 128 * b:128 * b + 128], w[:, kk, col:col + n], start and kk == 0, stop and kk == nk - 1)
        return self.P.did(ins)

    def qk_norm(self, psb, t, dst, gain, lhs_ones, banks, sq, rt, inv, tsm):
        sk, sqb, sf = sq.take()
        t1 = self.A.did(self.A.on(t, sf).activation(sqb, psb, ACT.Square))
        k, bk, f = banks.take()
        t2 = self.P.did(self.P.on(t1, f, self.t_const).matmul(self.bank(bk), lhs_ones, sqb, start=True, stop=True))
        sq.give(sk, t2)
        rk, rb, rf = rt.take()
        t3 = self.A.did(self.A.on(t2, rf).activation(rb, self.bank(bk), ACT.Sqrt, bias=self.epsc[:, 0:1], scale=inv))
        banks.give(k, t3)
        t4 = self.V.did(self.V.on(t3).reciprocal(rb, rb))
        t5 = self.V.did(self.V.on(t4, t, tsm).scalar_tensor_tensor(dst, psb, gain, rb, ALU.mult, ALU.mult))
        rt.give(rk, t5)
        return t5


def even(k, last_out=None):
    nc, d, V, A, P, G, S = k.nc, k.d, k.V, k.A, k.P, k.G, k.S
    PH = k.PH0
    QT, KT, VN = k.at(PH, [4, 1024]), k.at(PH + 16 * KB, [1024]), k.at(PH + 20 * KB, [8, 128])
    GA, GB = k.at(PH + 24 * KB, [4, 1024]), k.at(PH + 40 * KB, [4, 1024])
    BIA = k.at(PH + 56 * KB, [8, 256])
    R2 = PH + 64 * KB
    L = Ring([k.at(R2 + 4 * KB * i, [1024]) for i in range(2)])
    PT = Ring([k.at(R2 + 8 * KB + 4 * KB * i, [2, 512]) for i in range(2)])
    sq = Ring([k.at(R2 + 16 * KB, [512])])
    rt = Ring([k.at(R2 + 18 * KB, [512])])
    Z, Y = (k.at(R2 + (20 + 2 * i) * KB, [4, 128]) for i in range(2))
    proj = Ring([0, 1, 2])
    mis = Ring([3, 4, 5, 6, 7])

    tx = []
    for q in range(4):
        tx.append(k.dma().start(S, k.H[:, 2 * q:2 * q + 2, :],
                                d["x"][256 * q:256 * q + 256, :].rearrange("(b p) n -> p b n", p=128)))
    k.wjunk = None
    junk = k.at(PH + 16 * KB, [1024])
    ready = [k.rms_rows(k.H[:, b, :], b, k.H[:, b, :], tx[b // 2], 1e-6, junk) for b in range(8)]
    tX = k.transpose_to(k.H, k.XT, mis, ready, scale=k.sm("g_ev"))
    xr = list(tX.values())

    O = PH + 40 * KB
    BB, BX, CC, CX = (k.at(O + 2 * KB * i, [32, 16]) for i in range(4))
    PR, PIm = k.at(O + 8 * KB, [32, 9]), k.at(O + 9 * KB + 256, [32, 9])
    sm = k.at(O + 10 * KB + 512, [12, 32])
    raw = k.at(PH + 24 * KB, [4, 32, 16])
    sc = k.at(PH + 32 * KB, [6, 32, 9])
    tr = k.dma().start(S, raw, d["ssmw"].rearrange("p (a g h) -> p a g h", a=4, g=32))
    KS = k.at(O + 12 * KB + 512, [128])
    tks = G.did(nc.gpsimd.iota(KS, pattern=[[1, 128]], base=1, channel_multiplier=0, allow_small_or_imprecise_dtypes=True))
    J9 = k.at(O + 13 * KB, [9])
    tj9 = G.did(nc.gpsimd.iota(J9, pattern=[[1, 9]], base=0, channel_multiplier=0, allow_small_or_imprecise_dtypes=True))
    DT, AT, TH, DEN, NR, NI, FR, FI, U1, U2, R8, TH8 = (sm[:, i, :] for i in range(12))
    tsm = k.t_small
    t = A.did(A.on(tsm).activation(DT, k.sm("ldt"), ACT.Exp))
    t1 = V.did(V.on(t, tsm).tensor_tensor(AT, k.sm("are"), DT, ALU.mult))
    t2 = V.did(V.e.tensor_tensor(TH, k.sm("aim"), DT, ALU.mult))
    aj, tj, em, mg, cs, sn = (sc[:, i, :, :] for i in range(6))
    t1 = V.did(V.on(t1, tj9).tensor_tensor(aj, bc(AT, 2, 9), bc(J9, 1, 32), ALU.mult))
    t2 = V.did(V.on(t2).tensor_tensor(tj, bc(TH, 2, 9), bc(J9, 1, 32), ALU.mult))
    ta = A.did(A.on(t1).activation(em, aj, ACT.Exp))
    tb = A.did(A.on(t1).activation(mg, aj, ACT.Tanh, scale=0.5))
    t = V.did(V.on(ta, tb).scalar_tensor_tensor(em, em, 1.0, mg, ALU.add, ALU.mult))
    tmg = V.did(V.on(t).tensor_scalar(mg, em, 1.0, None, ALU.add))

    def reduce_angle(eng, ang, n, tok):
        e = eng.e
        t = eng.did(eng.on(tok).tensor_scalar(n, ang, 1.0 / (2 * PI), 12582912.0, ALU.mult, ALU.add))
        t = eng.did(eng.on(t).tensor_scalar(n, n, 12582912.0, None, ALU.subtract))
        t = eng.did(eng.on(t).scalar_tensor_tensor(ang, n, -6.28125, ang, ALU.mult, ALU.add))
        t = eng.did(eng.on(t).scalar_tensor_tensor(ang, n, -(2 * PI - 6.28125), ang, ALU.mult, ALU.add))
        return eng.did(eng.on(t).tensor_scalar(ang, ang, 3.1415925, -3.1415925, ALU.min, ALU.max))

    def quarter(eng, out, ang, n, tok):
        t = eng.did(eng.on(tok).tensor_scalar(n, ang, PI / 2, -2 * PI, ALU.is_gt, ALU.mult))
        t = eng.did(eng.on(t).scalar_tensor_tensor(out, ang, PI / 2, n, ALU.add, ALU.add))
        return eng.did(eng.on(t).tensor_scalar(out, out, 3.1415925, -3.1415925, ALU.min, ALU.max))

    t = reduce_angle(V, tj, sn, t2)
    tq = quarter(V, cs, tj, sn, t)
    ts_ = A.did(A.on(tq).activation(sn, tj, ACT.Sin))
    tc_ = A.did(A.on(tq).activation(cs, cs, ACT.Sin))
    t = V.did(V.on(tc_, tmg).tensor_tensor(PR, mg, cs, ALU.mult))
    t1 = V.did(V.on(ts_).tensor_tensor(PIm, mg, sn, ALU.mult))
    tR8 = V.did(V.on(tmg).tensor_copy(R8, mg[:, :, 8]))
    tT8 = V.did(V.e.tensor_scalar(TH8, TH, 8.0, None, ALU.mult))
    tpow = [t, t1]
    hs = U1
    th_ = A.did(A.on(t1).activation(hs, tj[:, :, 1], ACT.Sin, scale=0.5))
    t = V.did(V.on(th_).tensor_tensor(hs, hs, hs, ALU.mult))
    t1 = V.did(V.e.tensor_tensor(NR, em[:, :, 1], cs[:, :, 1], ALU.mult))
    t = V.did(V.on(t, t1).scalar_tensor_tensor(NR, hs, -2.0, NR, ALU.mult, ALU.add))
    ar, ai = k.sm("are"), k.sm("aim")
    ni = PIm[:, :, 1]
    t1 = V.did(V.e.tensor_tensor(DEN, ar, ar, ALU.mult))
    t2 = V.did(V.e.tensor_tensor(U2, ai, ai, ALU.mult))
    t1 = V.did(V.on(t1, t2).tensor_tensor(DEN, DEN, U2, ALU.add))
    t1 = V.did(V.on(t1).reciprocal(DEN, DEN))
    ta = V.did(V.on(t).tensor_tensor(FR, NR, ar, ALU.mult))
    tb = V.did(V.on(*tpow).tensor_tensor(U1, ni, ai, ALU.mult))
    ta = V.did(V.on(ta, tb).tensor_tensor(FR, FR, U1, ALU.add))
    tb = V.did(V.e.tensor_tensor(FI, ni, ar, ALU.mult))
    tc = V.did(V.on(t2).tensor_tensor(U2, NR, ai, ALU.mult))
    tb = V.did(V.on(tb, tc).tensor_tensor(FI, FI, U2, ALU.subtract))
    ta = V.did(V.on(ta, t1).tensor_tensor(FR, FR, DEN, ALU.mult))
    tb = V.did(V.on(tb).tensor_tensor(FI, FI, DEN, ALU.mult))
    lo, hi = slice(0, 64), slice(64, 128)
    V.on(ta, tb, tr)
    q = []
    for h, f1, f2, op in ((lo, FR, FI, ALU.subtract), (hi, FI, FR, ALU.add)):
        a1 = V.did(V.e.tensor_tensor(BB[h], bc(f1[h], 2, 16), raw[h, 0], ALU.mult))
        a2 = V.did(V.e.tensor_tensor(BX[h], bc(f2[h], 2, 16), raw[h, 1], ALU.mult))
        q.append(V.did(V.on(a1, a2).tensor_tensor(BB[h], BB[h], BX[h], op)))
    for h, f1, f2, op in ((lo, FI, FR, ALU.add), (hi, FR, FI, ALU.subtract)):
        a1 = V.did(V.on(*q).tensor_tensor(BX[h], bc(f1[h], 2, 16), raw[h, 0], ALU.mult))
        a2 = V.did(V.e.tensor_tensor(CX[h], bc(f2[h], 2, 16), raw[h, 1], ALU.mult))
        a1 = V.did(V.on(a1, a2).tensor_tensor(BX[h], BX[h], CX[h], op))
        if h is lo:
            a1 = V.did(V.on(a1).tensor_scalar(BX[h], BX[h], -1.0, None, ALU.mult))
        q.append(a1)
    V.on(*q)
    q.append(V.did(V.e.tensor_copy(CC[lo], raw[lo, 2])))
    q.append(V.did(V.e.tensor_scalar(CC[hi], raw[hi, 3], -1.0, None, ALU.mult)))
    q.append(V.did(V.e.tensor_scalar(CX[lo], raw[lo, 3], -1.0, None, ALU.mult)))
    q.append(V.did(V.e.tensor_scalar(CX[hi], raw[hi, 2], -1.0, None, ALU.mult)))
    QR, QI = k.at(O + 13 * KB + 64, [32, 8]), k.at(O + 14 * KB + 64, [32, 8])
    V.on(*tpow)
    for j in range(8):
        q.append(V.did(V.e.tensor_copy(QR[:, :, j], PR[:, :, 7 - j])))
        q.append(V.did(V.e.tensor_copy(QI[:, :, j], PIm[:, :, 7 - j])))
    tset = q + tpow + [tR8, tT8]

    ohA, ohB = k.at(PH, [STRIP_A]), k.at(PH + 2 * KB, [STRIP_B])
    rbt, rows = k.at(PH + 7 * KB, [8]), k.at(PH + 8 * KB, [STRIP_A + STRIP_B])
    dm = k.dma()
    dm.start(S, ohA[0:33], d["ohA"])
    dm.start(S, ohB[0:33], d["ohB"])
    toh = dm.start(S, rbt[0:32], d["rb"])
    tneg = G.did(G.on(G.now()).memset(rbt[32:33], NEG))
    trow = []
    for src, o, n in ((ohA, 0, STRIP_A), (ohB, STRIP_A, 512), (ohB, STRIP_A + 512, 512), (ohB, STRIP_A + 1024, STRIP_B - 1024)):
        kk, bk, f = mis.take()
        so = 0 if src is ohA else o - STRIP_A
        t = P.did(P.on(f, toh, tneg).matmul(k.bank(bk)[0:8, 0:n], rbt[0:33], src[0:33, so:so + n], start=True, stop=True))
        t = A.did(A.on(t).activation(rows[0:8, o:o + n], k.bank(bk)[0:8, 0:n], ACT.Copy))
        mis.give(kk, t)
        trow.append(t)
    tdr = k.dma().start(S, d["strip"][:, :], rows[0:8], trow)
    k.t_strip = tdr
    rawb = k.at(PH, [8, 256])
    traw = k.dma().start(S, rawb, bass.AP(d["strip"].tensor, 0, [[1, 128], [STRIP_A + STRIP_B, 8], [1, 256]]), tdr, trow)
    tbia = []
    for i in range(4):
        kk, bk, f = mis.take()
        t = P.did(P.on(f, traw, k.t_const).matmul(k.bank(bk), k.flip, rawb[:, 2 * i:2 * i + 2, :].rearrange("p a b -> p (a b)"), start=True, stop=True))
        t = A.did(A.on(t).activation(BIA[:, 2 * i:2 * i + 2, :], k.bank(bk).rearrange("p (a b) -> p a b", a=2), ACT.Copy))
        mis.give(kk, t)
        tbia.append(t)

    ut = Ring([k.at(PH + 24 * KB + 16 * KB - 4 * KB, [8, 128]), k.at(PH + 16 * KB, [8, 128])])
    w, tw = k.panel("w_u")
    du = [k.dma() for _ in range(2)]
    uback = []
    udone = []
    for m in range(4):
        kk, ub, f = ut.take()
        toks = []

        def evac(half, ps, t, ub=ub, f=f, toks=toks, m=m):
            o = ub[:, :, 64 * half:64 * half + 64].rearrange("p j c -> p c j")
            t = A.did(A.on(t, f, tset if m < 2 else None).activation(o, ps.rearrange("p (c j) -> p c j", j=8), ACT.Copy))
            toks.append(t)
            return [t]

        tl = k.proj_T(w, tw, 128 * m, 128, proj, evac, xr)
        t = du[m % 2].start(S, d["uscr"][128 * m:128 * m + 128], ub, toks)
        ut.give(kk, t)
        udone.append(t)
    k.done("w_u", tl)

    Hb = k.H0
    n2 = 2 * KB
    UR = Ring([k.at(Hb + n2 * i, [4, 128]) for i in range(2)])
    UD = [k.dma() for _ in range(2)]
    TC, TS, M1, M2, M3, M4, WN, WT, WS = (k.at(Hb + n2 * (2 + i), [4, 128]) for i in range(9))
    PW = k.at(Hb + 22 * KB, [4, 9, 16])
    PS = k.at(Hb + 24 * KB + 512, [4, 9, 16])
    TP = k.at(Hb + 27 * KB, [4, 128])
    BP = k.at(Hb + 29 * KB, [3, 240])
    BP2 = k.at(O + 15 * KB + 64, [1, 240])
    bp = [BP[:, 0, :], BP[:, 1, :], BP[:, 2, :], BP2[:, 0, :]]
    tz = [G.did(G.on(xr, tneg).memset(BP, 0.0)), G.did(G.e.memset(BP2, 0.0))]
    yd = [k.dma() for _ in range(2)]
    tyd = []

    def ssm():
        prev = {}
        for n in range(8):
            gs = slice(4 * n, 4 * n + 4)
            kk, U, f = UR.take()
            for gi in range(4):
                g = 4 * n + gi
                tu = UD[n % 2].start(S, U[:, gi, :], d["uscr"][16 * g:16 * g + 16].rearrange("h j c -> j h c"), f, udone[n // 2], xr)
            t = V.did(V.on(tks, tset, prev.get("tcts"), xr).tensor_tensor(TS, bc(TH8[:, gs], 2, 128), bc(KS, 1, 4), ALU.mult))
            t = reduce_angle(V, TS, M1, [t, prev.get("m")])
            t = quarter(V, TC, TS, M1, t)
            t1 = A.did(A.on(t).activation(TS, TS, ACT.Sin))
            t2 = A.did(A.e.activation(TC, TC, ACT.Sin))
            ttab = [t1, t2]
            m3, m4 = M3.rearrange("p g (j h) -> p g j h", j=8), M4.rearrange("p g (j h) -> p g j h", j=8)
            ta = G.did(G.on(tset, prev.get("m34"), xr).tensor_tensor(m3, bc(QR[:, gs, :], 3, 16), bc(BB[:, gs, :], 2, 8), ALU.mult))
            tb = G.did(G.e.tensor_tensor(m4, bc(QI[:, gs, :], 3, 16), bc(BX[:, gs, :], 2, 8), ALU.mult))
            twn = G.did(G.on(ta, tb, prev.get("wn")).tensor_tensor(WN, M3, M4, ALU.add))
            ops = []
            for dst, x, y, op, key in ((PW, CC, CX, ALU.add, "pw"), (PS, CX, CC, ALU.subtract, "ps")):
                t = ops[-1] if ops else twn
                for s0, s1 in ((0, 5), (5, 9)):
                    ns = s1 - s0
                    a4 = M3.rearrange("p g (j h) -> p g j h", j=8)[:, :, 0:ns, :]
                    b4 = M4.rearrange("p g (j h) -> p g j h", j=8)[:, :, 0:ns, :]
                    ta = G.did(G.on(t).tensor_tensor(a4, bc(PR[:, gs, s0:s1], 3, 16), bc(x[:, gs, :], 2, ns), ALU.mult))
                    tb = G.did(G.e.tensor_tensor(b4, bc(PIm[:, gs, s0:s1], 3, 16), bc(y[:, gs, :], 2, ns), ALU.mult))
                    t = G.did(G.on(ta, tb, prev.get("y")).tensor_tensor(dst[:, :, s0:s1, :], a4, b4, op))
                ops.append(t)
            prev["m34"] = t
            tb = [G.did(G.on(tz, prev.get("toep")).tensor_copy(bp[gi][:, 112:128], BB[:, 4 * n + gi, :])) for gi in range(4)]
            yield
            kk_, bk, f = mis.take()
            for gi in range(4):
                P.on(f, twn, k.t_const)
                ins = k.tr(k.bank(bk)[:, 128 * gi:128 * gi + 128], WN[:, gi, :])
            t = P.did(ins)
            prev["wn"] = t
            b4 = k.bank(bk).rearrange("p (g m) -> p g m", g=4)
            A.on(t, prev.get("v"), xr)
            ta = A.did(A.e.activation(WT, b4, ACT.Copy))
            tb2 = A.did(A.e.activation(WS[:, :, 0:64], b4[:, :, 64:128], ACT.Copy))
            tc = A.did(A.e.activation(WS[:, :, 64:128], b4[:, :, 0:64], ACT.Copy, scale=-1.0))
            mis.give(kk_, tc)
            kk_, bk, f = mis.take()
            P.on(f, tb, ops[0])
            for gi in range(4):
                for j in range(8):
                    ins = k.mm(k.bank(bk)[:, 128 * gi + 16 * j:128 * gi + 128], bp[gi][:, 112 - 16 * j:240 - 16 * j],
                               PW[:, gi, 0:8 - j, :].rearrange("p s h -> p (s h)"), j == 0 and gi == 0, j == 7)
            t = P.did(ins)
            prev["toep"] = t
            ttp = A.did(A.on(t, prev.get("y"), xr).activation(TP, k.bank(bk).rearrange("p (g m) -> p g m", g=4), ACT.Copy))
            mis.give(kk_, ttp)
            yield
            k1, b1, f1 = mis.take()
            k2, b2, f2 = mis.take()
            P.on(ta, tb2, tc, tu, f1, f2)
            for wt, b_ in ((WT, b1), (WS, b2)):
                for gi in range(4):
                    ins = k.mm(k.bank(b_)[:, 128 * gi:128 * gi + 128], wt[:, gi, :], U[:, gi, :], gi == 0, True)
            t = P.did(ins)
            prev["v"] = t
            fl = lambda x: x.rearrange("p g m -> p (g m)")
            ta = V.did(V.on(t, ttab, prev.get("m")).tensor_tensor(fl(M1), k.bank(b1), fl(TC), ALU.mult))
            tb = V.did(V.e.tensor_tensor(fl(M2), k.bank(b2), fl(TS), ALU.mult))
            mis.give(k1, ta)
            mis.give(k2, tb)
            tw_ = V.did(V.on(ta, tb).tensor_tensor(fl(M1), fl(M1), fl(M2), ALU.add))
            tl_ = []
            for gi in range(4):
                tl_.append(V.did(V.on(tw_).tensor_tensor_scan(Z[:, gi, :], R8[:, 4 * n + gi:4 * n + gi + 1].to_broadcast([128, 128]),
                                                              M1[:, gi, :], 0.0, ALU.mult, ALU.add)))
            ta = V.did(V.on(*tl_, prev.get("y")).tensor_tensor(fl(M1), fl(Z), fl(TC), ALU.mult))
            tb = V.did(V.e.tensor_tensor(fl(M2), fl(Z), fl(TS), ALU.mult))
            prev["tcts"] = [ta, tb]
            yield
            kk_, bk, f = mis.take()
            P.on(f, ttp, ta, tb, ops)
            for gi in range(4):
                o = k.bank(bk)
                k.mm(o[:, 128 * gi:128 * gi + 128], TP[:, gi, :], U[:, gi, :], gi == 0, False)
                k.mm(o[:, 128 * gi + 1:128 * gi + 128], PW[:, gi, 1:9, :].rearrange("p s h -> p (s h)"), M1[:, gi, 0:127], False, False)
                ins = k.mm(o[:, 128 * gi + 1:128 * gi + 128], PS[:, gi, 1:9, :].rearrange("p s h -> p (s h)"), M2[:, gi, 0:127], False, True)
            t = P.did(ins)
            prev["y"] = prev["m"] = t
            V.on(t, tyd[-1] if tyd else None)
            ty = []
            for gi in range(4):
                ty.append(V.did(V.e.scalar_tensor_tensor(Y[:, gi, :], U[:, gi, :], k.sm("dsk")[:, 4 * n + gi:4 * n + gi + 1],
                                                         k.bank(bk)[:, 128 * gi:128 * gi + 128], ALU.mult, ALU.add)))
            mis.give(kk_, *ty)
            UR.give(kk, *ty)
            for gi in range(4):
                g = 4 * n + gi
                t = yd[n % 2].start(S, d["yscr"][16 * g:16 * g + 16].rearrange("h j c -> j h c"), Y[:, gi, :], ty)
            tyd.append(t)
            yield

    bg = ssm()

    def step(n=1):
        for _ in range(n):
            next(bg, None)

    step()
    w, tw = k.panel("w_q")
    tq = {}
    for m in range(4):
        def evac(half, ps, t, m=m):
            t = k.qk_norm(ps, t, QT[:, m, 512 * half:512 * half + 512], k.sm("qg_ev"), k.bones, mis, sq, rt, 1.0 / 64, [tsm, tbia, udone, trow])
            tq[m, half] = t
            return [t]
        tl = k.proj_T(w, tw, 128 * m, 128, proj, evac, xr)
        step()
    k.done("w_q", tl)
    w, tw = k.panel("w_kv")
    tk, tv = {}, {}

    def evac(half, ps, t):
        tk[half] = k.qk_norm(ps, t, KT[:, 512 * half:512 * half + 512], k.sm("kg_ev"), k.bones, mis, sq, rt, 1.0 / 64, [tsm, udone])
        return [tk[half]]
    k.proj_T(w, tw, 0, 128, proj, evac, xr)
    step()
    for b in range(8):
        kk, bk, f = proj.take()
        P.on(f)
        t = tl = k.proj_N(w, tw, 128, 128, b, k.bank(bk)[:, 0:128])
        tv[b] = A.did(A.on(t, udone).activation(VN[:, b, :], k.bank(bk)[:, 0:128], ACT.Copy))
        proj.give(kk, tv[b])
    k.done("w_kv", tl)
    step()
    w, tw = k.panel("w_ga")
    tga = {}
    for m in range(4):
        def evac(half, ps, t, m=m):
            tga[m, half] = A.did(A.on(t, udone, tset).activation(GA[:, m, 512 * half:512 * half + 512], ps, ACT.Silu))
            return [tga[m, half]]
        tl = k.proj_T(w, tw, 128 * m, 128, proj, evac, xr)
        step()
    k.done("w_ga", tl)

    st = {}
    tsink = A.did(A.on(tsm).activation(k.tiny[:, 224:232], k.sm("sink"), ACT.Copy, scale=-1.0))
    smr = Ring([k.tiny[:, 192 + 16 * i:208 + 16 * i] for i in range(2)])

    def s1(b, h):
        nk, k0 = (256, 128 * b - 128) if b else (128, 0)
        lk, Lb, lf = L.take()
        sk, sb, sf = smr.take()
        hl = slice(64 * h, 64 * h + 64)
        tls = []
        for pair in range(2):
            kk, bk, f = mis.take()
            P.on(f, tq[2 * pair, b // 4], tq[2 * pair + 1, b // 4], tk[b // 4], tk[0])
            for i in range(2):
                m = 2 * pair + i
                ins = k.mm(k.bank(bk)[:, 256 * i:256 * i + nk], QT[hl, m, 128 * b:128 * b + 128], KT[hl, k0:k0 + nk], i == 0, True)
            t = P.did(ins)
            Lv = Lb.rearrange("p (m n) -> p m n", m=4)[:, 2 * pair:2 * pair + 2, 0:nk]
            ps = k.bank(bk).rearrange("p (m n) -> p m n", m=2)[:, :, 0:nk]
            t = V.did(V.on(t, lf, tbia).scalar_tensor_tensor(Lv, ps, 0.125, BIA[:, 4 * h + 2 * pair:4 * h + 2 * pair + 2, 256 - nk:256], ALU.mult, ALU.add))
            mis.give(kk, t)
            tls.append(t)
        Lv = Lb.rearrange("p (m n) -> p m n", m=4)[:, :, 0:nk]
        nm, rs, es, di = sb[:, 0:4], sb[:, 4:8], sb[:, 8:12], sb[:, 12:16]
        t = V.did(V.on(tls, sf).tensor_reduce(nm, Lv, AX.X, ALU.max, negate=True))
        t = V.did(V.on(t, tsink).tensor_tensor(nm, nm, k.tiny[:, 224 + 4 * h:228 + 4 * h], ALU.min))
        t0 = V.did(V.on(t).tensor_tensor(es, nm, k.tiny[:, 224 + 4 * h:228 + 4 * h], ALU.subtract))
        te = []
        A.on(t, t0)
        for m in range(4):
            te.append(A.did(A.e.activation(Lv[:, m], Lv[:, m], ACT.Exp, bias=nm[:, m:m + 1], accum_out=rs[:, m:m + 1])))
        te.append(A.did(A.e.activation(es, es, ACT.Exp)))
        t = V.did(V.on(te).tensor_tensor(di, rs, es, ALU.add))
        t = V.did(V.on(t).reciprocal(di, di))
        ts = [V.did(V.on(t).tensor_scalar(Lv[:, m], Lv[:, m], di[:, m:m + 1], None, ALU.mult)) for m in range(4)]
        smr.give(sk, ts)
        st[b, h] = (nk, k0, lk, Lv, ts)

    def s2(b, h):
        nk, k0, lk, Lv, ts = st[b, h]
        pk, pt, pf = PT.take()
        nc_ = nk // 128
        tt = []
        for c in range(nc_):
            kk, bk, f = mis.take()
            P.on(f, ts)
            for m in range(4):
                ins = k.tr(k.bank(bk)[:, 128 * m:128 * m + 128], Lv[:, m, 128 * c:128 * c + 128])
            t = P.did(ins)
            if c == 1:
                t2 = V.did(V.on(t, pf).tensor_copy(pt[:, c, :], k.bank(bk)))
            else:
                t2 = A.did(A.on(t, pf).activation(pt[:, c, :], k.bank(bk), ACT.Copy))
            mis.give(kk, t2)
            tt.append(t2)
        L.give(lk, t)
        st[b, h] = (nk, k0, pk, pt, tt)

    tatt = []

    def s3(b, h):
        nk, k0, pk, pt, tt = st[b, h]
        hl = slice(64 * h, 64 * h + 64)
        kk, bk, f = mis.take()
        P.on(f, tt, tv[b], tv[max(b - 1, 0)])
        for c in range(nk // 128):
            ins = k.mm(k.bank(bk)[hl, :], VN[:, k0 // 128 + c, hl], pt[:, c, :], c == 0, c == nk // 128 - 1)
        t = P.did(ins)
        PT.give(pk, t)
        g = GA[hl, :, 128 * b:128 * b + 128]
        t = V.did(V.on(t, *[tga[m, b // 4] for m in range(4)]).tensor_tensor(g, k.bank(bk)[hl, :].rearrange("p (m q) -> p m q", m=4), g, ALU.mult))
        mis.give(kk, t)
        tatt.append(t)

    units = [(b, h) for b in range(8) for h in range(2)]
    for i in range(len(units) + 2):
        if i < len(units):
            s1(*units[i])
        if 1 <= i <= len(units):
            s2(*units[i - 1])
        if i >= 2:
            s3(*units[i - 2])
        step()
    step(99)

    YT = [k.at(Hb + 4 * KB * i, [8, 128]) for i in range(4)]
    YG = k.at(Hb + 16 * KB, [4, 1024])
    SM = QT
    mk = k.mark()
    tyg = []
    dmy = k.dma()
    ty = [dmy.start(S, YT[m], d["yscr"][128 * m:128 * m + 128], tyd[-1], tyd[-2], mk) for m in range(4)]
    for m in range(4):
        tyg.append(A.did(A.on(ty[-1], mk).activation(YG[:, m, :].rearrange("p (c j) -> p c j", j=8),
                                                     YT[m].rearrange("p j c -> p c j"), ACT.Gelu_apprx_tanh)))
    w, tw = k.panel("w_gb")
    tgb = {}
    for m in range(4):
        def evac(half, ps, t, m=m):
            tgb[m, half] = A.did(A.on(t, mk).activation(GB[:, m, 512 * half:512 * half + 512], ps, ACT.Silu))
            return [tgb[m, half]]
        tl = k.proj_T(w, tw, 128 * m, 128, proj, evac, xr)
    k.done("w_gb", tl)
    w, tw = k.panel("w_glu")
    tmix = []
    for m in range(4):
        for half in range(2):
            hs_ = slice(512 * half, 512 * half + 512)
            kk1, b1, f1 = mis.take()
            kk2, b2, f2 = mis.take()
            P.on(f1, f2, tw, tyg)
            for bk, col in ((b1, 512 + 128 * m), (b2, 128 * m)):
                for q_ in range(4):
                    ins = k.mm(k.bank(bk), w[:, q_, col:col + 128], YG[:, q_, hs_], q_ == 0, q_ == 3)
                if bk == b1:
                    tg = P.did(ins)
            ta = tl = P.did(ins)
            sk, sb, sf = sq.take()
            t = A.did(A.on(tg, sf, mk).activation(sb, k.bank(b1), ACT.Sigmoid, bias=k.sm("glub")[:, 4 + m:5 + m]))
            mis.give(kk1, t)
            t = V.did(V.on(t, ta, mk).scalar_tensor_tensor(SM[:, m, hs_], k.bank(b2), k.sm("glub")[:, m:m + 1], sb, ALU.add, ALU.mult))
            mis.give(kk2, t)
            sq.give(sk, t)
            tmix.append(V.did(V.on(t, tgb[m, half]).tensor_tensor(SM[:, m, hs_], SM[:, m, hs_], GB[:, m, hs_], ALU.mult)))
    k.done("w_glu", tl)
    dx = k.dma()
    tx = dx.start(S, k.H, d["x"].rearrange("(b p) n -> p b n", p=128), tl, k.mark())
    tH = []
    for h in range(2):
        w, tw = k.panel(f"w_eo{h}")
        P.on(tatt, tmix)
        for b in range(8):
            kk, bk, f = proj.take()
            P.on(f)
            k.proj_N(w[:, 0:4], tw, 0, 512, b, k.bank(bk), X=GA, nk=4, stop=False)
            t = tl = k.proj_N(w[:, 4:8], tw, 0, 512, b, k.bank(bk), X=SM, nk=4, start=False)
            o = k.H[:, b, 512 * h:512 * h + 512]
            t = V.did(V.on(t, tx).tensor_tensor(o, k.bank(bk), o, ALU.add))
            proj.give(kk, t)
            tH.append(t)
        k.done(f"w_eo{h}", tl)
    return {b: [tH[b], tH[8 + b]] for b in range(8)}


def odd(k, tH):
    nc, d, V, A, P, G, S = k.nc, k.d, k.V, k.A, k.P, k.G, k.S
    PH = k.PH0
    mk0 = k.mark()
    QT, GT = k.at(PH, [8, 1024]), k.at(PH + 32 * KB, [8, 1024])
    KT, VN = k.at(PH + 64 * KB, [2, 1024]), k.at(PH + 72 * KB, [8, 256])
    MK = k.at(PH + 80 * KB, [33 * 128], BF16)
    TN = k.at(PH + 80 * KB + 8448, [128])
    mo = {b: sum(128 * (c + 1) for c in range(2, b)) for b in range(2, 9)}
    H0 = k.H0
    QI, KI = k.at(H0, [4, 1024]), k.at(H0 + 16 * KB, [1024])
    rel = Ring([k.at(H0 + 20 * KB + 2 * KB * i, [512]) for i in range(2)])
    scr = Ring([k.at(H0 + 24 * KB + 4 * KB * i, [1024]) for i in range(2)])
    WI = k.tiny[:, 128:192].rearrange("p (b n) -> p b n", b=8)
    m8 = k.tiny[:, 64:72]
    proj = Ring([0, 1])
    mis = Ring([2, 3, 4, 5, 6, 7])
    tsm = k.t_small

    XN = QT
    k.wjunk = mk0
    junk = k.at(PH + 64 * KB, [1024])
    ready = [k.rms_rows(k.H[:, b, :], b, XN[:, b, :], [tH[b], mk0], 1e-6, junk) for b in range(8)]
    dh = k.dma()
    tsp = dh.start(S, d["hscr"].rearrange("(b p) n -> p b n", p=128), k.H, [tH[b] for b in range(8)])
    k.P.on(mk0)
    tX = k.transpose_to(XN, k.XT, mis, ready, scale=k.sm("g_od"))
    xr = list(tX.values())
    free = [tsp, ready, k.A.now()]
    t = G.did(G.on(mk0).memset(TN, 0.0))
    tTN = G.did(G.on(t).affine_select(out=TN, in_=TN, compare_op=ALU.is_ge, fill=NEG, base=0,
                                      pattern=[[-1, 128]], channel_multiplier=1))

    w, tw = k.panel("w_qi")
    tqi, tki = {}, {}
    for m in range(4):
        def evac(half, ps, t, m=m):
            tqi[m, half] = A.did(A.on(t, free).activation(QI[:, m, 512 * half:512 * half + 512], ps, ACT.Copy))
            return [tqi[m, half]]
        tl = k.proj_T(w, tw, 128 * m, 128, proj, evac, xr)
    k.done("w_qi", tl)
    w, tw = k.panel("w_ki")

    def evac(half, ps, t):
        tki[half] = A.did(A.on(t, free).activation(KI[:, 512 * half:512 * half + 512], ps, ACT.Copy))
        return [tki[half]]
    k.proj_T(w, tw, 0, 128, proj, evac, xr)
    kk, bk, f = proj.take()
    P.on(f)
    for b in range(8):
        tl = k.proj_N(w, tw, 128, 8, b, k.bank(bk)[:, 8 * b:8 * b + 8], start=(b == 0))
    twi = A.did(A.on(tl, mk0).activation(WI, k.bank(bk)[:, 0:64].rearrange("p (b n) -> p b n", b=8), ACT.Copy, scale=8 ** -0.5))
    proj.give(kk, twi)
    k.done("w_ki", tl)

    scores, tmk = {}, {}

    def score(b):
        n = 128 * (b + 1)
        sk, sc, sf = scr.take()
        first = {}
        for h in range(8):
            hl = slice(64 * (h % 2), 64 * (h % 2) + 64)
            for c in range(0, n, 512):
                e = min(n, c + 512)
                kk, bk, f = mis.take()
                P.on(f, tqi[h // 2, b // 4], tki[0], tki[(e - 1) // 512])
                t = P.did(k.mm(k.bank(bk)[:, 0:e - c], QI[hl, h // 2, 128 * b:128 * b + 128], KI[hl, c:e], True, True))
                rk, rb, rf = rel.take()
                t = A.did(A.on(t, rf, free).activation(rb[:, 0:e - c], k.bank(bk)[:, 0:e - c], ACT.Relu, scale=0.125))
                mis.give(kk, t)
                wv = WI[:, b, h:h + 1]
                if h == 0:
                    t = V.did(V.on(t, sf, twi, free).tensor_scalar(sc[:, c:e], rb[:, 0:e - c], wv, None, ALU.mult))
                else:
                    t = V.did(V.on(t, first[c]).scalar_tensor_tensor(sc[:, c:e], rb[:, 0:e - c], wv, sc[:, c:e], ALU.mult, ALU.add))
                first[c] = t
                rel.give(rk, t)
            yield
        t = V.did(V.on(*first.values(), tTN).tensor_tensor(sc[:, n - 128:n], sc[:, n - 128:n], TN, ALU.add))
        scores[b] = (sk, sc, t)

    def select(b):
        n = 128 * (b + 1)
        sk, sc, t = scores[b]
        for r in range(32):
            t = V.did(V.on(t).max(m8, sc[:, 0:n]))
            t = V.did(V.on(t).match_replace(sc[:, 0:n], m8, sc[:, 0:n], -3e38))
            yield
        tmk[b] = V.did(V.on(t).tensor_scalar(MK[:, mo[b]:mo[b] + n], sc[:, 0:n], -2e38, NEG, ALU.is_gt, ALU.mult))
        scr.give(sk, tmk[b])
        yield

    order = [7, 6, 5, 4, 3, 2]

    def chain():
        yield from score(order[0])
        for i, b in enumerate(order):
            nxt = score(order[i + 1]) if i + 1 < 6 else iter(())
            for j, _ in enumerate(select(b)):
                if j % 3 == 0:
                    next(nxt, None)
                yield
            for _ in nxt:
                pass

    bg = chain()
    for _ in range(8):
        next(bg)

    def step(n):
        for _ in range(n):
            next(bg, None)

    rt1 = Ring([GT[:, 7, 0:512]])
    sq1 = Ring([GT[:, 7, 512:1024]])
    w, tw = k.panel("w_okv")
    tk, tq, tv, tg = {}, {}, {}, {}
    for m in range(2):
        def evac(half, ps, t, m=m):
            step(2)
            tk[m, half] = k.qk_norm(ps, t, KT[:, m, 512 * half:512 * half + 512], k.sm("kg_od"), k.ones, mis, sq1, rt1, 1.0 / 128, [tsm, k.A.now()])
            return [tk[m, half]]
        k.proj_T(w, tw, 128 * m, 128, proj, evac, xr)
    for b in range(8):
        kk, bk, f = proj.take()
        P.on(f)
        t = tl = k.proj_N(w, tw, 256, 256, b, k.bank(bk)[:, 0:256])
        tv[b] = A.did(A.on(t).activation(VN[:, b, :], k.bank(bk)[:, 0:256], ACT.Copy))
        proj.give(kk, tv[b])
        step(2)
    k.done("w_okv", tl)
    qg = k.tiny[:, 80:81]
    tqg = V.did(V.on(tsm).tensor_scalar(qg, k.sm("qg_od"), 128 ** -0.5, None, ALU.mult))
    for h2 in range(2):
        w, tw = k.panel(f"w_oq{h2}")
        for m in range(4):
            def evac(half, ps, t, m=4 * h2 + m):
                step(2)
                tq[m, half] = k.qk_norm(ps, t, QT[:, m, 512 * half:512 * half + 512], qg, k.ones, mis, sq1, rt1, 1.0 / 128, [tqg, xr])
                return [tq[m, half]]
            tl = k.proj_T(w, tw, 128 * m, 128, proj, evac, xr)
        k.done(f"w_oq{h2}", tl)
    for h2 in range(2):
        w, tw = k.panel(f"w_og{h2}")
        for m in range(4):
            def evac(half, ps, t, m=4 * h2 + m):
                step(3)
                tg[m, half] = A.did(A.on(t, [tq[7, 1], tq[7, 0]]).activation(GT[:, m, 512 * half:512 * half + 512], ps, ACT.Silu))
                return [tg[m, half]]
            tl = k.proj_T(w, tw, 128 * m, 128, proj, evac, xr)
        k.done(f"w_og{h2}", tl)
    step(9999)

    mk = k.mark()
    X0 = k.X0
    strips = Ring([k.at(H0 + 4 * KB * i, [1024]) for i in range(2)])
    bms = Ring([k.at(H0 + 8 * KB + 4 * KB * i, [1024]) for i in range(2)])
    pr = Ring([k.at(H0 + 16 * KB + 4 * KB * i, [1024]) for i in range(3)])
    pts = Ring([k.at(X0 + 16 * KB * i, [8, 4, 128]) for i in range(2)])
    smr = Ring([k.tiny[:, 128 + 8 * i:136 + 8 * i] for i in range(3)])
    pairs, ptb, avb = Ring([4, 6]), Ring([0, 1, 2]), Ring([3])
    for r in (strips, bms, pr, pts, smr, pairs, ptb, avb):
        r.free = [list(mk) for _ in r.items]
    raws = Ring([k.at(H0 + 28 * KB, [1024])])
    raws.free = [list(mk)]
    sdm = k.dma()
    cur, st, tatt = {}, {}, []

    def load_strip(n):
        rk, rb, rf = raws.take()
        t = sdm.start(S, rb, bass.AP(d["strip"].tensor, n * (STRIP_A + STRIP_B) + STRIP_A, [[1, 128], [1, 1024]]), rf, k.t_strip)
        return rk, rb, t

    def turn_strip(n, raw):
        rk, rb, tr_ = raw
        sk, sb, sf = strips.take()
        toks = []
        for c in range(2):
            kk, bk, f = ptb.take()
            t = P.did(P.on(f, tr_).matmul(k.bank(bk), k.flip, rb[:, 512 * c:512 * c + 512], start=True, stop=True))
            t2 = A.did(A.on(t, sf).activation(sb[:, 512 * c:512 * c + 512], k.bank(bk), ACT.Copy))
            ptb.give(kk, t2)
            toks.append(t2)
        raws.give(rk, t)
        cur[n] = (sk, sb, toks, [])

    pend = {}

    def s1(n, b):
        nk = 128 * (b + 1)
        if n == 0 and b == 0:
            turn_strip(0, load_strip(0))
        if n < 7 and b == 0:
            pend[n + 1] = load_strip(n + 1)
        if n < 7 and b == 5:
            turn_strip(n + 1, pend[n + 1])
        sk, sb, tst, users = cur[n]
        win = sb[:, 1024 - nk:1024]
        if b >= 2:
            bk_, bm, bf = bms.take()
            t = G.did(G.on(tst, bf, tmk[b]).tensor_tensor(bm[:, 0:nk], win, MK[:, mo[b]:mo[b] + nk], ALU.add))
            win, tst2 = bm[:, 0:nk], t
            users.append(t)
        else:
            tst2 = tst
        kk, bk, f = pairs.take()
        P.on(f)
        for c in range(0, nk, 512):
            e = min(nk, c + 512)
            P.on(tq[n, b // 4], tk[n // 4, 0], tk[n // 4, (e - 1) // 512])
            ins = k.mm(k.bank(bk + c // 512)[:, 0:e - c], QT[:, n, 128 * b:128 * b + 128], KT[:, n // 4, c:e], True, True)
        t = P.did(ins)
        pk, pb, pf = pr.take()
        mk_, sb_, sf = smr.take()
        p = pb[:, 0:nk]
        t = V.did(V.on(t, tst2, pf, sf).tensor_tensor_reduce(out=p, in0=k.bank(bk, 2)[:, 0:nk], in1=win, scale=1.0, scalar=-3e38,
                                                            op0=ALU.add, op1=ALU.max, accum_out=sb_[:, 0:1]))
        pairs.give(kk, t)
        if b >= 2:
            bms.give(bk_, t)
        else:
            users.append(t)
        if b == 7:
            strips.give(sk, users)
        t = V.did(V.on(t).tensor_scalar(sb_[:, 1:2], sb_[:, 0:1], -1.0, None, ALU.mult))
        t = A.did(A.on(t).activation(p, p, ACT.Exp, bias=sb_[:, 1:2], accum_out=sb_[:, 2:3]))
        st[n, b] = [t, pk, p, mk_, sb_]

    def s1b(n, b):
        t, pk, p, mk_, sb_ = st[n, b]
        t = V.did(V.on(t).reciprocal(sb_[:, 3:4], sb_[:, 2:3]))
        t = V.did(V.on(t).tensor_scalar(p, p, sb_[:, 3:4], None, ALU.mult))
        smr.give(mk_, t)
        st[n, b] = (t, pk, p)

    quad = {}

    def s2(n, b):
        t0, pk, p = st[n, b]
        Q = b // 4
        if b % 4 == 0:
            quad[n, Q] = [*pts.take(), []]
        qk, pt, qf, toks = quad[n, Q]
        for j0 in range(0, b + 1, 4):
            nj = min(4, b + 1 - j0)
            kk, bk, f = ptb.take()
            P.on(f, t0)
            for j in range(nj):
                ins = k.tr(k.bank(bk)[:, 128 * j:128 * j + 128], p[:, 128 * (j0 + j):128 * (j0 + j) + 128])
            t = P.did(ins)
            o = pt[:, j0:j0 + nj, b % 4, :]
            src = k.bank(bk)[:, 0:128 * nj].rearrange("p (j q) -> p j q", j=nj)
            if j0 == 0 and b % 4 != 3:
                t2 = A.did(A.on(t, qf).activation(o, src, ACT.Copy))
            else:
                t2 = V.did(V.on(t, qf).tensor_copy(o, src))
            ptb.give(kk, t2)
            toks.append(t2)
        pr.give(pk, t)

    def s3(n, Q):
        qk, pt, qf, toks = quad[n, Q]
        kk, bk, f = avb.take()
        P.on(f, toks, list(tv.values()))
        kv = n // 4
        last = 4 * Q + 3
        for j in range(last + 1):
            q0 = max(0, j - 4 * Q)
            ins = k.mm(k.bank(bk)[:, 128 * q0:512], VN[:, j, 128 * kv:128 * kv + 128],
                       pt[:, j, q0:4, :].rearrange("p q s -> p (q s)"), j == 0, j == last)
        t = P.did(ins)
        pts.give(qk, t)
        g = GT[:, n, 512 * Q:512 * Q + 512]
        t = V.did(V.on(t, tg[n, Q]).tensor_tensor(g, k.bank(bk), g, ALU.mult))
        avb.give(kk, t)
        tatt.append(t)

    units = [(n, b) for n in range(8) for b in range(8)]
    for i in range(len(units) + 3):
        if i < len(units):
            s1(*units[i])
        if 1 <= i <= len(units):
            s1b(*units[i - 1])
        if 2 <= i <= len(units) + 1:
            s2(*units[i - 2])
        if i >= 3 and units[i - 3][1] % 4 == 3:
            s3(units[i - 3][0], units[i - 3][1] // 4)

    tx = k.dma().start(S, k.H, d["hscr"].rearrange("(b p) n -> p b n", p=128), tsp, k.mark())
    proj = Ring([0, 1, 2])
    proj.free = [list(k.mark()) for _ in range(3)]
    out = {b: [] for b in range(8)}
    for h in range(2):
        w, tw = k.panel(f"w_oo{h}")
        P.on(tatt)
        for b in range(8):
            kk, bk, f = proj.take()
            P.on(f)
            t = tl = k.proj_N(w, tw, 0, 512, b, k.bank(bk), X=GT)
            o = k.H[:, b, 512 * h:512 * h + 512]
            t = V.did(V.on(t, tx).tensor_tensor(o, k.bank(bk), o, ALU.add))
            proj.give(kk, t)
            out[b].append(t)
        k.done(f"w_oo{h}", tl)
    return out


def second(k, tH, out_d):
    nc, d, V, A, P, G, S = k.nc, k.d, k.V, k.A, k.P, k.G, k.S
    PH, H0, X0 = k.PH0, k.H0, k.X0
    mk = k.mark()
    tsm = k.t_small
    CV, XN = k.at(PH, [8, 1024]), k.at(PH + 32 * KB, [8, 1024])
    BT, CT, BN = k.at(PH + 64 * KB, [2, 1024]), k.at(PH + 72 * KB, [2, 1024]), k.at(PH + 80 * KB, [8, 256])
    DT, AD = k.at(PH + 88 * KB, [8, 16]), k.at(PH + 88 * KB + 512, [8, 16])
    proj = Ring([0, 1, 2])
    mis = Ring([3, 4, 5, 6, 7])
    for r in (proj, mis):
        r.free = [list(mk) for _ in r.items]

    def row(i):
        return d["lnp"][i:i + 1, :].partition_broadcast(128)

    def bcast(i, off, after):
        ap = k.at(off, [1024])
        return ap, k.dma().start(S, ap, row(i), after)

    (g0, t0), (b0, t1), (bo, t2) = (bcast(i, PH + 4 * KB * j, mk) for j, i in enumerate((0, 1, 6)))
    G.on(mk)
    ready = [k.ln_rows(k.H[:, b, :], b, k.H[:, b, :], [tH[b], mk], 1e-5, g0, b0, [t0, t1]) for b in range(8)]
    tX = k.transpose_to(k.H, k.XT, mis, ready)
    xr = list(tX.values())
    tb = [V.did(V.on(ready[b], P.now(), t2).scalar_tensor_tensor(k.H[:, b, :], k.H[:, b, :], ALPHA, bo, ALU.mult, ALU.add)) for b in range(8)]
    tsp = k.dma().start(S, d["hscr"].rearrange("(b p) n -> p b n", p=128), k.H, tb)

    UP = 4352
    ur = Ring([k.at(H0 + UP * i, [1054]) for i in range(2)])
    sg = Ring([k.at(H0 + 2 * UP + 2 * KB * i, [512]) for i in range(2)])
    xp = Ring([k.at(H0 + 2 * UP + 4 * KB + 4224 * i, [1027]) for i in range(2)])
    tm = Ring([k.at(H0 + 2 * UP + 4 * KB + 2 * 4224 + 4 * KB * i, [1024]) for i in range(2)])
    tzero = [G.did(G.on(tsp).memset(u[:, 0:30], 0.0)) for u in ur.items] + [G.did(G.e.memset(x[:, 0:3], 0.0)) for x in xp.items]

    convq = []

    def conv(m, uk, u, tu):
        w = k.sm("cfw", 31 * m, 31 * m + 31)
        o = CV[:, m, :]
        t = V.did(V.on(tu, tsm, tb).tensor_scalar(o, u[:, 0:1024], w[:, 0:1], k.sm("cfb")[:, m:m + 1], ALU.mult, ALU.add))
        yield
        for j in range(1, 31):
            t = V.did(V.on(t).scalar_tensor_tensor(o, u[:, j:j + 1024], w[:, j:j + 1], o, ALU.mult, ALU.add))
            if j < 30:
                yield
        tcv[m] = t
        ur.give(uk, t)
        yield

    tcv = {}

    def step(n):
        while n > 0 and convq:
            if next(convq[0], "end") == "end":
                convq.pop(0)
            else:
                n -= 1

    def glu(m):
        w, tw = k.panel(f"w_cf{m // 2}")
        c = 256 * (m % 2)
        while ur.free[(ur.k + 1) % 2] is None:
            step(1)
        uk, u, uf = ur.take()
        toks = []
        for half in range(2):
            k1_, b1, f1 = proj.take()
            P.on(f1, tw, xr)
            for kk in range(8):
                ins = k.mm(k.bank(b1), w[:, kk, c + 128:c + 256], k.XT[:, kk, 512 * half:512 * half + 512], kk == 0, kk == 7)
            t = P.did(ins)
            sk, sb, sf = sg.take()
            t = A.did(A.on(t, sf, tsp).activation(sb, k.bank(b1), ACT.Sigmoid, bias=k.sm("bglu")[:, 8 + m:9 + m]))
            proj.give(k1_, t)
            k2_, b2, f2 = proj.take()
            P.on(f2)
            for kk in range(8):
                ins = k.mm(k.bank(b2), w[:, kk, c:c + 128], k.XT[:, kk, 512 * half:512 * half + 512], kk == 0, kk == 7)
            t2 = tl = P.did(ins)
            t = V.did(V.on(t, t2, uf, tzero).scalar_tensor_tensor(u[:, 30 + 512 * half:542 + 512 * half], k.bank(b2), k.sm("bglu")[:, m:m + 1],
                                                                  sb, ALU.add, ALU.mult))
            proj.give(k2_, t)
            sg.give(sk, t)
            toks.append(t)
            step(8)
        convq.append(conv(m, uk, u, toks))
        if m % 2:
            k.done(f"w_cf{m // 2}", tl)

    txn, tbt, tct, tbn = {}, {}, {}, {}

    def xbc(i):
        name, c = (f"w_xs{i // 4}", 128 * (i % 4)) if i < 8 else ("w_bc", 128 * (i - 8))
        w, tw = k.panel(name)
        xk, x, xf = xp.take()
        toks = []

        def evac(half, ps, t):
            toks.append(A.did(A.on(t, xf, tzero).activation(x[:, 3 + 512 * half:515 + 512 * half], ps, ACT.Copy)))
            return [toks[-1]]
        tl = k.proj_T(w, tw, c, 128, proj, evac, xr)
        if i % 4 == 3:
            k.done(name, tl)
        tk_, tmp, tf = tm.take()
        cw = k.sm("cxw", 4 * i, 4 * i + 4)
        t = V.did(V.on(toks, tf, tsm).tensor_scalar(tmp, x[:, 0:1024], cw[:, 0:1], k.sm("cxb")[:, i:i + 1], ALU.mult, ALU.add))
        for j in range(1, 4):
            t = V.did(V.on(t).scalar_tensor_tensor(tmp, x[:, j:j + 1024], cw[:, j:j + 1], tmp, ALU.mult, ALU.add))
        xp.give(xk, t)
        if i >= 8:
            dst = BT if i < 10 else CT
            t = A.did(A.on(t).activation(dst[:, i % 2, :], tmp, ACT.Silu))
            tm.give(tk_, t)
            (tbt if i < 10 else tct)[i % 2] = t
            if i >= 10:
                return
            src = dst[:, i % 2, :]
        else:
            t = A.did(A.on(t).activation(tmp, tmp, ACT.Silu))
            src = tmp
        for half in range(2):
            kk, bk, f = mis.take()
            P.on(f, t)
            for j in range(4):
                b = 4 * half + j
                ins = k.tr(k.bank(bk)[:, 128 * j:128 * j + 128], src[:, 128 * b:128 * b + 128])
            t1 = P.did(ins)
            o = (XN[:, 4 * half:4 * half + 4, 128 * i:128 * i + 128] if i < 8 else
                 BN[:, 4 * half:4 * half + 4, 128 * (i - 8):128 * (i - 8) + 128])
            t2 = A.did(A.on(t1, mk).activation(o, k.bank(bk).rearrange("p (b n) -> p b n", b=4), ACT.Copy))
            mis.give(kk, t2)
            (txn if i < 8 else tbn)[i % 8, half] = t2
        if i < 8:
            tm.give(tk_, t1)

    seq = [8, 9, 10, 11, 0, 1, 2, 3, 4, 5, 6, 7]
    for m in range(8):
        glu(m)
        n = 2 if m % 2 == 0 else 1
        for _ in range(n):
            step(6)
            xbc(seq.pop(0))
            step(6)
        while len(convq) > 1:
            step(1)

    w, tw = k.panel("w_dt")
    kk, bk, f = mis.take()
    P.on(f, xr)
    for b in range(8):
        tl = k.proj_N(w, tw, 0, 16, b, k.bank(bk)[:, 16 * b:16 * b + 16], start=(b == 0))
    k.done("w_dt", tl)
    v8 = k.bank(bk)[:, 0:128].rearrange("p (b n) -> p b n", b=8)
    an = k.tiny[:, 224:240]
    t = V.did(V.on(tl, tsm, mk).tensor_tensor(DT, v8, bc(k.sm("dtb"), 1, 8), ALU.add))
    mis.give(kk, t)
    t1 = A.did(A.on(t).activation(AD, DT, ACT.Abs))
    t1 = A.did(A.on(t1).activation(AD, AD, ACT.Exp, scale=-1.0))
    t1 = A.did(A.on(t1).activation(AD, AD, ACT.Ln, bias=1.0))
    t3 = A.did(A.on(mk, ready).activation(an, k.sm("alog"), ACT.Exp))
    tdt = V.did(V.on(t1).scalar_tensor_tensor(DT, DT, 0.0, AD, ALU.max, ALU.add))
    tad = V.did(V.on(tdt, t3).scalar_tensor_tensor(AD, DT, -1.0, bc(an, 1, 8), ALU.mult, ALU.mult))
    while convq:
        step(1)

    mk2 = k.mark()
    R = Ring([k.at(H0, [8, 128])])
    E = Ring([k.at(H0 + 4 * KB + 4 * KB * i, [8, 128]) for i in range(2)])
    XD = Ring([k.at(H0 + 12 * KB + 2 * KB * i, [8, 64]) for i in range(2)])
    XE = Ring([k.at(H0 + 16 * KB + 2 * KB * i, [8, 64]) for i in range(2)])
    YB = Ring([k.at(H0 + 20 * KB + 2 * KB * i, [8, 64]) for i in range(2)])
    ZS = Ring([k.at(H0 + 24 * KB + 2 * KB * i, [512]) for i in range(2)])
    PV = k.at(H0 + 28 * KB, [2, 8, 64])
    EX = Ring([k.tiny[:, 48 * i:48 * i + 48] for i in range(2)])
    CB = Ring([k.tiny[:, 96:224]])
    for r in (R, E, XD, XE, YB, ZS, EX, CB):
        r.free = [list(mk2) for _ in r.items]
    zp, segp, one = Ring([0, 1]), Ring([2]), Ring([4, 5, 6, 7])
    for r in (zp, segp, one):
        r.free = [list(mk2) for _ in r.items]
    z0, z1 = k.panel("w_z0"), k.panel("w_z1")
    tyn, tpv = {}, {0: None, 1: None}
    fl = lambda x: x.rearrange("p a b -> p (a b)")

    def chunk(c):
        ek, ex, ef = EX.take()
        kk, bk, f = one.take()
        P.on(f, tad, k.t_const)
        for i, m_ in enumerate((k.tle, k.tgt, k.ones)):
            ins = k.mm(k.bank(bk)[:, 16 * i:16 * i + 16], m_, AD[:, c, :], i == 0, i == 2)
        t = P.did(ins)
        tex = A.did(A.on(t, ef).activation(ex, k.bank(bk)[:, 0:48], ACT.Exp))
        one.give(kk, tex)
        return ek, ex, tex

    def pre(c, g, ex, tex):
        s = {}
        cs = slice(128 * c, 128 * c + 128)
        hs = slice(8 * g, 8 * g + 8)
        rk, r, rf = R.take()
        t = G.did(G.on(rf, tad, k.t_const).tensor_tensor(r, bc(AD[:, c, hs], 2, 128), bc(k.tle, 1, 8), ALU.mult))
        kk, bk, f = segp.take()
        P.on(t, f)
        for i in range(2):
            ins = k.mm(k.bank(bk + i), k.tgt, fl(r)[:, 512 * i:512 * i + 512], True, True)
        t = P.did(ins)
        R.give(rk, t)
        s["ek"], e, ef = E.take()
        te = A.did(A.on(t, ef).activation(fl(e), k.bank(bk, 2), ACT.Exp))
        segp.give(kk, te)
        kk, bk, f = one.take()
        P.on(f, tbt[g], tct[g])
        t = P.did(k.mm(k.bank(bk)[:, 0:128], BT[:, g, cs], CT[:, g, cs], True, True))
        ck, cb, cf = CB.take()
        t = V.did(V.on(t, cf).tensor_tensor(cb, k.bank(bk)[:, 0:128], k.tle, ALU.mult))
        one.give(kk, t)
        s["tE"] = V.did(V.on(t, te).tensor_tensor(e, e, bc(cb, 1, 8), ALU.mult))
        CB.give(ck, s["tE"])
        x = XN[:, c, 512 * g:512 * g + 512].rearrange("p (h q) -> p h q", h=8)
        s["xk"], xd, xf = XD.take()
        s["tx"] = V.did(V.on(xf, tdt, [txn[i, c // 4] for i in range(8)]).tensor_tensor(xd, x, bc(DT[:, c, hs], 2, 64), ALU.mult))
        s["yk"], y, yf = YB.take()
        s["tD"] = G.did(G.on(yf, [txn[i, c // 4] for i in range(8)]).tensor_tensor(y, x, bc(k.sm("dk2")[:, hs], 2, 64), ALU.mult))
        s["ak"], xe, af = XE.take()
        s["ta"] = G.did(G.on(s["tx"], tex, af).tensor_tensor(xe, xd, bc(ex[:, 16 + 8 * g:24 + 8 * g], 2, 64), ALU.mult))
        s.update(e=e, xd=xd, y=y, xe=xe, x=x, cs=cs)
        return s

    def zproj(c, g, s):
        w, tw = (z0, z1)[g]
        kk, bk, f = zp.take()
        P.on(f)
        t = k.proj_N(w, tw, 0, 512, c, k.bank(bk))
        s["zk"], zs, zf = ZS.take()
        s["tz"] = A.did(A.on(t, zf).activation(zs, k.bank(bk), ACT.Silu))
        s["zs"] = zs
        zp.give(kk, s["tz"])
        return t

    def post(c, g, ex, tex, s):
        e, xd, y, xe, x = s["e"], s["xd"], s["y"], s["xe"], s["x"]
        kk, bk, f = one.take()
        P.on(f, s["tE"], s["tx"])
        for h in range(8):
            ins = k.mm(k.bank(bk)[:, 64 * h:64 * h + 64], e[:, h, :], xd[:, h, :], h == 0, True)
        t = P.did(ins)
        XD.give(s["xk"], t, s["ta"])
        t = ty = V.did(V.on(t, s["tD"]).tensor_tensor(y, y, k.bank(bk).rearrange("p (h q) -> p h q", h=8), ALU.add))
        one.give(kk, t)
        if c:
            kk, bk, f = one.take()
            P.on(f, tpv[g])
            t = P.did(k.mm(k.bank(bk), CT[:, g, s["cs"]], fl(PV[:, g]), True, True))
            tpr = t
            t = V.did(V.on(t, tex, ty).tensor_tensor(e[:, :, 0:64], k.bank(bk).rearrange("p (h q) -> p h q", h=8), bc(ex[:, 8 * g:8 * g + 8], 2, 64), ALU.mult))
            one.give(kk, t)
            t = V.did(V.on(t).tensor_tensor(y, y, e[:, :, 0:64], ALU.add))
        E.give(s["ek"], t)
        t0 = t
        kk, bk, f = one.take()
        P.on(f, s["ta"], tbn[g, c // 4])
        t = P.did(k.mm(k.bank(bk), BN[:, c, 128 * g:128 * g + 128], fl(xe), True, True))
        XE.give(s["ak"], t)
        pv = PV[:, g]
        if c == 0:
            tpv[g] = A.did(A.on(t).activation(fl(pv), k.bank(bk), ACT.Copy))
        else:
            t1 = G.did(G.on(tex, tpr, tpv[g]).tensor_tensor(pv, pv, bc(ex[:, 32 + 8 * g:40 + 8 * g], 2, 64), ALU.mult))
            tpv[g] = V.did(V.on(t, t1).tensor_tensor(fl(pv), fl(pv), k.bank(bk), ALU.add))
        one.give(kk, tpv[g])
        t = V.did(V.on(t0, s["tz"]).tensor_tensor(fl(y), fl(y), s["zs"], ALU.mult))
        ss = k.tiny[:, 240 + 2 * g:241 + 2 * g]
        rs = k.tiny[:, 241 + 2 * g:242 + 2 * g]
        t = A.did(A.on(t, tyn.get((c - 1, g))).activation(s["zs"], fl(y), ACT.Square, accum_out=ss))
        ZS.give(s["zk"], t)
        t = G.did(G.on(t).tensor_scalar(rs, ss, 1.0 / 512, 1e-5, ALU.mult, ALU.add))
        t = G.did(G.on(t).tensor_tensor(ss, rs, k.mhalf[:, 0:1], ALU.pow))
        t = V.did(V.on(t, s["tx"], s["tD"]).tensor_scalar(XN[:, c, 512 * g:512 * g + 512], fl(y), ss, None, ALU.mult))
        YB.give(s["yk"], t)
        tyn[c, g] = t
        return t

    prev = None
    for c in range(8):
        ek, ex, tex = chunk(c)
        for g in range(2):
            s = pre(c, g, ex, tex)
            tl = zproj(c, g, s)
            if prev is not None:
                post(*prev)
                if prev[1] == 1:
                    EX.give(pek, V.now(), G.now())
            prev = (c, g, ex, tex, s)
        pek = ek
    k.done("w_z0", tl)
    k.done("w_z1", tl)
    post(*prev)

    mk3 = k.mark()
    SM = k.at(H0, [8, 1024])
    mis = Ring([3, 4, 5, 6, 7])
    proj = Ring([0, 1, 2])
    for r in (proj, mis):
        r.free = [list(mk3) for _ in r.items]
    V.on(mk3)
    A.on(mk3)
    tS = k.transpose_to(XN, SM, mis, [[tyn[b, 0], tyn[b, 1]] for b in range(8)], scale=k.sm("sng"))
    ts = list(tS.values())

    Q0 = PH + 32 * KB
    MU, RS = k.at(Q0, [1024]), k.at(Q0 + 4 * KB, [1024])
    sq = Ring([k.at(Q0 + 8 * KB + 4 * KB * i, [1024]) for i in range(2)])
    cgr = Ring([k.at(Q0 + 16 * KB + 4 * KB * i, [1024]) for i in range(4)])
    tp = P.now()
    tmu = []
    for half in range(2):
        kk, bk, f = mis.take()
        P.on(f, list(tcv.values()))
        for m in range(8):
            ins = k.mm(k.bank(bk), k.ones, CV[:, m, 512 * half:512 * half + 512], m == 0, m == 7)
        t = P.did(ins)
        t = A.did(A.on(t, tp).activation(MU[:, 512 * half:512 * half + 512], k.bank(bk), ACT.Copy, scale=1.0 / 1024))
        mis.give(kk, t)
        tmu.append(t)
    tc2 = [V.did(V.on(tmu).tensor_tensor(CV[:, m, :], CV[:, m, :], MU, ALU.subtract)) for m in range(8)]
    tcg, cgb = {}, {}

    def cgate(m):
        w, tw = k.panel(f"w_cg{m // 4}")
        kk, cb, f = cgr.take()
        toks = []

        def evac(half, ps, t):
            toks.append(A.did(A.on(t, f, tp).activation(cb[:, 512 * half:512 * half + 512], ps, ACT.Silu)))
            return [toks[-1]]
        tl = k.proj_T(w, tw, 128 * (m % 4), 128, proj, evac, xr)
        if m % 4 == 3:
            k.done(f"w_cg{m // 4}", tl)
        tcg[m], cgb[m] = toks, (kk, cb)

    cgate(0)
    cgate(1)
    vb = [mis.take() for _ in range(2)]
    for m in range(8):
        sk, sb, sf = sq.take()
        t = A.did(A.on(tc2[m], sf, tp).activation(sb, CV[:, m, :], ACT.Square))
        P.on(t)
        for half in range(2):
            P.on(vb[half][2])
            ins = k.mm(k.bank(vb[half][1]), k.ones, sb[:, 512 * half:512 * half + 512], m == 0, m == 7)
        t = P.did(ins)
        sq.give(sk, t)
    epc = k.tiny[:, 250:251]
    te = G.did(nc.gpsimd.memset(epc, 1e-5))
    tr_ = []
    for half in range(2):
        o = RS[:, 512 * half:512 * half + 512]
        t1 = A.did(A.on(t, te, tp).activation(o, k.bank(vb[half][1]), ACT.Sqrt, bias=epc, scale=1.0 / 1024))
        mis.give(vb[half][0], t1)
        tr_.append(V.did(V.on(t1).reciprocal(o, o)))
    cgate(2)
    cgate(3)
    tcf = {}
    for m in range(8):
        t = V.did(V.on(tr_).tensor_tensor(CV[:, m, :], CV[:, m, :], RS, ALU.mult))
        t = A.did(A.on(t).activation(CV[:, m, :], CV[:, m, :], ACT.Silu, scale=k.sm("clg")[:, m:m + 1], bias=k.sm("clb")[:, m:m + 1]))
        t = V.did(V.on(t, tcg[m]).tensor_tensor(CV[:, m, :], CV[:, m, :], cgb[m][1], ALU.mult))
        cgr.give(cgb[m][0], t)
        tcf[m] = t
        if m < 4:
            cgate(m + 4)

    mk4 = [*k.mark()]
    (g1, t1), (b1, t2), (g2, t3), (b2, t4) = (bcast(i, PH + 64 * KB + 4 * KB * j, mk4) for j, i in enumerate((2, 3, 4, 5)))
    HN = XN
    tx = k.dma().start(S, HN, d["hscr"].rearrange("(b p) n -> p b n", p=128), tsp, mk4)
    tO = {b: [] for b in range(8)}
    for h in range(2):
        (wa, ta), (wb, tb_) = k.panel(f"w_so{h}0"), k.panel(f"w_so{h}1")
        P.on(ts, list(tcf.values()))
        for b in range(8):
            kk, bk, f = proj.take()
            P.on(f)
            k.proj_N(wa, ta, 0, 512, b, k.bank(bk), X=SM, stop=False)
            t = tl = k.proj_N(wb, tb_, 0, 512, b, k.bank(bk), X=CV, start=False)
            o = HN[:, b, 512 * h:512 * h + 512]
            t = V.did(V.on(t, tx).tensor_tensor(o, o, k.bank(bk), ALU.add))
            proj.give(kk, t)
            tO[b].append(t)
        k.done(f"w_so{h}0", tl)
        k.done(f"w_so{h}1", tl)
    G.on(mk4)
    ready = [k.ln_rows(HN[:, b, :], b, HN[:, b, :], tO[b], 1e-5, g1, b1, [t1, t2, mk4]) for b in range(8)]
    tX = k.transpose_to(HN, k.XT, mis, ready)
    xr = list(tX.values())

    PTt = k.at(PH, [2, 1024])
    tpt = k.dma().start(S, PTt, d["pT"].rearrange("p (k t) -> p k t", k=2), tl)
    sgr = Ring([k.at(PH + 8 * KB + 2 * KB * i, [512]) for i in range(3)])
    for i in range(3):
        sgr.free[i] = [tl]
    (wg0, tg0), (wg1, tg1), (wp, twp) = k.panel("w_pg0"), k.panel("w_pg1"), k.panel("w_pp")
    touts = k.dma()
    t_end = None
    for b in range(8):
        last = []
        for h, (w, tw) in enumerate(((wg0, tg0), (wg1, tg1))):
            kk, bk, f = proj.take()
            P.on(f, xr)
            t = k.proj_N(w, tw, 0, 512, b, k.bank(bk))
            sk, sb, sf = sgr.take()
            t = A.did(A.on(t, sf).activation(sb, k.bank(bk), ACT.Sigmoid))
            proj.give(kk, t)
            kk, bk, f = mis.take()
            P.on(f, tpt)
            t2_ = k.proj_N(wp, twp, 512 * h, 512, b, k.bank(bk), X=PTt, nk=2)
            t = V.did(V.on(t, t2_).tensor_tensor(sb, sb, k.bank(bk), ALU.mult))
            mis.give(kk, t)
            o = HN[:, b, 512 * h:512 * h + 512]
            t = V.did(V.on(t, ready).scalar_tensor_tensor(o, o, ALPHA, sb, ALU.mult, ALU.add))
            sgr.give(sk, t)
            last.append(t)
        t = k.ln_rows(HN[:, b, :], b, HN[:, b, :], last, 1e-5, g2, b2, [t3, t4])
        t_end = touts.start(S, out_d[128 * b:128 * b + 128, :], HN[:, b, :], t)
    S.on(t_end)


def dump(k, out, ready):
    t = k.mark()
    o = k.dma().start(k.S, out.rearrange("(b p) n -> p b n", p=128), k.H, t)
    k.S.on(o)


def host(inp):
    a = {n: np.asarray(v) for n, v in inp.items()}
    out = {}

    def pan(name, w):
        kk, n = w.shape
        out[name] = np.ascontiguousarray(w.reshape(kk // 128, 128, n).transpose(1, 0, 2).reshape(128, -1))

    w = a["ev_w_in"][0]
    perm = np.concatenate([np.r_[64 * m:64 * m + 64, 64 * (m + 4):64 * (m + 4) + 64] for m in range(4)])
    q, kv, ga, u, gb = w[:, 0:512], w[:, 512:768], w[:, 768:1280], w[:, 1280:1792], w[:, 1792:2304]
    pan("w_u", u)
    pan("w_q", q[:, perm])
    pan("w_kv", kv)
    pan("w_ga", ga[:, perm])
    pan("w_gb", gb)
    pan("w_glu", a["ev_glu_w"][0])
    wo = a["ev_w_out"][0]
    wo = np.concatenate([wo[0:512][perm], wo[512:]], 0)
    pan("w_eo0", wo[:, 0:512])
    pan("w_eo1", wo[:, 512:])
    w = a["od_w_in"][0]
    q, ok, ov, g, qi, ki, wi = np.split(w, np.cumsum([1024, 256, 256, 1024, 512, 64]), axis=1)
    pan("w_qi", qi)
    pan("w_ki", np.concatenate([ki, ki, wi], 1))
    pan("w_okv", np.concatenate([ok, ov], 1))
    wo = a["od_w_out"][0]
    for h in range(2):
        hs = slice(512 * h, 512 * h + 512)
        pan(f"w_og{h}", g[:, hs])
        pan(f"w_oq{h}", q[:, hs])
        pan(f"w_oo{h}", wo[:, hs])
    w = a["w_in_2"][0]
    xs, z, bm, cm, dt, ga_, gb_, cg = np.split(w, np.cumsum([1024, 1024, 256, 256, 16, 1024, 1024]), axis=1)
    for p in range(4):
        pan(f"w_cf{p}", np.concatenate([x[:, 128 * m:128 * m + 128] for m in (2 * p, 2 * p + 1) for x in (ga_, gb_)], 1))
    pan("w_bc", np.concatenate([bm, cm], 1))
    pan("w_dt", dt)
    wo = a["w_out_2"][0]
    for h in range(2):
        hs = slice(512 * h, 512 * h + 512)
        pan(f"w_xs{h}", xs[:, hs])
        pan(f"w_z{h}", z[:, hs])
        pan(f"w_cg{h}", cg[:, hs])
        pan(f"w_so{h}0", wo[0:1024, hs])
        pan(f"w_so{h}1", wo[1024:, hs])
        pan(f"w_pg{h}", a["w_ple_gate_2"][0][:, hs])
    pan("w_pp", a["w_ple_proj_2"][0])

    def col(v):
        return v.reshape(-1, 128).T

    sm = {}
    sm["g_ev"], sm["g_od"] = col(a["norm_g"][0]), col(a["norm_g"][1])
    sm["qg_ev"] = np.tile(a["ev_q_norm_g"][0], 2)[:, None]
    sm["kg_ev"] = np.tile(a["ev_k_norm_g"][0], 2)[:, None]
    sm["sink"] = np.tile(a["ev_sinks"][0][None], (128, 1))
    sm["ldt"] = np.tile(a["ev_ssm_log_dt"][0][None], (128, 1))
    sm["are"] = np.tile(a["ev_ssm_a_re"][0].T, (2, 1))
    sm["aim"] = np.tile(a["ev_ssm_a_im"][0].T, (2, 1))
    sm["dsk"] = np.tile(a["ev_ssm_d"][0].T, (8, 1))
    sm["glub"] = col(a["ev_glu_b"][0])
    sm["qg_od"], sm["kg_od"] = a["od_q_norm_g"][0][:, None], a["od_k_norm_g"][0][:, None]
    cw, cb = a["ssm_conv_w_2"][0], a["ssm_conv_b_2"][0]
    sm["cxw"] = cw.T.reshape(12, 128, 4).transpose(1, 0, 2).reshape(128, 48)
    sm["cxb"] = col(cb)
    sm["dtb"] = np.tile(a["dt_bias_2"][0][None], (128, 1))
    sm["alog"] = np.tile(a["a_log_2"][0][None], (128, 1))
    sm["dk2"] = np.tile(a["d_skip_2"][0][None], (128, 1))
    sm["sng"] = col(a["ssm_norm_g_2"][0])
    sm["bglu"] = col(a["b_glu_2"][0])
    sm["cfw"] = a["conf_conv_w_2"][0].T.reshape(8, 128, 31).transpose(1, 0, 2).reshape(128, 248)
    sm["cfb"], sm["clg"], sm["clb"] = col(a["conf_conv_b_2"][0]), col(a["conf_ln_g_2"][0]), col(a["conf_ln_b_2"][0])
    out["small"] = np.ascontiguousarray(np.concatenate([sm[n] for n in SMALL], 1))
    br, bi = (a[f"ev_ssm_b_{x}"][0].transpose(1, 0, 2).reshape(64, 512) for x in ("re", "im"))
    cr, ci = (a[f"ev_ssm_c_{x}"][0].transpose(2, 0, 1).reshape(64, 512) for x in ("re", "im"))
    out["ssmw"] = np.ascontiguousarray(np.tile(np.concatenate([br, bi, cr, ci], 1), (2, 1)))
    out["x"] = np.ascontiguousarray(a["x"][0])
    out["pT"] = np.ascontiguousarray(a["p_2"][0, 0].T.reshape(2, 128, 1024).transpose(1, 0, 2).reshape(128, 2048))
    out["rb"] = np.ascontiguousarray(a["rel_bias"])
    out["lnp"] = np.ascontiguousarray(np.stack([a["ln_emb_g_2"], a["ln_emb_b_2"], a["ln1_g_2"][0], a["ln1_b_2"][0],
                                                a["ln2_g_2"][0], a["ln2_b_2"][0], a["b_out_2"][0]]))
    out["ohA"], out["ohB"] = onehots()
    return out


def bucket(n):
    if n < 16:
        return n
    b = 16
    while b < 31 and n ** 8 >= 2 ** (4 * 8 + 3 * (b - 15)):
        b += 1
    return b


def onehots():
    A_ = np.zeros((33, STRIP_A), np.float32)
    B_ = np.zeros((33, STRIP_B), np.float32)
    for x in range(STRIP_A):
        dist = 255 - x
        A_[bucket(dist) if 0 <= dist < 128 else 32, x] = 1
    for x in range(STRIP_B):
        dist = 1023 - x
        B_[bucket(dist) if dist >= 0 else 32, x] = 1
    return A_, B_


SHAPES = {"x": (1024, 1024), "ssmw": (128, 2048), "small": (128, SM_COLS), "rb": (32, 8), "ohA": (33, STRIP_A),
          "ohB": (33, STRIP_B), "pT": (128, 2048), "lnp": (7, 1024)}
for _n, _k, _c in PANELS:
    SHAPES[_n] = (128, _k * _c)
SCRATCH = {"strip": (8, STRIP_A + STRIP_B), "uscr": (512, 8, 128), "yscr": (512, 8, 128), "hscr": (1024, 1024)}


def drams(nc, names):
    d = {n: nc.dram_tensor(f"in_{n}", SHAPES[n], F32, kind="ExternalInput").ap() for n in names}
    for n, s in SCRATCH.items():
        d[n] = nc.dram_tensor(f"scr_{n}", s, F32, kind="Internal").ap()
    return d


def build(nc, d, out):
    k = K(nc, d, EVEN_P + ODD_P + SEC_P)
    k.setup()
    tH = even(k)
    tH = odd(k, tH)
    second(k, tH, out)


def kernel(**inputs):
    import concourse.bacc as _bacc
    from concourse.bass_utils import run_bass_kernel_spmd as _run

    arrays = {f"in_{n}": v for n, v in host(inputs).items()}
    nc = _bacc.Bacc("TRN2", target_bir_lowering=False, num_devices=1)
    d = drams(nc, list(SHAPES))
    out = nc.dram_tensor("out_0_dram", (1024, 1024), F32, kind="ExternalOutput").ap()
    build(nc, d, out)
    r = _run(nc, [arrays], core_ids=[0])
    return np.asarray(r.results[0]["out_0_dram"]).reshape(1, 1024, 1024)
```

```python
import math

import numpy as np

import concourse.bass as bass
from concourse import mybir

F32 = mybir.dt.float32
BF16 = mybir.dt.bfloat16
F32R = mybir.dt.float32r
I32 = mybir.dt.int32
ALU = mybir.AluOpType
ACT = mybir.ActivationFunctionType
AX = mybir.AxisListType

T = 1024
NB = 8
KB = 1024
NEG = -1e30
PI = math.pi
ALPHA = 2.0 ** 0.25


class Eng:

    def __init__(self, eng, sem, every):
        self.e, self.sem, self.n, self.seen = eng, sem, 0, {}
        every.append(self)

    def on(self, *toks):
        for t in toks:
            if t is None:
                continue
            if isinstance(t, list):
                self.on(*t)
                continue
            s, v = t
            if self.seen.get(s.name, 0) < v:
                self.e.wait_ge(s, v)
                self.seen[s.name] = v
        return self.e

    def did(self, ins):
        ins.then_inc(self.sem, 1)
        self.n += 1
        return (self.sem, self.n)

    def now(self):
        return (self.sem, self.n) if self.n else None


class Ring:

    def __init__(self, items):
        self.items, self.free, self.k = items, [[] for _ in items], -1

    def take(self):
        self.k = (self.k + 1) % len(self.items)
        f = self.free[self.k]
        assert f is not None, "buffer still out"
        self.free[self.k] = None
        return self.k, self.items[self.k], f

    def give(self, k, *toks):
        self.free[k] = list(toks)


class Dma:

    def __init__(self, sem):
        self.sem, self.n = sem, 0

    def start(self, eng, out, in_, *after):
        eng.on(*after).dma_start(out, in_).then_inc(self.sem, 16)
        self.n += 16
        return (self.sem, self.n)


def bc(ap, axis, n):
    u = ap.unsqueeze(axis)
    shape = list(u.shape)
    shape[axis] = n
    return u.to_broadcast(shape)


def _chunks():
    t = lambda p, n: [(f"{p}{i}", 8, 128) for i in range(n)]
    wide = lambda p, kc: [(f"{p}{h}{i}", 2, 512) for h in range(2) for i in range(kc)]
    ev = t("u", 4) + t("q", 4) + [("kk", 8, 128), ("vv", 8, 128)] + t("ga", 4) + t("gb", 4)
    ev += [(f"glu{i}", 4, 256) for i in range(4)] + wide("eo", 4)
    od = t("qi", 4) + [("ki", 8, 128), ("wi", 8, 8)] + t("ok", 2) + t("oq", 8) + t("ov", 2) + t("og", 8) + wide("oo", 4)
    se, x = [], iter([("xb%d" % i, 8, 128) for i in XORDER])
    for m in range(8):
        se += [(f"cb{m}", 8, 128), (f"ca{m}", 8, 128)]
        se += [next(x) for _ in range(2 - m % 2)]
    se += [("dt", 8, 16)] + wide("z", 4) + t("cg", 8) + wide("so", 8)
    se += [("pp0", 2, 512), ("pp1", 2, 512)] + wide("pg", 4)
    return ev, od, se


XORDER = [8, 9, 10, 11, 0, 1, 2, 3, 4, 5, 6, 7]
EVEN_P, ODD_P, SEC_P = _chunks()
PANELS = EVEN_P + ODD_P + SEC_P
CH_OFF = {}
_o = 0
for _n, _k, _c in PANELS:
    CH_OFF[_n] = (_o, _k, _c)
    _o += _k * _c
CH_COLS = _o

SMALL = {
    "g_ev": 8, "g_od": 8, "qg_ev": 1, "kg_ev": 1, "sink": 8, "ldt": 32, "are": 32, "aim": 32,
    "dsk": 32, "glub": 8, "qg_od": 1, "kg_od": 1,
    "cxw": 48, "cxb": 12, "dtb": 16, "alog": 16, "sng": 8, "bglu": 16, "cfw": 248, "cfb": 8,
    "clg": 8, "clb": 8, "dk2": 16,
}
SM_OFF = {}
_o = 0
for _n, _c in SMALL.items():
    SM_OFF[_n] = _o
    _o += _c
SM_COLS = _o
STRIP_A = 383
STRIP_B = 1151


class K:

    def __init__(self, nc, d, panels):
        self.nc, self.d = nc, d
        ev = self.every = []
        self.V = Eng(nc.vector, nc.alloc_semaphore("s_dve"), ev)
        self.A = Eng(nc.scalar, nc.alloc_semaphore("s_act"), ev)
        self.P = Eng(nc.tensor, nc.alloc_semaphore("s_pe"), ev)
        self.G = Eng(nc.gpsimd, nc.alloc_semaphore("s_pool"), ev)
        self.S = Eng(nc.sync, nc.alloc_semaphore("s_sp"), ev)
        self.base = (nc.sbuf_base + 63) // 64 * 64
        self.end = nc.sbuf_usable_end
        self.nname = 0
        self.psum = nc.alloc_psum_tensor("psum", [128, 8, 512], F32)
        self.dsems = 0
        self.X0, self.R0, self.C0 = 0, 64 * KB, 104 * KB
        self.XH, self.XL = self.at(self.X0, [8, 1024], F32R), self.at(self.X0 + 32 * KB, [8, 1024], F32R)
        o = self.C0
        self.ident = self.at(o, [128]); o += 512
        self.ones = self.at(o, [128]); o += 512
        self.tle = self.at(o, [128]); o += 512
        self.tgt = self.at(o, [128]); o += 512
        self.bones = self.at(o, [128]); o += 512
        self.flip = self.at(o, [128]); o += 512
        self.mhalf = self.at(o, [16]); o += 64
        self.epsc = self.at(o, [16]); o += 64
        self.tiny = self.at(o, [256]); o += 1024
        self.small = self.at(o, [SM_COLS]); o += (SM_COLS * 4 + 63) // 64 * 64
        self.H0 = o
        self.H = self.at(self.H0, [8, 1024])
        self.PH0 = o + 32 * KB
        self.raw = [self.at(self.R0 + 4 * KB * i, [1024]) for i in range(2)]
        self.hi = [self.at(self.R0 + (8 + 8 * i) * KB, [1024], F32R) for i in range(4)]
        self.lo = [self.at(self.R0 + (12 + 8 * i) * KB, [1024], F32R) for i in range(4)]
        self.raw_dma = [self.dma() for _ in range(2)]
        self.queue = [c[0] for c in panels]
        self.nload = self.nsplit = 0
        self.late = []
        self.raw_tok, self.raw_free = [None, None], [None, None]
        self.slots = [[] for _ in range(4)]
        self.loaded = {}
        for _ in range(2):
            self.load()
        for i in range(4):
            self.split(i)

    def at(self, off, shape, dt=F32):
        self.nname += 1
        size = 4 if dt == F32 else 2
        for s in shape:
            size *= s
        assert self.base + off + size <= self.end, (off, size, self.end - self.base)
        h = self.nc.alloc_sbuf_tensor_at(f"m{self.nname}", [128] + list(shape), dt, offset=self.base + off)
        return h[tuple(slice(None) for _ in range(len(shape) + 1))]

    def dma(self):
        self.dsems += 1
        return Dma(self.nc.alloc_semaphore(f"d{self.dsems}"))

    def bank(self, i, n=1):
        return self.psum[:, i, :] if n == 1 else self.psum[:, i:i + n, :].rearrange("p a b -> p (a b)")

    def sm(self, name, a=0, b=None):
        o = SM_OFF[name]
        return self.small[:, o + a:o + (SMALL[name] if b is None else b)]

    def load(self):
        if self.nload == len(self.queue):
            return
        o, kk, n = CH_OFF[self.queue[self.nload]]
        i = self.nload % 2
        src = self.d["w"][128 * o:128 * (o + kk * n)].rearrange("(p c) -> p c", p=128)
        self.raw_tok[i] = self.raw_dma[i].start(self.S, self.raw[i][:, 0:kk * n], src, self.raw_free[i])
        self.nload += 1

    def split(self, slot):
        if self.nsplit == len(self.queue):
            return
        name = self.queue[self.nsplit]
        _, kk, n = CH_OFF[name]
        i = self.nsplit % 2
        raw, hi, lo = self.raw[i][:, 0:kk * n], self.hi[slot][:, 0:kk * n], self.lo[slot][:, 0:kk * n]
        t1 = self.A.did(self.A.on(self.raw_tok[i], self.slots[slot]).activation(hi, raw, ACT.Copy))
        t2 = self.G.did(self.G.on(t1, self.raw_tok[i], self.slots[slot]).tensor_tensor(lo, raw, hi.bitcast(F32), ALU.subtract))
        self.raw_free[i] = [t1, t2]
        v = lambda x: x.rearrange("p (k n) -> p k n", k=kk)
        self.loaded[name] = (slot, v(hi), v(lo), [t1, t2])
        self.nsplit += 1
        self.load()

    def chunk(self, name):
        return self.loaded[name][1:]

    def done(self, name, tok):
        slot = self.loaded.pop(name)[0]
        self.slots[slot] = tok
        self.split(slot)

    def mark(self):
        return [e.now() for e in self.every]

    def mm(self, out, lhsT, rhs, start, stop):
        return self.nc.tensor.matmul(out, lhsT, rhs, start=start, stop=stop, skip_group_check=True)

    def tr(self, out, in_):
        return self.nc.tensor.transpose(out, in_, self.ident[:, :])

    def setup(self):
        nc, G = self.nc, self.G
        self.t_small = self.dma().start(self.S, self.small[:, :], self.d["small"])
        a = [G.did(nc.gpsimd.memset(self.ident[:, :], 0.0)), G.did(nc.gpsimd.memset(self.ones[:, :], 1.0)),
             G.did(nc.gpsimd.memset(self.bones[:, :], 0.0)), G.did(nc.gpsimd.memset(self.mhalf[:, :], -0.5))]
        a.append(G.did(nc.gpsimd.memset(self.epsc[:, :], 1e-6)))
        G.on(*a)
        b = [G.did(nc.gpsimd.memset(self.bones[0:64, 0:64], 1.0)),
             G.did(nc.gpsimd.memset(self.bones[64:128, 64:128], 1.0))]
        aff = nc.gpsimd.affine_select
        G.on(*b)
        b.append(G.did(aff(out=self.ident[:, :], in_=self.ident[:, :], compare_op=ALU.not_equal, fill=1.0, base=0,
                           pattern=[[-1, 128]], channel_multiplier=1)))
        a2 = G.did(nc.gpsimd.memset(self.flip[:, :], 0.0))
        b.append(G.did(G.on(a2).affine_select(out=self.flip[:, :], in_=self.flip[:, :], compare_op=ALU.not_equal, fill=1.0,
                                              base=-127, pattern=[[1, 128]], channel_multiplier=1)))
        b.append(G.did(aff(out=self.tle[:, :], in_=self.ones[:, :], compare_op=ALU.is_ge, fill=0.0, base=0,
                           pattern=[[1, 128]], channel_multiplier=-1)))
        b.append(G.did(aff(out=self.tgt[:, :], in_=self.ones[:, :], compare_op=ALU.is_gt, fill=0.0, base=0,
                           pattern=[[-1, 128]], channel_multiplier=1)))
        self.t_const = b

    def transpose_to(self, src, banks, ready, dst=None, scale=None, after=None):
        hi, lo = dst or (self.XH, self.XL)
        out = []
        for half in range(2):
            for dt in range(8):
                k, bk, f = banks.take()
                self.P.on(f, self.t_const)
                for j in range(4):
                    b = 4 * half + j
                    self.P.on(ready[b])
                    ins = self.tr(self.bank(bk)[:, 128 * j:128 * j + 128], src[:, b, 128 * dt:128 * dt + 128])
                t = self.P.did(ins)
                h = hi[:, dt, 512 * half:512 * half + 512]
                l = lo[:, dt, 512 * half:512 * half + 512]
                sc = 1.0 if scale is None else scale[:, dt:dt + 1]
                t2 = self.A.did(self.A.on(t, self.t_small, after).activation(h, self.bank(bk), ACT.Copy, scale=sc))
                t3 = self.V.did(self.V.on(t2, self.t_small, after).scalar_tensor_tensor(l, self.bank(bk), sc, h.bitcast(F32), ALU.mult, ALU.subtract))
                banks.give(k, t2, t3)
                out += [t2, t3]
        return out

    def flush(self):
        todo, self.late = self.late, []
        for f in todo:
            f()

    def parts(self, src, hi, lo, tok, free=None, eng=None):
        t1 = self.A.did(self.A.on(tok, free).activation(hi, src, ACT.Copy))
        e = eng or self.G
        t2 = e.did(e.on(t1, tok, free).tensor_tensor(lo, src, hi.bitcast(F32), ALU.subtract))
        return [t1, t2]

    def rms_rows(self, src, b, dst, ready, eps, junk, n=1024):
        c = self.tiny[:, 8 * b:8 * b + 1]
        e = self.tiny[:, 8 * b + 1:8 * b + 2]
        t = self.A.did(self.A.on(ready, self.wjunk).activation(junk, src, ACT.Square, accum_out=c))
        self.wjunk = t
        t = self.G.did(self.G.on(t, self.t_const).tensor_scalar(e, c, 1.0 / n, eps, ALU.mult, ALU.add))
        t = self.G.did(self.G.on(t).tensor_tensor(c, e, self.mhalf[:, 0:1], ALU.pow))
        return self.V.did(self.V.on(t, ready).tensor_scalar(dst, src, c, None, ALU.mult))

    def ln_rows(self, src, b, dst, ready, eps, gbc, bbc, tgb):
        V, G = self.V, self.G
        o = 24 * b
        st, mv, rs = self.tiny[:, o:o + 12], self.tiny[:, o + 12:o + 14], self.tiny[:, o + 14:o + 16]
        V.on(ready)
        ts = [V.did(V.e.bn_stats(st[:, 6 * i:6 * i + 6], src[:, 512 * i:512 * i + 512])) for i in range(2)]
        t = V.did(V.on(*ts).bn_aggr(mv, st))
        t1 = G.did(G.on(t, self.t_const).tensor_scalar(rs[:, 0:1], mv[:, 1:2], 1.0, eps, ALU.mult, ALU.add))
        t1 = G.did(G.on(t1).tensor_tensor(rs[:, 1:2], rs[:, 0:1], self.mhalf[:, 0:1], ALU.pow))
        t1 = G.did(G.on(t1).tensor_scalar(rs[:, 0:1], mv[:, 0:1], rs[:, 1:2], -1.0, ALU.mult, ALU.mult))
        t = self.A.did(self.A.on(t1, ready).activation(dst, src, ACT.Identity, bias=rs[:, 0:1], scale=rs[:, 1:2]))
        t = G.did(G.on(t, tgb).tensor_tensor(dst, dst, gbc, ALU.mult))
        return V.did(V.on(t, tgb).tensor_tensor(dst, dst, bbc, ALU.add))

    def mm3(self, out, w, x, first, last):
        (wh, wl), (xh, xl) = w, x
        self.mm(out, wh, xh, first, False)
        self.mm(out, wh, xl, False, False)
        return self.mm(out, wl, xh, False, last)

    def proj_T(self, name, m, banks, evac, xr=None, col=0, X=None, keep=False):
        xh, xl = X or (self.XH, self.XL)
        wh, wl, tw = self.chunk(name)
        nk = wh.shape[1]
        for half in range(2):
            k, bk, f = banks.take()
            self.P.on(f, tw, xr)
            hs = slice(512 * half, 512 * half + 512)
            for kk in range(nk):
                ins = self.mm3(self.bank(bk)[0:m, :], (wh[:, kk, col:col + m], wl[:, kk, col:col + m]),
                               (xh[:, kk, hs], xl[:, kk, hs]), kk == 0, kk == nk - 1)
            last = self.P.did(ins)
            self.flush()
            t = evac(half, self.bank(bk), last)
            if callable(t):
                self.late.append(lambda k=k, t=t: banks.give(k, *t()))
            else:
                banks.give(k, *t)
        if not keep:
            self.done(name, last)
        return last

    def rows(self, name, b, out, start=True, stop=True, X=None, k0=0):
        xh, xl = X or (self.XH, self.XL)
        wh, wl, tw = self.chunk(name)
        self.P.on(tw)
        nk = wh.shape[1]
        bs = slice(128 * b, 128 * b + 128)
        for kk in range(nk):
            ins = self.mm3(out, (xh[:, k0 + kk, bs], xl[:, k0 + kk, bs]), (wh[:, kk, :], wl[:, kk, :]),
                           start and kk == 0, stop and kk == nk - 1)
        return ins

    def wide(self, name, pieces, evac, free, final=False, mid=None):
        n0 = len(pieces) - 4
        last = None
        for i in range(n0):
            for b in range(8):
                self.P.on(free[b])
                last = self.rows(name + pieces[i][0], b, self.bank(b), i == 0, False, pieces[i][1], pieces[i][2])
            last = self.P.did(last)
            self.done(name + pieces[i][0], last)
        self.P.on(mid)
        for grp in range(2):
            bs = range(4 * grp, 4 * grp + 4)
            if grp and final:
                for b in bs:
                    if not n0:
                        self.P.on(free[b])
                    for i in range(n0, n0 + 4):
                        ins = self.rows(name + pieces[i][0], b, self.bank(b), i == 0, i == n0 + 3, pieces[i][1], pieces[i][2])
                    t = self.P.did(ins)
                    free[b] = evac(b, self.bank(b), t)
                for i in range(n0, n0 + 4):
                    self.done(name + pieces[i][0], t)
                return
            for i in range(n0, n0 + 4):
                for b in bs:
                    if i == 0:
                        self.P.on(free[b])
                    ins = self.rows(name + pieces[i][0], b, self.bank(b), i == 0, i == n0 + 3, pieces[i][1], pieces[i][2])
                    if i == n0 + 3:
                        t = self.P.did(ins)
                        free[b] = evac(b, self.bank(b), t)
                if grp:
                    self.done(name + pieces[i][0], t if i == n0 + 3 else self.P.did(ins))

    def qk_norm(self, psb, t, dst, gain, lhs_ones, banks, sq, rt, inv, tsm, keep):
        sk, sqb, sf = sq.take()
        t1 = self.A.did(self.A.on(t, sf).activation(sqb, psb, ACT.Square))

        def rest():
            k, bk, f = banks.take()
            t2 = self.P.did(self.P.on(t1, f, self.t_const).matmul(self.bank(bk), lhs_ones, sqb, start=True, stop=True))
            sq.give(sk, t2)
            rk, rb, rf = rt.take()
            t3 = self.A.did(self.A.on(t2, rf).activation(rb, self.bank(bk), ACT.Sqrt, bias=self.epsc[:, 0:1], scale=inv))
            banks.give(k, t3)
            t4 = self.V.did(self.V.on(t3).reciprocal(rb, rb))
            t5 = self.V.did(self.V.on(t4, t, tsm).scalar_tensor_tensor(dst, psb, gain, rb, ALU.mult, ALU.mult))
            rt.give(rk, t5)
            keep(t5)
            return [t5]
        return rest


def even(k, last_out=None):
    nc, d, V, A, P, G, S = k.nc, k.d, k.V, k.A, k.P, k.G, k.S
    PH = k.PH0
    QT, KT, VN = k.at(PH, [4, 1024]), k.at(PH + 16 * KB, [1024]), k.at(PH + 20 * KB, [8, 128])
    O = PH + 24 * KB
    BIA = k.at(PH + 40 * KB, [8, 256])
    sq = Ring([k.at(PH + 48 * KB, [512])])
    rt = Ring([k.at(PH + 50 * KB, [512])])
    Z, Y = (k.at(PH + (52 + 2 * i) * KB, [4, 128]) for i in range(2))
    gev = Ring([k.at(PH + (56 + 4 * i) * KB, [1024]) for i in range(2)])
    proj = Ring([0, 1, 2])
    mis = Ring([3, 4, 5, 6, 7])

    tx = []
    for q in range(4):
        tx.append(k.dma().start(S, k.H[:, 2 * q:2 * q + 2, :],
                                d["x"][256 * q:256 * q + 256, :].rearrange("(b p) n -> p b n", p=128)))
    k.wjunk = None
    junk = k.at(PH + 16 * KB, [1024])
    ready = [k.rms_rows(k.H[:, b, :], b, k.H[:, b, :], tx[b // 2], 1e-6, junk) for b in range(8)]
    xr = k.transpose_to(k.H, mis, ready, scale=k.sm("g_ev"))

    BB, BX, CC, CX = (k.at(O + 2 * KB * i, [32, 16]) for i in range(4))
    PR, PIm = k.at(O + 8 * KB, [32, 9]), k.at(O + 9 * KB + 256, [32, 9])
    sm = k.at(O + 10 * KB + 512, [12, 32])
    raw = k.at(PH + 56 * KB, [4, 32, 16])
    sc = k.at(PH + 48 * KB, [6, 32, 9])
    tr = k.dma().start(S, raw, d["ssmw"].rearrange("p (a g h) -> p a g h", a=4, g=32))
    KS = k.at(O + 12 * KB + 512, [128])
    tks = G.did(nc.gpsimd.iota(KS, pattern=[[1, 128]], base=1, channel_multiplier=0, allow_small_or_imprecise_dtypes=True))
    J9 = k.at(O + 13 * KB, [9])
    tj9 = G.did(nc.gpsimd.iota(J9, pattern=[[1, 9]], base=0, channel_multiplier=0, allow_small_or_imprecise_dtypes=True))
    DT, AT, TH, DEN, NR, NI, FR, FI, U1, U2, R8, TH8 = (sm[:, i, :] for i in range(12))
    tsm = k.t_small
    t = A.did(A.on(tsm).activation(DT, k.sm("ldt"), ACT.Exp))
    t1 = V.did(V.on(t, tsm).tensor_tensor(AT, k.sm("are"), DT, ALU.mult))
    t2 = V.did(V.e.tensor_tensor(TH, k.sm("aim"), DT, ALU.mult))
    aj, tj, em, mg, cs, sn = (sc[:, i, :, :] for i in range(6))
    t1 = V.did(V.on(t1, tj9).tensor_tensor(aj, bc(AT, 2, 9), bc(J9, 1, 32), ALU.mult))
    t2 = V.did(V.on(t2).tensor_tensor(tj, bc(TH, 2, 9), bc(J9, 1, 32), ALU.mult))
    ta = A.did(A.on(t1).activation(em, aj, ACT.Exp))
    tb = A.did(A.on(t1).activation(mg, aj, ACT.Tanh, scale=0.5))
    t = V.did(V.on(ta, tb).scalar_tensor_tensor(em, em, 1.0, mg, ALU.add, ALU.mult))
    tmg = V.did(V.on(t).tensor_scalar(mg, em, 1.0, None, ALU.add))

    def reduce_angle(eng, ang, n, tok):
        e = eng.e
        t = eng.did(eng.on(tok).tensor_scalar(n, ang, 1.0 / (2 * PI), 12582912.0, ALU.mult, ALU.add))
        t = eng.did(eng.on(t).tensor_scalar(n, n, 12582912.0, None, ALU.subtract))
        t = eng.did(eng.on(t).scalar_tensor_tensor(ang, n, -6.28125, ang, ALU.mult, ALU.add))
        t = eng.did(eng.on(t).scalar_tensor_tensor(ang, n, -(2 * PI - 6.28125), ang, ALU.mult, ALU.add))
        return eng.did(eng.on(t).tensor_scalar(ang, ang, 3.1415925, -3.1415925, ALU.min, ALU.max))

    def quarter(eng, out, ang, n, tok):
        t = eng.did(eng.on(tok).tensor_scalar(n, ang, PI / 2, -2 * PI, ALU.is_gt, ALU.mult))
        t = eng.did(eng.on(t).scalar_tensor_tensor(out, ang, PI / 2, n, ALU.add, ALU.add))
        return eng.did(eng.on(t).tensor_scalar(out, out, 3.1415925, -3.1415925, ALU.min, ALU.max))

    t = reduce_angle(V, tj, sn, t2)
    tq = quarter(V, cs, tj, sn, t)
    ts_ = A.did(A.on(tq).activation(sn, tj, ACT.Sin))
    tc_ = A.did(A.on(tq).activation(cs, cs, ACT.Sin))
    t = V.did(V.on(tc_, tmg).tensor_tensor(PR, mg, cs, ALU.mult))
    t1 = V.did(V.on(ts_).tensor_tensor(PIm, mg, sn, ALU.mult))
    tR8 = V.did(V.on(tmg).tensor_copy(R8, mg[:, :, 8]))
    tT8 = V.did(V.e.tensor_scalar(TH8, TH, 8.0, None, ALU.mult))
    tpow = [t, t1]
    hs = U1
    th_ = A.did(A.on(t1).activation(hs, tj[:, :, 1], ACT.Sin, scale=0.5))
    t = V.did(V.on(th_).tensor_tensor(hs, hs, hs, ALU.mult))
    t1 = V.did(V.e.tensor_tensor(NR, em[:, :, 1], cs[:, :, 1], ALU.mult))
    t = V.did(V.on(t, t1).scalar_tensor_tensor(NR, hs, -2.0, NR, ALU.mult, ALU.add))
    ar, ai = k.sm("are"), k.sm("aim")
    ni = PIm[:, :, 1]
    t1 = V.did(V.e.tensor_tensor(DEN, ar, ar, ALU.mult))
    t2 = V.did(V.e.tensor_tensor(U2, ai, ai, ALU.mult))
    t1 = V.did(V.on(t1, t2).tensor_tensor(DEN, DEN, U2, ALU.add))
    t1 = V.did(V.on(t1).reciprocal(DEN, DEN))
    ta = V.did(V.on(t).tensor_tensor(FR, NR, ar, ALU.mult))
    tb = V.did(V.on(*tpow).tensor_tensor(U1, ni, ai, ALU.mult))
    ta = V.did(V.on(ta, tb).tensor_tensor(FR, FR, U1, ALU.add))
    tb = V.did(V.e.tensor_tensor(FI, ni, ar, ALU.mult))
    tc = V.did(V.on(t2).tensor_tensor(U2, NR, ai, ALU.mult))
    tb = V.did(V.on(tb, tc).tensor_tensor(FI, FI, U2, ALU.subtract))
    ta = V.did(V.on(ta, t1).tensor_tensor(FR, FR, DEN, ALU.mult))
    tb = V.did(V.on(tb).tensor_tensor(FI, FI, DEN, ALU.mult))
    lo, hi = slice(0, 64), slice(64, 128)
    V.on(ta, tb, tr)
    q = []
    for h, f1, f2, op in ((lo, FR, FI, ALU.subtract), (hi, FI, FR, ALU.add)):
        a1 = V.did(V.e.tensor_tensor(BB[h], bc(f1[h], 2, 16), raw[h, 0], ALU.mult))
        a2 = V.did(V.e.tensor_tensor(BX[h], bc(f2[h], 2, 16), raw[h, 1], ALU.mult))
        q.append(V.did(V.on(a1, a2).tensor_tensor(BB[h], BB[h], BX[h], op)))
    for h, f1, f2, op in ((lo, FI, FR, ALU.add), (hi, FR, FI, ALU.subtract)):
        a1 = V.did(V.on(*q).tensor_tensor(BX[h], bc(f1[h], 2, 16), raw[h, 0], ALU.mult))
        a2 = V.did(V.e.tensor_tensor(CX[h], bc(f2[h], 2, 16), raw[h, 1], ALU.mult))
        a1 = V.did(V.on(a1, a2).tensor_tensor(BX[h], BX[h], CX[h], op))
        if h is lo:
            a1 = V.did(V.on(a1).tensor_scalar(BX[h], BX[h], -1.0, None, ALU.mult))
        q.append(a1)
    V.on(*q)
    q.append(V.did(V.e.tensor_copy(CC[lo], raw[lo, 2])))
    q.append(V.did(V.e.tensor_scalar(CC[hi], raw[hi, 3], -1.0, None, ALU.mult)))
    q.append(V.did(V.e.tensor_scalar(CX[lo], raw[lo, 3], -1.0, None, ALU.mult)))
    q.append(V.did(V.e.tensor_scalar(CX[hi], raw[hi, 2], -1.0, None, ALU.mult)))
    QR, QI = k.at(O + 13 * KB + 64, [32, 8]), k.at(O + 14 * KB + 64, [32, 8])
    V.on(*tpow)
    for j in range(8):
        q.append(V.did(V.e.tensor_copy(QR[:, :, j], PR[:, :, 7 - j])))
        q.append(V.did(V.e.tensor_copy(QI[:, :, j], PIm[:, :, 7 - j])))
    tset = q + tpow + [tR8, tT8]

    ohA, ohB = k.at(PH, [STRIP_A]), k.at(PH + 2 * KB, [STRIP_B])
    rbt, rows = k.at(PH + 7 * KB, [8]), k.at(PH + 8 * KB, [STRIP_A + STRIP_B])
    dm = k.dma()
    dm.start(S, ohA[0:33], d["ohA"])
    dm.start(S, ohB[0:33], d["ohB"])
    toh = dm.start(S, rbt[0:32], d["rb"])
    tneg = G.did(G.on(G.now()).memset(rbt[32:33], NEG))
    trow = []
    for src, o, n in ((ohA, 0, STRIP_A), (ohB, STRIP_A, 512), (ohB, STRIP_A + 512, 512), (ohB, STRIP_A + 1024, STRIP_B - 1024)):
        kk, bk, f = mis.take()
        so = 0 if src is ohA else o - STRIP_A
        t = P.did(P.on(f, toh, tneg).matmul(k.bank(bk)[0:8, 0:n], rbt[0:33], src[0:33, so:so + n], start=True, stop=True))
        t = A.did(A.on(t).activation(rows[0:8, o:o + n], k.bank(bk)[0:8, 0:n], ACT.Copy))
        mis.give(kk, t)
        trow.append(t)
    tdr = k.dma().start(S, d["strip"][:, :], rows[0:8], trow)
    k.t_strip = tdr
    rawb = k.at(PH, [8, 256])
    traw = k.dma().start(S, rawb, bass.AP(d["strip"].tensor, 0, [[1, 128], [STRIP_A + STRIP_B, 8], [1, 256]]), tdr, trow)
    tbia = []
    for i in range(4):
        kk, bk, f = mis.take()
        t = P.did(P.on(f, traw, k.t_const).matmul(k.bank(bk), k.flip, rawb[:, 2 * i:2 * i + 2, :].rearrange("p a b -> p (a b)"), start=True, stop=True))
        t = A.did(A.on(t).activation(BIA[:, 2 * i:2 * i + 2, :], k.bank(bk).rearrange("p (a b) -> p a b", a=2), ACT.Copy))
        mis.give(kk, t)
        tbia.append(t)

    ut = Ring([k.at(PH + 12 * KB, [8, 128]), k.at(PH + 16 * KB, [8, 128])])
    du = [k.dma() for _ in range(2)]
    uback = []
    udone = []
    for m in range(4):
        kk, ub, f = ut.take()
        toks = []

        def evac(half, ps, t, ub=ub, f=f, toks=toks, m=m):
            o = ub[:, :, 64 * half:64 * half + 64].rearrange("p j c -> p c j")
            t = A.did(A.on(t, f, tbia, trow).activation(o, ps.rearrange("p (c j) -> p c j", j=8), ACT.Copy))
            toks.append(t)
            return [t]

        k.proj_T(f"u{m}", 128, proj, evac, xr)
        t = du[m % 2].start(S, d["uscr"][128 * m:128 * m + 128], ub, toks)
        ut.give(kk, t)
        udone.append(t)
    Hb = k.H0
    n2 = 2 * KB
    UR = Ring([k.at(Hb + n2 * i, [4, 128]) for i in range(2)])
    UD = [k.dma() for _ in range(2)]
    TC, TS, M1, M2, M3, M4, WN, WT, WS = (k.at(Hb + n2 * (2 + i), [4, 128]) for i in range(9))
    PW = k.at(Hb + 22 * KB, [4, 9, 16])
    PS = k.at(Hb + 24 * KB + 512, [4, 9, 16])
    TP = k.at(Hb + 27 * KB, [4, 128])
    BP = k.at(Hb + 29 * KB, [3, 240])
    BP2 = k.at(O + 15 * KB + 64, [1, 240])
    bp = [BP[:, 0, :], BP[:, 1, :], BP[:, 2, :], BP2[:, 0, :]]
    tz = [G.did(G.on(xr, tneg).memset(BP, 0.0)), G.did(G.e.memset(BP2, 0.0))]
    yd = [k.dma() for _ in range(2)]
    tyd = []

    def ssm():
        prev = {}
        for n in range(8):
            gs = slice(4 * n, 4 * n + 4)
            kk, U, f = UR.take()
            for gi in range(4):
                g = 4 * n + gi
                tu = UD[n % 2].start(S, U[:, gi, :], d["uscr"][16 * g:16 * g + 16].rearrange("h j c -> j h c"), f, udone[n // 2], xr)
            t = V.did(V.on(tks, tset, prev.get("tcts"), xr).tensor_tensor(TS, bc(TH8[:, gs], 2, 128), bc(KS, 1, 4), ALU.mult))
            t = reduce_angle(V, TS, M1, [t, prev.get("m")])
            t = quarter(V, TC, TS, M1, t)
            t1 = A.did(A.on(t).activation(TS, TS, ACT.Sin))
            t2 = A.did(A.e.activation(TC, TC, ACT.Sin))
            ttab = [t1, t2]
            m3, m4 = M3.rearrange("p g (j h) -> p g j h", j=8), M4.rearrange("p g (j h) -> p g j h", j=8)
            ta = G.did(G.on(tset, prev.get("m34"), xr).tensor_tensor(m3, bc(QR[:, gs, :], 3, 16), bc(BB[:, gs, :], 2, 8), ALU.mult))
            tb = G.did(G.e.tensor_tensor(m4, bc(QI[:, gs, :], 3, 16), bc(BX[:, gs, :], 2, 8), ALU.mult))
            twn = G.did(G.on(ta, tb, prev.get("wn")).tensor_tensor(WN, M3, M4, ALU.add))
            ops = []
            for dst, x, y, op, key in ((PW, CC, CX, ALU.add, "pw"), (PS, CX, CC, ALU.subtract, "ps")):
                t = ops[-1] if ops else twn
                for s0, s1 in ((0, 5), (5, 9)):
                    ns = s1 - s0
                    a4 = M3.rearrange("p g (j h) -> p g j h", j=8)[:, :, 0:ns, :]
                    b4 = M4.rearrange("p g (j h) -> p g j h", j=8)[:, :, 0:ns, :]
                    ta = G.did(G.on(t).tensor_tensor(a4, bc(PR[:, gs, s0:s1], 3, 16), bc(x[:, gs, :], 2, ns), ALU.mult))
                    tb = G.did(G.e.tensor_tensor(b4, bc(PIm[:, gs, s0:s1], 3, 16), bc(y[:, gs, :], 2, ns), ALU.mult))
                    t = G.did(G.on(ta, tb, prev.get("y")).tensor_tensor(dst[:, :, s0:s1, :], a4, b4, op))
                ops.append(t)
            prev["m34"] = t
            tb = [G.did(G.on(tz, prev.get("toep")).tensor_copy(bp[gi][:, 112:128], BB[:, 4 * n + gi, :])) for gi in range(4)]
            yield
            yield
            yield
            kk_, bk, f = mis.take()
            for gi in range(4):
                P.on(f, twn, k.t_const)
                ins = k.tr(k.bank(bk)[:, 128 * gi:128 * gi + 128], WN[:, gi, :])
            t = P.did(ins)
            prev["wn"] = t
            b4 = k.bank(bk).rearrange("p (g m) -> p g m", g=4)
            A.on(t, prev.get("v"), xr)
            ta = A.did(A.e.activation(WT, b4, ACT.Copy))
            tb2 = A.did(A.e.activation(WS[:, :, 0:64], b4[:, :, 64:128], ACT.Copy))
            tc = A.did(A.e.activation(WS[:, :, 64:128], b4[:, :, 0:64], ACT.Copy, scale=-1.0))
            mis.give(kk_, tc)
            kk_, bk, f = mis.take()
            P.on(f, tb, ops[0])
            for gi in range(4):
                for j in range(8):
                    ins = k.mm(k.bank(bk)[:, 128 * gi + 16 * j:128 * gi + 128], bp[gi][:, 112 - 16 * j:240 - 16 * j],
                               PW[:, gi, 0:8 - j, :].rearrange("p s h -> p (s h)"), j == 0 and gi == 0, j == 7)
            t = P.did(ins)
            prev["toep"] = t
            ttp = A.did(A.on(t, prev.get("y"), xr).activation(TP, k.bank(bk).rearrange("p (g m) -> p g m", g=4), ACT.Copy))
            mis.give(kk_, ttp)
            yield
            k1, b1, f1 = mis.take()
            k2, b2, f2 = mis.take()
            P.on(ta, tb2, tc, tu, f1, f2)
            for wt, b_ in ((WT, b1), (WS, b2)):
                for gi in range(4):
                    ins = k.mm(k.bank(b_)[:, 128 * gi:128 * gi + 128], wt[:, gi, :], U[:, gi, :], gi == 0, True)
            t = P.did(ins)
            prev["v"] = t
            fl = lambda x: x.rearrange("p g m -> p (g m)")
            ta = V.did(V.on(t, ttab, prev.get("m")).tensor_tensor(fl(M1), k.bank(b1), fl(TC), ALU.mult))
            tb = V.did(V.e.tensor_tensor(fl(M2), k.bank(b2), fl(TS), ALU.mult))
            mis.give(k1, ta)
            mis.give(k2, tb)
            tw_ = V.did(V.on(ta, tb).tensor_tensor(fl(M1), fl(M1), fl(M2), ALU.add))
            tl_ = []
            for gi in range(4):
                tl_.append(V.did(V.on(tw_).tensor_tensor_scan(Z[:, gi, :], R8[:, 4 * n + gi:4 * n + gi + 1].to_broadcast([128, 128]),
                                                              M1[:, gi, :], 0.0, ALU.mult, ALU.add)))
            ta = V.did(V.on(*tl_, prev.get("y")).tensor_tensor(fl(M1), fl(Z), fl(TC), ALU.mult))
            tb = V.did(V.e.tensor_tensor(fl(M2), fl(Z), fl(TS), ALU.mult))
            prev["tcts"] = [ta, tb]
            yield
            yield
            kk_, bk, f = mis.take()
            P.on(f, ttp, ta, tb, ops)
            for gi in range(4):
                o = k.bank(bk)
                k.mm(o[:, 128 * gi:128 * gi + 128], TP[:, gi, :], U[:, gi, :], gi == 0, False)
                k.mm(o[:, 128 * gi + 1:128 * gi + 128], PW[:, gi, 1:9, :].rearrange("p s h -> p (s h)"), M1[:, gi, 0:127], False, False)
                ins = k.mm(o[:, 128 * gi + 1:128 * gi + 128], PS[:, gi, 1:9, :].rearrange("p s h -> p (s h)"), M2[:, gi, 0:127], False, True)
            t = P.did(ins)
            prev["y"] = prev["m"] = t
            V.on(t, tyd[-1] if tyd else None)
            ty = []
            for gi in range(4):
                ty.append(V.did(V.e.scalar_tensor_tensor(Y[:, gi, :], U[:, gi, :], k.sm("dsk")[:, 4 * n + gi:4 * n + gi + 1],
                                                         k.bank(bk)[:, 128 * gi:128 * gi + 128], ALU.mult, ALU.add)))
            mis.give(kk_, *ty)
            UR.give(kk, *ty)
            for gi in range(4):
                g = 4 * n + gi
                t = yd[n % 2].start(S, d["yscr"][16 * g:16 * g + 16].rearrange("h j c -> j h c"), Y[:, gi, :], ty)
            tyd.append(t)
            yield

    bg = ssm()

    def step(n=1):
        for _ in range(n):
            next(bg, None)

    step()
    tq = {}
    for m in range(4):
        def evac(half, ps, t, m=m):
            return k.qk_norm(ps, t, QT[:, m, 512 * half:512 * half + 512], k.sm("qg_ev"), k.bones, mis, sq, rt, 1.0 / 64,
                             [tsm, tbia, udone, trow, tset], lambda t: tq.update({(m, half): t}))
        k.proj_T(f"q{m}", 128, proj, evac, xr)
        step(2)
    tk, tv = {}, {}

    def evac(half, ps, t):
        return k.qk_norm(ps, t, KT[:, 512 * half:512 * half + 512], k.sm("kg_ev"), k.bones, mis, sq, rt, 1.0 / 64,
                         [tsm, udone], lambda t: tk.update({half: t}))
    k.proj_T("kk", 128, proj, evac, xr)
    step()
    for b in range(8):
        kk, bk, f = proj.take()
        P.on(f)
        t = P.did(k.rows("vv", b, k.bank(bk)[:, 0:128]))
        k.flush()
        tv[b] = A.did(A.on(t, udone).activation(VN[:, b, :], k.bank(bk)[:, 0:128], ACT.Copy))
        proj.give(kk, tv[b])
        if b % 4 == 3:
            step()
    k.done("vv", t)
    gdm = [k.dma() for _ in range(2)]
    tgs = {}
    for m in range(8):
        kk, gb_, f = gev.take()
        toks = []

        def evac(half, ps, t):
            toks.append(A.did(A.on(t, f, tset).activation(gb_[:, 512 * half:512 * half + 512], ps, ACT.Silu)))
            return [toks[-1]]
        tlast = k.proj_T(f"g{'ab'[m // 4]}{m % 4}", 128, proj, evac, xr)
        tgs[m] = gdm[m % 2].start(S, d["gscr"][128 * m:128 * m + 128], gb_, toks)
        gev.give(kk, tgs[m])
        step(2)

    X0 = k.X0
    GA, L = k.at(X0, [4, 1024]), Ring([k.at(X0 + 16 * KB + 4 * KB * i, [1024]) for i in range(3)])
    PT = Ring([k.at(X0 + 28 * KB, [2, 512]), k.at(PH + 56 * KB, [2, 512])])
    MH, ML = k.at(X0 + 32 * KB, [4, 1024], F32R), k.at(X0 + 48 * KB, [4, 1024], F32R)
    gtmp = Ring([k.at(PH + 60 * KB + 2 * KB * i, [4, 128]) for i in range(2)])
    for r in (L, PT, gtmp):
        r.free = [[tlast, tgs[6], tgs[7]] for _ in r.items]
    tga = k.dma().start(S, GA, d["gscr"][0:512].rearrange("(m p) t -> p m t", p=128), tlast, tgs[0], tgs[1], tgs[2], tgs[3])
    tgs_a = [tgs[6], tgs[7]]

    st = {}
    tsink = A.did(A.on(tsm).activation(k.tiny[:, 224:232], k.sm("sink"), ACT.Copy, scale=-1.0))
    smr = Ring([k.tiny[:, 64 + 16 * i:80 + 16 * i] for i in range(3)])

    def s1(b, h):
        nk, k0 = (256, 128 * b - 128) if b else (128, 0)
        lk, Lb, lf = L.take()
        sk, sb, sf = smr.take()
        hl = slice(64 * h, 64 * h + 64)
        tls = []
        for pair in range(2):
            kk, bk, f = mis.take()
            P.on(f, tq[2 * pair, b // 4], tq[2 * pair + 1, b // 4], tk[b // 4], tk[0])
            for i in range(2):
                m = 2 * pair + i
                ins = k.mm(k.bank(bk)[:, 256 * i:256 * i + nk], QT[hl, m, 128 * b:128 * b + 128], KT[hl, k0:k0 + nk], i == 0, True)
            t = P.did(ins)
            Lv = Lb.rearrange("p (m n) -> p m n", m=4)[:, 2 * pair:2 * pair + 2, 0:nk]
            ps = k.bank(bk).rearrange("p (m n) -> p m n", m=2)[:, :, 0:nk]
            t = V.did(V.on(t, lf, tbia).scalar_tensor_tensor(Lv, ps, 0.125, BIA[:, 4 * h + 2 * pair:4 * h + 2 * pair + 2, 256 - nk:256], ALU.mult, ALU.add))
            mis.give(kk, t)
            tls.append(t)
        Lv = Lb.rearrange("p (m n) -> p m n", m=4)[:, :, 0:nk]
        nm, rs, es, di = sb[:, 0:4], sb[:, 4:8], sb[:, 8:12], sb[:, 12:16]
        t = V.did(V.on(tls, sf).tensor_reduce(nm, Lv, AX.X, ALU.max, negate=True))
        t = V.did(V.on(t, tsink).tensor_tensor(nm, nm, k.tiny[:, 224 + 4 * h:228 + 4 * h], ALU.min))
        t0 = V.did(V.on(t).tensor_tensor(es, nm, k.tiny[:, 224 + 4 * h:228 + 4 * h], ALU.subtract))
        te = []
        A.on(t, t0)
        for m in range(4):
            te.append(A.did(A.e.activation(Lv[:, m], Lv[:, m], ACT.Exp, bias=nm[:, m:m + 1], accum_out=rs[:, m:m + 1])))
        te.append(A.did(A.e.activation(es, es, ACT.Exp)))
        st[b, h] = (nk, k0, lk, Lv, te, sk, sb)

    def s1b(b, h):
        nk, k0, lk, Lv, te, sk, sb = st[b, h]
        nm, rs, es, di = sb[:, 0:4], sb[:, 4:8], sb[:, 8:12], sb[:, 12:16]
        t = V.did(V.on(te).tensor_tensor(di, rs, es, ALU.add))
        t = V.did(V.on(t).reciprocal(di, di))
        ts = [V.did(V.on(t).tensor_scalar(Lv[:, m], Lv[:, m], di[:, m:m + 1], None, ALU.mult)) for m in range(4)]
        smr.give(sk, ts)
        st[b, h] = (nk, k0, lk, Lv, ts)

    def s2(b, h):
        nk, k0, lk, Lv, ts = st[b, h]
        pk, pt, pf = PT.take()
        nc_ = nk // 128
        tt = []
        for c in range(nc_):
            kk, bk, f = mis.take()
            P.on(f, ts)
            for m in range(4):
                ins = k.tr(k.bank(bk)[:, 128 * m:128 * m + 128], Lv[:, m, 128 * c:128 * c + 128])
            t = P.did(ins)
            if c == 1:
                t2 = V.did(V.on(t, pf).tensor_copy(pt[:, c, :], k.bank(bk)))
            else:
                t2 = A.did(A.on(t, pf).activation(pt[:, c, :], k.bank(bk), ACT.Copy))
            mis.give(kk, t2)
            tt.append(t2)
        L.give(lk, t)
        st[b, h] = (nk, k0, pk, pt, tt)

    tatt = []

    def s3(b, h):
        nk, k0, pk, pt, tt = st[b, h]
        hl = slice(64 * h, 64 * h + 64)
        kk, bk, f = mis.take()
        P.on(f, tt, tv[b], tv[max(b - 1, 0)])
        for c in range(nk // 128):
            ins = k.mm(k.bank(bk)[hl, :], VN[:, k0 // 128 + c, hl], pt[:, c, :], c == 0, c == nk // 128 - 1)
        t = P.did(ins)
        PT.give(pk, t)
        qs = slice(128 * b, 128 * b + 128)
        gk, gt, gf = gtmp.take()
        t = V.did(V.on(t, tga, gf).tensor_tensor(gt[hl], k.bank(bk)[hl, :].rearrange("p (m q) -> p m q", m=4), GA[hl, :, qs], ALU.mult))
        mis.give(kk, t)
        tt = k.parts(gt[hl], MH[hl, :, qs], ML[hl, :, qs], t, [tlast, tgs_a], eng=V)
        gtmp.give(gk, tt)
        tatt.extend(tt)

    units = [(b, h) for b in range(8) for h in range(2)]
    for i in range(len(units) + 3):
        if i < len(units):
            s1(*units[i])
        if 1 <= i <= len(units):
            s1b(*units[i - 1])
            step()
        if 2 <= i <= len(units) + 1:
            s2(*units[i - 2])
        if i >= 3:
            s3(*units[i - 3])
        step()
    step(99)

    YT = [k.at(Hb + 4 * KB * i, [8, 128]) for i in range(4)]
    GB = k.at(Hb + 16 * KB, [4, 1024])
    YF = k.at(PH, [2, 1024])
    YH, YL = k.at(X0, [4, 1024], F32R), k.at(X0 + 16 * KB, [4, 1024], F32R)
    SH, SL = k.at(PH + 8 * KB, [4, 1024], F32R), k.at(PH + 24 * KB, [4, 1024], F32R)
    sgr = Ring([k.at(PH + 40 * KB + 2 * KB * i, [512]) for i in range(4)])
    mk = k.mark()
    tyg = []
    dmy = k.dma()
    ty = [dmy.start(S, YT[m], d["yscr"][128 * m:128 * m + 128], tyd[-1], tyd[-2], mk) for m in range(4)]
    tgb = k.dma().start(S, GB, d["gscr"][512:1024].rearrange("(m p) t -> p m t", p=128), mk, tgs[4], tgs[5], tgs[6], tgs[7])
    for m in range(4):
        yf = YF[:, m % 2, :]
        t = A.did(A.on(ty[-1], mk, tyg[-4:-2]).activation(yf.rearrange("p (c j) -> p c j", j=8), YT[m].rearrange("p j c -> p c j"), ACT.Gelu_apprx_tanh))
        tyg += k.parts(yf, YH[:, m, :], YL[:, m, :], t, mk, eng=V)
    tmix = []
    for m in range(4):
        wh, wl, tw = k.chunk(f"glu{m}")
        for half in range(2):
            hs_ = slice(512 * half, 512 * half + 512)
            kk1, b1, f1 = mis.take()
            kk2, b2, f2 = mis.take()
            P.on(f1, f2, tw, tyg)
            for bk, col in ((b1, 128), (b2, 0)):
                for q_ in range(4):
                    ins = k.mm3(k.bank(bk), (wh[:, q_, col:col + 128], wl[:, q_, col:col + 128]), (YH[:, q_, hs_], YL[:, q_, hs_]), q_ == 0, q_ == 3)
                if bk == b1:
                    tg = P.did(ins)
            ta = tl = P.did(ins)
            sk, sb, sf = sgr.take()
            t = A.did(A.on(tg, sf, mk).activation(sb, k.bank(b1), ACT.Sigmoid, bias=k.sm("glub")[:, 4 + m:5 + m]))
            mis.give(kk1, t)
            t = V.did(V.on(t, ta, mk).scalar_tensor_tensor(sb, k.bank(b2), k.sm("glub")[:, m:m + 1], sb, ALU.add, ALU.mult))
            mis.give(kk2, t)
            t = V.did(V.on(t, tgb).tensor_tensor(sb, sb, GB[:, m, hs_], ALU.mult))
            tt = k.parts(sb, SH[:, m, hs_], SL[:, m, hs_], t, mk)
            sgr.give(sk, tt)
            tmix += tt
        k.done(f"glu{m}", tl)
    tx = k.dma().start(S, k.H, d["x"].rearrange("(b p) n -> p b n", p=128), tl, k.mark())
    free = [k.mark() for _ in range(8)]
    P.on(tatt, tmix)
    tH = {b: [] for b in range(8)}
    for h in range(2):
        def evac(b, ps, t):
            o = k.H[:, b, 512 * h:512 * h + 512]
            t = V.did(V.on(t, tx).tensor_tensor(o, ps, o, ALU.add))
            tH[b].append(t)
            return [t]
        k.wide(f"eo{h}", [("0", (MH, ML), 0), ("1", (MH, ML), 2), ("2", (SH, SL), 0), ("3", (SH, SL), 2)], evac, free, h == 1)
    return tH


def odd(k, tH):
    nc, d, V, A, P, G, S = k.nc, k.d, k.V, k.A, k.P, k.G, k.S
    PH = k.PH0
    mk0 = k.mark()
    QT = k.at(PH, [8, 1024])
    KT, VN = k.at(PH + 32 * KB, [2, 1024]), k.at(PH + 40 * KB, [8, 256])
    MK = k.at(PH + 48 * KB, [33 * 128], BF16)
    TN = k.at(PH + 48 * KB + 8448, [128])
    O = PH + 48 * KB + 8960
    sq1, rt1 = Ring([k.at(O, [512])]), Ring([k.at(O + 2 * KB, [512])])
    gev = Ring([k.at(O + 4 * KB, [1024])])
    mo = {b: sum(128 * (c + 1) for c in range(2, b)) for b in range(2, 9)}
    H0 = k.H0
    QI, KI = k.at(H0, [4, 1024]), k.at(H0 + 16 * KB, [1024])
    rel = Ring([k.at(H0 + 20 * KB + 2 * KB * i, [512]) for i in range(2)])
    scr = Ring([k.at(H0 + 24 * KB + 4 * KB * i, [1024]) for i in range(2)])
    WI = k.tiny[:, 128:192].rearrange("p (b n) -> p b n", b=8)
    m8 = k.tiny[:, 64:72]
    proj = Ring([0, 1, 2])
    mis = Ring([3, 4, 5, 6, 7])
    tsm = k.t_small

    XN = QT
    k.wjunk = mk0
    junk = k.at(PH + 32 * KB, [1024])
    ready = [k.rms_rows(k.H[:, b, :], b, XN[:, b, :], [tH[b], mk0], 1e-6, junk) for b in range(8)]
    dh = k.dma()
    tsp = dh.start(S, d["hscr"].rearrange("(b p) n -> p b n", p=128), k.H, [tH[b] for b in range(8)])
    xr = k.transpose_to(XN, mis, ready, scale=k.sm("g_od"), after=mk0)
    free = [tsp, ready]
    tjunk = k.wjunk
    t = G.did(G.on(mk0).memset(TN, 0.0))
    tTN = G.did(G.on(t).affine_select(out=TN, in_=TN, compare_op=ALU.is_ge, fill=NEG, base=0,
                                      pattern=[[-1, 128]], channel_multiplier=1))

    tqi, tki = {}, {}
    for m in range(4):
        def evac(half, ps, t, m=m):
            tqi[m, half] = A.did(A.on(t, free).activation(QI[:, m, 512 * half:512 * half + 512], ps, ACT.Copy))
            return [tqi[m, half]]
        k.proj_T(f"qi{m}", 128, proj, evac, xr)

    def evac(half, ps, t):
        tki[half] = A.did(A.on(t, free).activation(KI[:, 512 * half:512 * half + 512], ps, ACT.Copy))
        return [tki[half]]
    k.proj_T("ki", 128, proj, evac, xr)
    kk, bk, f = proj.take()
    P.on(f)
    for b in range(8):
        ins = k.rows("wi", b, k.bank(bk)[:, 8 * b:8 * b + 8], start=(b == 0))
    tl = P.did(ins)
    twi = A.did(A.on(tl, mk0).activation(WI, k.bank(bk)[:, 0:64].rearrange("p (b n) -> p b n", b=8), ACT.Copy, scale=8 ** -0.5))
    proj.give(kk, twi)
    k.done("wi", tl)

    scores, tmk = {}, {}

    def score(b):
        n = 128 * (b + 1)
        sk, sc, sf = scr.take()
        first = {}
        for h in range(8):
            hl = slice(64 * (h % 2), 64 * (h % 2) + 64)
            for c in range(0, n, 512):
                e = min(n, c + 512)
                kk, bk, f = mis.take()
                P.on(f, tqi[h // 2, b // 4], tki[0], tki[(e - 1) // 512])
                t = P.did(k.mm(k.bank(bk)[:, 0:e - c], QI[hl, h // 2, 128 * b:128 * b + 128], KI[hl, c:e], True, True))
                rk, rb, rf = rel.take()
                t = A.did(A.on(t, rf, free).activation(rb[:, 0:e - c], k.bank(bk)[:, 0:e - c], ACT.Relu, scale=0.125))
                mis.give(kk, t)
                wv = WI[:, b, h:h + 1]
                if h == 0:
                    t = V.did(V.on(t, sf, twi, free).tensor_scalar(sc[:, c:e], rb[:, 0:e - c], wv, None, ALU.mult))
                else:
                    t = V.did(V.on(t, first[c]).scalar_tensor_tensor(sc[:, c:e], rb[:, 0:e - c], wv, sc[:, c:e], ALU.mult, ALU.add))
                first[c] = t
                rel.give(rk, t)
            yield
        t = V.did(V.on(*first.values(), tTN).tensor_tensor(sc[:, n - 128:n], sc[:, n - 128:n], TN, ALU.add))
        scores[b] = (sk, sc, t)

    def select(b):
        n = 128 * (b + 1)
        sk, sc, t = scores[b]
        for r in range(32):
            t = V.did(V.on(t).max(m8, sc[:, 0:n]))
            t = V.did(V.on(t).match_replace(sc[:, 0:n], m8, sc[:, 0:n], -3e38))
            yield
        tmk[b] = V.did(V.on(t).tensor_scalar(MK[:, mo[b]:mo[b] + n], sc[:, 0:n], -2e38, NEG, ALU.is_gt, ALU.mult))
        scr.give(sk, tmk[b])
        yield

    order = [7, 6, 5, 4, 3, 2]

    def chain():
        yield from score(order[0])
        for i, b in enumerate(order):
            nxt = score(order[i + 1]) if i + 1 < 6 else iter(())
            for j, _ in enumerate(select(b)):
                if j % 3 == 0:
                    next(nxt, None)
                yield
            for _ in nxt:
                pass

    bg = chain()
    for _ in range(8):
        next(bg)

    def step(n):
        for _ in range(n):
            next(bg, None)

    for r in (sq1, rt1, gev):
        r.free = [list(mk0)]
    tk, tq, tv, tgs = {}, {}, {}, {}
    for m in range(2):
        def evac(half, ps, t, m=m):
            step(2)
            return k.qk_norm(ps, t, KT[:, m, 512 * half:512 * half + 512], k.sm("kg_od"), k.ones, mis, sq1, rt1, 1.0 / 128,
                             [tsm, tjunk], lambda t: tk.update({(m, half): t}))
        k.proj_T(f"ok{m}", 128, proj, evac, xr)
    qg = k.tiny[:, 80:81]
    tqg = V.did(V.on(tsm).tensor_scalar(qg, k.sm("qg_od"), 128 ** -0.5, None, ALU.mult))
    for m in range(8):
        def evac(half, ps, t, m=m):
            step(3)
            return k.qk_norm(ps, t, QT[:, m, 512 * half:512 * half + 512], qg, k.ones, mis, sq1, rt1, 1.0 / 128,
                             [tqg, xr], lambda t: tq.update({(m, half): t}))
        k.proj_T(f"oq{m}", 128, proj, evac, xr)
    for m in range(2):
        for b in range(8):
            kk, bk, f = proj.take()
            P.on(f)
            t = P.did(k.rows(f"ov{m}", b, k.bank(bk)[:, 0:128]))
            k.flush()
            tv[m, b] = A.did(A.on(t).activation(VN[:, b, 128 * m:128 * m + 128], k.bank(bk)[:, 0:128], ACT.Copy))
            proj.give(kk, tv[m, b])
            step(2)
        k.done(f"ov{m}", t)
    gdm = k.dma()
    for m in range(8):
        kk, gb_, f = gev.take()
        toks = []

        def evac(half, ps, t):
            step(3)
            toks.append(A.did(A.on(t, f).activation(gb_[:, 512 * half:512 * half + 512], ps, ACT.Silu)))
            return [toks[-1]]
        tlast = k.proj_T(f"og{m}", 128, proj, evac, xr)
        tgs[m] = gdm.start(S, d["gscr"][128 * m:128 * m + 128], gb_, toks)
        gev.give(kk, tgs[m])
    step(9999)

    mk = k.mark()
    X0 = k.X0
    strips = Ring([k.at(H0 + 4 * KB * i, [1024]) for i in range(2)])
    bms = Ring([k.at(H0 + 8 * KB + 4 * KB * i, [1024]) for i in range(2)])
    pr = Ring([k.at(H0 + 16 * KB + 4 * KB * i, [1024]) for i in range(3)])
    pts = Ring([k.at(X0, [4, 4, 128]), k.at(X0 + 8 * KB, [8, 4, 128])])
    gts = Ring([k.at(X0 + (24 + 4 * i) * KB, [1024]) for i in range(2)])
    MH, ML = k.at(PH, [8, 1024], F32R), k.at(X0 + 32 * KB, [8, 1024], F32R)
    smr = Ring([k.tiny[:, 128 + 8 * i:136 + 8 * i] for i in range(3)])
    pairs, ptb, avb = Ring([4, 6]), Ring([0, 1, 2]), Ring([3])
    for r in (strips, bms, pr, pts, gts, smr, pairs, ptb, avb):
        r.free = [list(mk) for _ in r.items]
    raws = Ring([k.at(H0 + 28 * KB, [1024])])
    raws.free = [list(mk)]
    sdm = k.dma()
    cur, st, tatt = {}, {}, []

    def load_strip(n):
        rk, rb, rf = raws.take()
        t = sdm.start(S, rb, bass.AP(d["strip"].tensor, n * (STRIP_A + STRIP_B) + STRIP_A, [[1, 128], [1, 1024]]), rf, k.t_strip)
        return rk, rb, t

    def turn_strip(n, raw):
        rk, rb, tr_ = raw
        sk, sb, sf = strips.take()
        toks = []
        for c in range(2):
            kk, bk, f = ptb.take()
            t = P.did(P.on(f, tr_).matmul(k.bank(bk), k.flip, rb[:, 512 * c:512 * c + 512], start=True, stop=True))
            t2 = A.did(A.on(t, sf).activation(sb[:, 512 * c:512 * c + 512], k.bank(bk), ACT.Copy))
            ptb.give(kk, t2)
            toks.append(t2)
        raws.give(rk, t)
        cur[n] = (sk, sb, toks, [])

    pend, gate = {}, {}
    gtd = [k.dma() for _ in range(2)]

    def load_gate(n):
        gk, g, gf = gts.take()
        gate[n] = (gk, g, gtd[n % 2].start(S, g, d["gscr"][128 * n:128 * n + 128], gf, tgs[n]))

    masked = {}

    def s0(n, b):
        nk = 128 * (b + 1)
        if n == 0 and b == 0:
            turn_strip(0, load_strip(0))
            load_gate(0)
        if n < 7 and b == 0:
            pend[n + 1] = load_strip(n + 1)
        if n < 7 and b == 5:
            load_gate(n + 1)
        if n < 7 and b == 5:
            turn_strip(n + 1, pend[n + 1])
        if b >= 2:
            sk, sb, tst, users = cur[n]
            bk_, bm, bf = bms.take()
            t = G.did(G.on(tst, bf, tmk[b]).tensor_tensor(bm[:, 0:nk], sb[:, 1024 - nk:1024], MK[:, mo[b]:mo[b] + nk], ALU.add))
            users.append(t)
            masked[n, b] = (bk_, bm[:, 0:nk], t)

    def s1(n, b):
        nk = 128 * (b + 1)
        sk, sb, tst, users = cur[n]
        win = sb[:, 1024 - nk:1024]
        if b >= 2:
            bk_, win, tst2 = masked.pop((n, b))
        else:
            tst2 = tst
        kk, bk, f = pairs.take()
        P.on(f)
        for c in range(0, nk, 512):
            e = min(nk, c + 512)
            P.on(tq[n, b // 4], tk[n // 4, 0], tk[n // 4, (e - 1) // 512])
            ins = k.mm(k.bank(bk + c // 512)[:, 0:e - c], QT[:, n, 128 * b:128 * b + 128], KT[:, n // 4, c:e], True, True)
        t = P.did(ins)
        pk, pb, pf = pr.take()
        mk_, sb_, sf = smr.take()
        p = pb[:, 0:nk]
        t = V.did(V.on(t, tst2, pf, sf).tensor_tensor_reduce(out=p, in0=k.bank(bk, 2)[:, 0:nk], in1=win, scale=1.0, scalar=-3e38,
                                                            op0=ALU.add, op1=ALU.max, accum_out=sb_[:, 0:1]))
        pairs.give(kk, t)
        if b >= 2:
            bms.give(bk_, t)
        else:
            users.append(t)
        if b == 7:
            strips.give(sk, users)
        t = V.did(V.on(t).tensor_scalar(sb_[:, 1:2], sb_[:, 0:1], -1.0, None, ALU.mult))
        t = A.did(A.on(t).activation(p, p, ACT.Exp, bias=sb_[:, 1:2], accum_out=sb_[:, 2:3]))
        st[n, b] = [t, pk, p, mk_, sb_]

    def s1b(n, b):
        t, pk, p, mk_, sb_ = st[n, b]
        t = V.did(V.on(t).reciprocal(sb_[:, 3:4], sb_[:, 2:3]))
        t = V.did(V.on(t).tensor_scalar(p, p, sb_[:, 3:4], None, ALU.mult))
        smr.give(mk_, t)
        st[n, b] = (t, pk, p)

    quad = {}

    def s2(n, b):
        t0, pk, p = st[n, b]
        Q = b // 4
        if b % 4 == 0:
            quad[n, Q] = [*pts.take(), []]
        qk, pt, qf, toks = quad[n, Q]
        for j0 in range(0, b + 1, 4):
            nj = min(4, b + 1 - j0)
            kk, bk, f = ptb.take()
            P.on(f, t0)
            for j in range(nj):
                ins = k.tr(k.bank(bk)[:, 128 * j:128 * j + 128], p[:, 128 * (j0 + j):128 * (j0 + j) + 128])
            t = P.did(ins)
            o = pt[:, j0:j0 + nj, b % 4, :]
            src = k.bank(bk)[:, 0:128 * nj].rearrange("p (j q) -> p j q", j=nj)
            if j0 == 0 and b % 4 != 3:
                t2 = A.did(A.on(t, qf).activation(o, src, ACT.Copy))
            else:
                t2 = V.did(V.on(t, qf).tensor_copy(o, src))
            ptb.give(kk, t2)
            toks.append(t2)
        pr.give(pk, t)

    def s3(n, Q):
        qk, pt, qf, toks = quad[n, Q]
        kk, bk, f = avb.take()
        P.on(f, toks, list(tv.values()))
        kv = n // 4
        last = 4 * Q + 3
        for j in range(last + 1):
            q0 = max(0, j - 4 * Q)
            ins = k.mm(k.bank(bk)[:, 128 * q0:512], VN[:, j, 128 * kv:128 * kv + 128],
                       pt[:, j, q0:4, :].rearrange("p q s -> p (q s)"), j == 0, j == last)
        t = P.did(ins)
        pts.give(qk, t)
        gk, g, tg = gate[n]
        o = slice(512 * Q, 512 * Q + 512)
        t = V.did(V.on(t, tg).tensor_tensor(g[:, o], k.bank(bk), g[:, o], ALU.mult))
        avb.give(kk, t)
        tt = k.parts(g[:, o], MH[:, n, o], ML[:, n, o], t, mk)
        tatt.extend(tt)
        if Q:
            gts.give(gk, tt, tatt[-4:-2])

    units = [(n, b) for n in range(8) for b in range(8)]
    s0(*units[0])
    for i in range(len(units) + 4):
        if i + 1 < len(units):
            s0(*units[i + 1])
        if i < len(units):
            s1(*units[i])
        if 1 <= i <= len(units):
            s1b(*units[i - 1])
        if i >= 4 and units[i - 4][1] % 4 == 3:
            s3(units[i - 4][0], units[i - 4][1] // 4)
        if 2 <= i <= len(units) + 1:
            s2(*units[i - 2])

    tx = k.dma().start(S, k.H, d["hscr"].rearrange("(b p) n -> p b n", p=128), tsp, k.mark())
    free = [list(k.mark()) for _ in range(8)]
    out = {b: [] for b in range(8)}
    P.on(tatt)
    for h in range(2):
        def evac(b, ps, t):
            o = k.H[:, b, 512 * h:512 * h + 512]
            t = V.did(V.on(t, tx).tensor_tensor(o, ps, o, ALU.add))
            out[b].append(t)
            return [t]
        k.wide(f"oo{h}", [(f"{i}", (MH, ML), 2 * i) for i in range(4)], evac, free, h == 1)
    return out


def second(k, tH, out_d):
    nc, d, V, A, P, G, S = k.nc, k.d, k.V, k.A, k.P, k.G, k.S
    PH, H0, X0 = k.PH0, k.H0, k.X0
    mk = k.mark()
    tsm = k.t_small
    XN = k.at(PH, [8, 1024])
    Q0 = PH + 32 * KB
    BT, CT, BN = k.at(Q0, [2, 1024]), k.at(Q0 + 8 * KB, [2, 1024]), k.at(Q0 + 16 * KB, [8, 256])
    cvr = Ring([k.at(Q0 + (24 + 4 * i) * KB, [1024]) for i in range(2)])
    cvd = [k.dma() for _ in range(2)]
    DT, AD = k.at(PH + 64 * KB, [8, 16]), k.at(PH + 64 * KB + 512, [8, 16])
    proj = Ring([0, 1, 2, 3])
    mis = Ring([4, 5, 6, 7])
    for r in (proj, mis, cvr):
        r.free = [list(mk) for _ in r.items]

    def row(i):
        return d["lnp"][i:i + 1, :].partition_broadcast(128)

    def bcast(i, off, after):
        ap = k.at(off, [1024])
        return ap, k.dma().start(S, ap, row(i), after)

    (g0, t0), (b0, t1), (bo, t2) = (bcast(i, PH + 4 * KB * j, mk) for j, i in enumerate((0, 1, 6)))
    G.on(mk)
    ready = [k.ln_rows(k.H[:, b, :], b, k.H[:, b, :], [tH[b], mk], 1e-5, g0, b0, [t0, t1]) for b in range(8)]
    xr = k.transpose_to(k.H, mis, ready, after=mk)
    tb = [V.did(V.on(ready[b], P.now(), t2).scalar_tensor_tensor(k.H[:, b, :], k.H[:, b, :], ALPHA, bo, ALU.mult, ALU.add)) for b in range(8)]
    tsp = k.dma().start(S, d["hscr"].rearrange("(b p) n -> p b n", p=128), k.H, tb)

    UP = 4352
    ur = Ring([k.at(H0 + UP * i, [1054]) for i in range(2)])
    sg = Ring([k.at(H0 + 2 * UP + 2 * KB * i, [512]) for i in range(2)])
    xp = Ring([k.at(H0 + 2 * UP + 4 * KB + 4224 * i, [1027]) for i in range(2)])
    tm = Ring([k.at(H0 + 2 * UP + 4 * KB + 2 * 4224 + 4 * KB * i, [1024]) for i in range(2)])
    tzero = [G.did(G.on(tsp).memset(u[:, 0:30], 0.0)) for u in ur.items] + [G.did(G.e.memset(x[:, 0:3], 0.0)) for x in xp.items]

    convq = []

    def conv(m, uk, u, tu):
        w = k.sm("cfw", 31 * m, 31 * m + 31)
        ck, o, cf = cvr.take()
        t = V.did(V.on(tu, tsm, cf).tensor_scalar(o, u[:, 0:1024], w[:, 0:1], k.sm("cfb")[:, m:m + 1], ALU.mult, ALU.add))
        yield
        for j in range(1, 31):
            t = V.did(V.on(t).scalar_tensor_tensor(o, u[:, j:j + 1024], w[:, j:j + 1], o, ALU.mult, ALU.add))
            if j < 30:
                yield
        tcv[m] = cvd[ck].start(S, d["cvscr"][128 * m:128 * m + 128], o, t)
        cvr.give(ck, tcv[m])
        ur.give(uk, t)
        yield

    tcv = {}

    def step(n):
        while n > 0 and convq:
            if next(convq[0], "end") == "end":
                convq.pop(0)
            else:
                n -= 1

    def glu(m):
        (gh, gl, tw), (ah, al, ta) = k.chunk(f"cb{m}"), k.chunk(f"ca{m}")
        while ur.free[(ur.k + 1) % 2] is None:
            step(1)
        uk, u, uf = ur.take()
        toks = []
        for half in range(2):
            hs = slice(512 * half, 512 * half + 512)
            k1_, b1, f1 = proj.take()
            P.on(f1, tw, ta, xr)
            for kk in range(8):
                ins = k.mm3(k.bank(b1), (gh[:, kk, :], gl[:, kk, :]), (k.XH[:, kk, hs], k.XL[:, kk, hs]), kk == 0, kk == 7)
            t = tg = P.did(ins)
            k.flush()
            sk, sb, sf = sg.take()
            t = A.did(A.on(t, sf, tsp).activation(sb, k.bank(b1), ACT.Sigmoid, bias=k.sm("bglu")[:, 8 + m:9 + m]))
            proj.give(k1_, t)
            k2_, b2, f2 = proj.take()
            P.on(f2)
            for kk in range(8):
                ins = k.mm3(k.bank(b2), (ah[:, kk, :], al[:, kk, :]), (k.XH[:, kk, hs], k.XL[:, kk, hs]), kk == 0, kk == 7)
            t2 = tl = P.did(ins)
            t = V.did(V.on(t, t2, uf, tzero).scalar_tensor_tensor(u[:, 30 + 512 * half:542 + 512 * half], k.bank(b2), k.sm("bglu")[:, m:m + 1],
                                                                  sb, ALU.add, ALU.mult))
            proj.give(k2_, t)
            sg.give(sk, t)
            toks.append(t)
            step(8)
        convq.append(conv(m, uk, u, toks))
        k.done(f"cb{m}", tg)
        k.done(f"ca{m}", tl)

    txn, tbt, tct, tbn = {}, {}, {}, {}

    def xbc(i):
        xk, x, xf = xp.take()
        toks = []

        def evac(half, ps, t):
            toks.append(A.did(A.on(t, xf, tzero).activation(x[:, 3 + 512 * half:515 + 512 * half], ps, ACT.Copy)))
            return [toks[-1]]
        k.proj_T(f"xb{i}", 128, proj, evac, xr)
        tk_, tmp, tf = tm.take()
        cw = k.sm("cxw", 4 * i, 4 * i + 4)
        t = V.did(V.on(toks, tf, tsm).tensor_scalar(tmp, x[:, 0:1024], cw[:, 0:1], k.sm("cxb")[:, i:i + 1], ALU.mult, ALU.add))
        for j in range(1, 4):
            t = V.did(V.on(t).scalar_tensor_tensor(tmp, x[:, j:j + 1024], cw[:, j:j + 1], tmp, ALU.mult, ALU.add))
        xp.give(xk, t)
        if i >= 8:
            dst = BT if i < 10 else CT
            t = A.did(A.on(t, mk).activation(dst[:, i % 2, :], tmp, ACT.Silu))
            tm.give(tk_, t)
            (tbt if i < 10 else tct)[i % 2] = t
            if i >= 10:
                return
            src = dst[:, i % 2, :]
        else:
            t = A.did(A.on(t).activation(tmp, tmp, ACT.Silu))
            src = tmp

        def turn():
            for half in range(2):
                kk, bk, f = mis.take()
                P.on(f, t)
                for j in range(4):
                    b = 4 * half + j
                    ins = k.tr(k.bank(bk)[:, 128 * j:128 * j + 128], src[:, 128 * b:128 * b + 128])
                t1 = P.did(ins)
                o = (XN[:, 4 * half:4 * half + 4, 128 * i:128 * i + 128] if i < 8 else
                     BN[:, 4 * half:4 * half + 4, 128 * (i - 8):128 * (i - 8) + 128])
                t2 = A.did(A.on(t1, tb).activation(o, k.bank(bk).rearrange("p (b n) -> p b n", b=4), ACT.Copy))
                mis.give(kk, t2)
                (txn if i < 8 else tbn)[i % 8, half] = t2
            if i < 8:
                tm.give(tk_, t1)
        k.late.append(turn)

    seq = list(XORDER)
    for m in range(8):
        glu(m)
        n = 2 if m % 2 == 0 else 1
        for _ in range(n):
            step(6)
            xbc(seq.pop(0))
            step(6)
        while len(convq) > 1:
            step(1)

    k.flush()
    kk, bk, f = mis.take()
    P.on(f, xr)
    for b in range(8):
        ins = k.rows("dt", b, k.bank(bk)[:, 16 * b:16 * b + 16], start=(b == 0))
    tl = P.did(ins)
    k.done("dt", tl)
    v8 = k.bank(bk)[:, 0:128].rearrange("p (b n) -> p b n", b=8)
    an = k.tiny[:, 224:240]
    t = V.did(V.on(tl, tsm, mk).tensor_tensor(DT, v8, bc(k.sm("dtb"), 1, 8), ALU.add))
    mis.give(kk, t)
    t1 = A.did(A.on(t).activation(AD, DT, ACT.Abs))
    t1 = A.did(A.on(t1).activation(AD, AD, ACT.Exp, scale=-1.0))
    t1 = A.did(A.on(t1).activation(AD, AD, ACT.Ln, bias=1.0))
    t3 = A.did(A.on(mk, ready).activation(an, k.sm("alog"), ACT.Exp))
    tdt = V.did(V.on(t1).scalar_tensor_tensor(DT, DT, 0.0, AD, ALU.max, ALU.add))
    tad = V.did(V.on(tdt, t3).scalar_tensor_tensor(AD, DT, -1.0, bc(an, 1, 8), ALU.mult, ALU.mult))

    zr = Ring([k.at(H0 + 2 * UP + 4 * KB + 2 * KB * i, [512]) for i in range(6)])
    zd = [k.dma() for _ in range(6)]
    mz = k.mark()
    zr.free = [list(mz) for _ in zr.items]
    free = [list(mz) for _ in range(8)]
    tz = {}
    for h in range(2):
        def evac(b, ps, t):
            zk, zb, zf = zr.take()
            t = A.did(A.on(t, zf).activation(zb, ps, ACT.Silu))
            tz[b, h] = zd[zk].start(S, d["zscr"][128 * b:128 * b + 128, 512 * h:512 * h + 512], zb, t)
            zr.give(zk, tz[b, h])
            step(3)
            return [t]
        k.wide(f"z{h}", [(f"{i}", None, 2 * i) for i in range(4)], evac, free)
    while convq:
        step(1)

    mk2 = [*k.mark(), *tz.values(), *tcv.values()]
    R = Ring([k.at(H0, [8, 128])])
    E = Ring([k.at(H0 + 4 * KB + 4 * KB * i, [8, 128]) for i in range(2)])
    XD = Ring([k.at(H0 + 12 * KB + 2 * KB * i, [8, 64]) for i in range(2)])
    XE = Ring([k.at(H0 + 16 * KB + 2 * KB * i, [8, 64]) for i in range(2)])
    YB = Ring([k.at(H0 + 20 * KB + 2 * KB * i, [8, 64]) for i in range(2)])
    ZS = Ring([k.at(H0 + 24 * KB + 2 * KB * i, [512]) for i in range(2)])
    PV = k.at(H0 + 28 * KB, [2, 8, 64])
    EX = Ring([k.tiny[:, 48 * i:48 * i + 48] for i in range(2)])
    CB = Ring([k.tiny[:, 96:224]])
    for r in (R, E, XD, XE, YB, ZS, EX, CB):
        r.free = [list(mk2) for _ in r.items]
    cgp, segp, one = Ring([0, 1]), Ring([2]), Ring([4, 5, 6, 7])
    for r in (cgp, segp, one):
        r.free = [list(mk2) for _ in r.items]
    zld = [k.dma() for _ in range(2)]
    tyn, tpv = {}, {0: None, 1: None}
    fl = lambda x: x.rearrange("p a b -> p (a b)")

    def chunk(c):
        ek, ex, ef = EX.take()
        kk, bk, f = one.take()
        P.on(f, tad, k.t_const)
        for i, m_ in enumerate((k.tle, k.tgt, k.ones)):
            ins = k.mm(k.bank(bk)[:, 16 * i:16 * i + 16], m_, AD[:, c, :], i == 0, i == 2)
        t = P.did(ins)
        tex = A.did(A.on(t, ef).activation(ex, k.bank(bk)[:, 0:48], ACT.Exp))
        one.give(kk, tex)
        return ek, ex, tex

    rr = []

    def ahead(i):
        if i < 16:
            rk, r, rf = R.take()
            a = AD[:, i // 2, 8 * (i % 2):8 * (i % 2) + 8]
            rr.append((rk, r, G.did(G.on(rf, tad, k.t_const).tensor_tensor(r, bc(a, 2, 128), bc(k.tle, 1, 8), ALU.mult))))

    def pre(c, g, ex, tex):
        s = {}
        cs = slice(128 * c, 128 * c + 128)
        hs = slice(8 * g, 8 * g + 8)
        rk, r, t = rr.pop()
        kk, bk, f = segp.take()
        P.on(t, f)
        for i in range(2):
            ins = k.mm(k.bank(bk + i), k.tgt, fl(r)[:, 512 * i:512 * i + 512], True, True)
        t = P.did(ins)
        R.give(rk, t)
        ahead(2 * c + g + 1)
        s["ek"], e, ef = E.take()
        te = A.did(A.on(t, ef).activation(fl(e), k.bank(bk, 2), ACT.Exp))
        segp.give(kk, te)
        kk, bk, f = one.take()
        P.on(f, tbt[g], tct[g])
        t = P.did(k.mm(k.bank(bk)[:, 0:128], BT[:, g, cs], CT[:, g, cs], True, True))
        ck, cb, cf = CB.take()
        t = V.did(V.on(t, cf).tensor_tensor(cb, k.bank(bk)[:, 0:128], k.tle, ALU.mult))
        one.give(kk, t)
        s["tE"] = V.did(V.on(t, te).tensor_tensor(e, e, bc(cb, 1, 8), ALU.mult))
        CB.give(ck, s["tE"])
        x = XN[:, c, 512 * g:512 * g + 512].rearrange("p (h q) -> p h q", h=8)
        s["xk"], xd, xf = XD.take()
        s["tx"] = V.did(V.on(xf, tdt, [txn[i, c // 4] for i in range(8)]).tensor_tensor(xd, x, bc(DT[:, c, hs], 2, 64), ALU.mult))
        s["yk"], y, yf = YB.take()
        s["tD"] = G.did(G.on(yf, [txn[i, c // 4] for i in range(8)]).tensor_tensor(y, x, bc(k.sm("dk2")[:, hs], 2, 64), ALU.mult))
        s["ak"], xe, af = XE.take()
        s["ta"] = G.did(G.on(s["tx"], tex, af).tensor_tensor(xe, xd, bc(ex[:, 16 + 8 * g:24 + 8 * g], 2, 64), ALU.mult))
        s.update(e=e, xd=xd, y=y, xe=xe, x=x, cs=cs)
        return s

    def zload(c, g, s):
        s["zk"], s["zs"], zf = ZS.take()
        s["tz"] = zld[s["zk"]].start(S, s["zs"], d["zscr"][128 * c:128 * c + 128, 512 * g:512 * g + 512], zf)

    cg, tcs = {}, {}

    def cgate(i):
        m, half = i // 2, i % 2
        if half == 0:
            cg[m] = cvr.take()
        ck, cb, cf = cg[m]
        wh, wl, tw = k.chunk(f"cg{m}")
        kk, bk, f = cgp.take()
        P.on(f, tw)
        hs = slice(512 * half, 512 * half + 512)
        for j in range(8):
            ins = k.mm3(k.bank(bk), (wh[:, j, :], wl[:, j, :]), (k.XH[:, j, hs], k.XL[:, j, hs]), j == 0, j == 7)
        t = P.did(ins)
        t2 = A.did(A.on(t, cf).activation(cb[:, hs], k.bank(bk), ACT.Copy))
        cgp.give(kk, t2)
        if half:
            k.done(f"cg{m}", t)
            tcs[m] = cvd[ck].start(S, d["cgscr"][128 * m:128 * m + 128], cb, t2)
            cvr.give(ck, tcs[m])

    def post(c, g, ex, tex, s):
        e, xd, y, xe, x = s["e"], s["xd"], s["y"], s["xe"], s["x"]
        kk, bk, f = one.take()
        P.on(f, s["tE"], s["tx"])
        for h in range(8):
            ins = k.mm(k.bank(bk)[:, 64 * h:64 * h + 64], e[:, h, :], xd[:, h, :], h == 0, True)
        t = P.did(ins)
        XD.give(s["xk"], t, s["ta"])
        t = ty = V.did(V.on(t, s["tD"]).tensor_tensor(y, y, k.bank(bk).rearrange("p (h q) -> p h q", h=8), ALU.add))
        one.give(kk, t)
        if c:
            kk, bk, f = one.take()
            P.on(f, tpv[g])
            t = P.did(k.mm(k.bank(bk), CT[:, g, s["cs"]], fl(PV[:, g]), True, True))
            tpr = t
            t = V.did(V.on(t, tex, ty).tensor_tensor(e[:, :, 0:64], k.bank(bk).rearrange("p (h q) -> p h q", h=8), bc(ex[:, 8 * g:8 * g + 8], 2, 64), ALU.mult))
            one.give(kk, t)
            t = V.did(V.on(t).tensor_tensor(y, y, e[:, :, 0:64], ALU.add))
        E.give(s["ek"], t)
        t0 = t
        kk, bk, f = one.take()
        P.on(f, s["ta"], tbn[g, c // 4])
        t = P.did(k.mm(k.bank(bk), BN[:, c, 128 * g:128 * g + 128], fl(xe), True, True))
        XE.give(s["ak"], t)
        pv = PV[:, g]
        if c == 0:
            tpv[g] = A.did(A.on(t).activation(fl(pv), k.bank(bk), ACT.Copy))
        else:
            t1 = G.did(G.on(tex, tpr, tpv[g]).tensor_tensor(pv, pv, bc(ex[:, 32 + 8 * g:40 + 8 * g], 2, 64), ALU.mult))
            tpv[g] = V.did(V.on(t, t1).tensor_tensor(fl(pv), fl(pv), k.bank(bk), ALU.add))
        one.give(kk, tpv[g])
        t = V.did(V.on(t0, s["tz"]).tensor_tensor(fl(y), fl(y), s["zs"], ALU.mult))
        ss = k.tiny[:, 240 + 2 * g:241 + 2 * g]
        rs = k.tiny[:, 241 + 2 * g:242 + 2 * g]
        t = A.did(A.on(t, tyn.get((c - 1, g))).activation(s["zs"], fl(y), ACT.Square, accum_out=ss))
        ZS.give(s["zk"], t)
        t = G.did(G.on(t).tensor_scalar(rs, ss, 1.0 / 512, 1e-5, ALU.mult, ALU.add))
        t = G.did(G.on(t).tensor_tensor(ss, rs, k.mhalf[:, 0:1], ALU.pow))
        t = V.did(V.on(t, s["tx"], s["tD"]).tensor_scalar(XN[:, c, 512 * g:512 * g + 512], fl(y), ss, None, ALU.mult))
        YB.give(s["yk"], t)
        tyn[c, g] = t
        return t

    prev = None
    ahead(0)
    for c in range(8):
        ek, ex, tex = chunk(c)
        for g in range(2):
            s = pre(c, g, ex, tex)
            zload(c, g, s)
            cgate(2 * c + g)
            if prev is not None:
                post(*prev)
                if prev[1] == 1:
                    EX.give(pek, V.now(), G.now())
            prev = (c, g, ex, tex, s)
        pek = ek
    post(*prev)

    mk3 = [*k.mark(), *tcs.values()]
    CV, CH, CL = k.at(H0, [8, 1024]), k.at(H0, [8, 1024], F32R), k.at(PH, [8, 1024], F32R)
    MU, RS = k.at(Q0, [1024]), k.at(Q0 + 4 * KB, [1024])
    sq = Ring([k.at(Q0 + 8 * KB + 4 * KB * i, [1024]) for i in range(2)])
    cgr = Ring([k.at(Q0 + 16 * KB + 4 * KB * i, [1024]) for i in range(4)])
    mis = Ring([4, 5, 6, 7])
    for r in (mis, sq, cgr):
        r.free = [list(mk3) for _ in r.items]
    tld = [k.dma().start(S, CV[:, 2 * i:2 * i + 2, :], d["cvscr"][256 * i:256 * i + 256].rearrange("(m p) t -> p m t", p=128), mk3) for i in range(4)]
    cgd = [k.dma() for _ in range(4)]
    cgb = {}

    def load_cg(m):
        ck, cb, cf = cgr.take()
        cgb[m] = (ck, cb, cgd[ck].start(S, cb, d["cgscr"][128 * m:128 * m + 128], cf, tcs[m]))

    for m in range(4):
        load_cg(m)
    tmu = []
    P.on(mk3)
    for m in range(8):
        P.on(tld[m // 2])
        for half in range(2):
            ins = k.mm(k.bank(half), k.ones, CV[:, m, 512 * half:512 * half + 512], m == 0, m == 7)
    t = P.did(ins)
    for half in range(2):
        tmu.append(A.did(A.on(t, mk3).activation(MU[:, 512 * half:512 * half + 512], k.bank(half), ACT.Copy, scale=1.0 / 1024)))
    tc2 = [G.did(G.on(tmu).tensor_tensor(CV[:, m, :], CV[:, m, :], MU, ALU.subtract)) for m in range(8)]
    ts = k.transpose_to(XN, mis, [[tyn[b, 0], tyn[b, 1]] for b in range(8)], scale=k.sm("sng"))
    ttr = P.now()
    epc = k.tiny[:, 250:251]
    te = G.did(nc.gpsimd.memset(epc, 1e-5))
    for m in range(8):
        sk, sb, sf = sq.take()
        t = A.did(A.on(tc2[m], sf).activation(sb, CV[:, m, :], ACT.Square))
        P.on(t)
        for half in range(2):
            ins = k.mm(k.bank(2 + half), k.ones, sb[:, 512 * half:512 * half + 512], m == 0, m == 7)
        t = P.did(ins)
        sq.give(sk, t)
    tr_ = []
    for half in range(2):
        o = RS[:, 512 * half:512 * half + 512]
        t1 = A.did(A.on(t, te, mk3).activation(o, k.bank(2 + half), ACT.Sqrt, bias=epc, scale=1.0 / 1024))
        tr_.append(V.did(V.on(t1).reciprocal(o, o)))
    tcf = []
    for m in range(8):
        ck, cb, tg = cgb[m]
        t = V.did(V.on(tr_).tensor_tensor(CV[:, m, :], CV[:, m, :], RS, ALU.mult))
        t2 = A.did(A.on(tg).activation(cb, cb, ACT.Silu))
        t = A.did(A.on(t).activation(CV[:, m, :], CV[:, m, :], ACT.Silu, scale=k.sm("clg")[:, m:m + 1], bias=k.sm("clb")[:, m:m + 1]))
        t = V.did(V.on(t, t2).tensor_tensor(cb, CV[:, m, :], cb, ALU.mult))
        tt = k.parts(cb, CH[:, m, :], CL[:, m, :], t, ttr)
        cgr.give(ck, tt)
        tcf += tt
        if m < 4:
            load_cg(m + 4)

    HN = k.at(Q0, [8, 1024])
    tx = k.dma().start(S, HN, d["hscr"].rearrange("(b p) n -> p b n", p=128), tsp, tcf, tr_, P.now())
    P.on(ts)
    tO = {b: [] for b in range(8)}
    free = [[*tr_, t1, *mis.free[0], *mis.free[1], *mis.free[2], *mis.free[3], *tmu] for _ in range(8)]
    first = [("%d" % i, None, 2 * i) for i in range(4)]
    second_ = [("%d" % (i + 4), (CH, CL), 2 * i) for i in range(4)]
    for h in range(2):
        def evac(b, ps, t):
            o = HN[:, b, 512 * h:512 * h + 512]
            t = V.did(V.on(t, tx).tensor_tensor(o, o, ps, ALU.add))
            tO[b].append(t)
            return [t]
        k.wide(f"so{h}", first + second_, evac, free, h == 1, mid=tcf)

    mk4 = k.mark()
    PTt, PTH, PTL = k.at(H0, [2, 1024]), k.at(H0 + 8 * KB, [2, 1024], F32R), k.at(H0 + 16 * KB, [2, 1024], F32R)
    PP = k.at(PH, [8, 1024])
    tpt = k.dma().start(S, PTt, d["pT"].rearrange("p (k t) -> p k t", k=2), mk4)
    (g1, t1), (b1, t2) = (bcast(i, H0 + (24 + 4 * j) * KB, mk4) for j, i in enumerate((2, 3)))
    tpp = [k.parts(PTt[:, i, :], PTH[:, i, :], PTL[:, i, :], tpt, mk4, eng=G) for i in range(2)]
    A.on(mk4)
    tpe = {}
    for h in range(2):
        for b in range(8):
            P.on(free[b], tpp)
            t = P.did(k.rows(f"pp{h}", b, k.bank(b), X=(PTH, PTL)))
            tpe[b, h] = A.did(A.on(t, mk4).activation(PP[:, b, 512 * h:512 * h + 512], k.bank(b), ACT.Copy))
            free[b] = [tpe[b, h]]
        k.done(f"pp{h}", t)
    ready = [k.ln_rows(HN[:, b, :], b, HN[:, b, :], tO[b], 1e-5, g1, b1, [t1, t2]) for b in range(8)]
    mis.free = [free[b] for b in (4, 5, 6, 7)]
    xr = k.transpose_to(HN, mis, ready, after=mk4)
    for i, b in enumerate((4, 5, 6, 7)):
        free[b] = mis.free[i]

    (g2, t3), (b2, t4) = (bcast(i, H0 + 4 * j * KB, [t, tpp]) for j, i in enumerate((4, 5)))
    sgr = Ring([k.at(H0 + 8 * KB + 2 * KB * i, [512]) for i in range(6)])
    for i in range(6):
        sgr.free[i] = [t]
    touts = k.dma()
    P.on(xr)
    for h in range(2):
        def evac(b, ps, t):
            sk, sb, sf = sgr.take()
            ta = A.did(A.on(t, sf).activation(sb, ps, ACT.Sigmoid))
            t = V.did(V.on(ta, tpe[b, h]).tensor_tensor(sb, sb, PP[:, b, 512 * h:512 * h + 512], ALU.mult))
            o = HN[:, b, 512 * h:512 * h + 512]
            t = V.did(V.on(t, ready).scalar_tensor_tensor(o, o, ALPHA, sb, ALU.mult, ALU.add))
            sgr.give(sk, t)
            tO[b].append(t)
            if h:
                t = k.ln_rows(HN[:, b, :], b, HN[:, b, :], tO[b][-2:], 1e-5, g2, b2, [t3, t4])
                tO["end"] = touts.start(S, out_d[128 * b:128 * b + 128, :], HN[:, b, :], t)
            return [ta]
        k.wide(f"pg{h}", [(f"{i}", None, 2 * i) for i in range(4)], evac, free, h == 1)
    S.on(tO["end"])


def dump(k, out, ready):
    t = k.mark()
    o = k.dma().start(k.S, out.rearrange("(b p) n -> p b n", p=128), k.H, t)
    k.S.on(o)


def host(inp):
    a = {n: np.asarray(v) for n, v in inp.items()}
    out = {}

    P = {}

    def pan(name, w):
        kk, n = w.shape
        P[name] = w.reshape(kk // 128, 128, n).transpose(1, 0, 2).reshape(-1)

    def tiles(name, w, n):
        for i in range(n):
            pan(f"{name}{i}", w[:, 128 * i:128 * i + 128])

    def wide(name, w):
        for h in range(2):
            for i in range(w.shape[0] // 256):
                pan(f"{name}{h}{i}", w[256 * i:256 * i + 256, 512 * h:512 * h + 512])

    w = a["ev_w_in"][0]
    perm = np.concatenate([np.r_[64 * m:64 * m + 64, 64 * (m + 4):64 * (m + 4) + 64] for m in range(4)])
    q, kv, ga, u, gb = w[:, 0:512], w[:, 512:768], w[:, 768:1280], w[:, 1280:1792], w[:, 1792:2304]
    tiles("u", u, 4)
    tiles("q", q[:, perm], 4)
    pan("kk", kv[:, 0:128])
    pan("vv", kv[:, 128:256])
    tiles("ga", ga[:, perm], 4)
    tiles("gb", gb, 4)
    w = a["ev_glu_w"][0]
    for m in range(4):
        pan(f"glu{m}", np.concatenate([w[:, 128 * m:128 * m + 128], w[:, 512 + 128 * m:640 + 128 * m]], 1))
    wo = a["ev_w_out"][0]
    wide("eo", np.concatenate([wo[0:512][perm], wo[512:]], 0))
    w = a["od_w_in"][0]
    q, ok, ov, g, qi, ki, wi = np.split(w, np.cumsum([1024, 256, 256, 1024, 512, 64]), axis=1)
    tiles("qi", qi, 4)
    pan("ki", np.concatenate([ki, ki], 1))
    pan("wi", wi)
    tiles("ok", ok, 2)
    tiles("oq", q, 8)
    tiles("ov", ov, 2)
    tiles("og", g, 8)
    wide("oo", a["od_w_out"][0])
    w = a["w_in_2"][0]
    xs, z, bm, cm, dt, ga_, gb_, cg = np.split(w, np.cumsum([1024, 1024, 256, 256, 16, 1024, 1024]), axis=1)
    tiles("xb", np.concatenate([xs, bm, cm], 1), 12)
    tiles("ca", ga_, 8)
    tiles("cb", gb_, 8)
    pan("dt", dt)
    wide("z", z)
    tiles("cg", cg, 8)
    wide("so", a["w_out_2"][0])
    wide("pg", a["w_ple_gate_2"][0])
    for h in range(2):
        pan(f"pp{h}", a["w_ple_proj_2"][0][:, 512 * h:512 * h + 512])
    out["w"] = np.concatenate([P[n] for n, _, _ in PANELS])

    def col(v):
        return v.reshape(-1, 128).T

    sm = {}
    sm["g_ev"], sm["g_od"] = col(a["norm_g"][0]), col(a["norm_g"][1])
    sm["qg_ev"] = np.tile(a["ev_q_norm_g"][0], 2)[:, None]
    sm["kg_ev"] = np.tile(a["ev_k_norm_g"][0], 2)[:, None]
    sm["sink"] = np.tile(a["ev_sinks"][0][None], (128, 1))
    sm["ldt"] = np.tile(a["ev_ssm_log_dt"][0][None], (128, 1))
    sm["are"] = np.tile(a["ev_ssm_a_re"][0].T, (2, 1))
    sm["aim"] = np.tile(a["ev_ssm_a_im"][0].T, (2, 1))
    sm["dsk"] = np.tile(a["ev_ssm_d"][0].T, (8, 1))
    sm["glub"] = col(a["ev_glu_b"][0])
    sm["qg_od"], sm["kg_od"] = a["od_q_norm_g"][0][:, None], a["od_k_norm_g"][0][:, None]
    cw, cb = a["ssm_conv_w_2"][0], a["ssm_conv_b_2"][0]
    sm["cxw"] = cw.T.reshape(12, 128, 4).transpose(1, 0, 2).reshape(128, 48)
    sm["cxb"] = col(cb)
    sm["dtb"] = np.tile(a["dt_bias_2"][0][None], (128, 1))
    sm["alog"] = np.tile(a["a_log_2"][0][None], (128, 1))
    sm["dk2"] = np.tile(a["d_skip_2"][0][None], (128, 1))
    sm["sng"] = col(a["ssm_norm_g_2"][0])
    sm["bglu"] = col(a["b_glu_2"][0])
    sm["cfw"] = a["conf_conv_w_2"][0].T.reshape(8, 128, 31).transpose(1, 0, 2).reshape(128, 248)
    sm["cfb"], sm["clg"], sm["clb"] = col(a["conf_conv_b_2"][0]), col(a["conf_ln_g_2"][0]), col(a["conf_ln_b_2"][0])
    out["small"] = np.ascontiguousarray(np.concatenate([sm[n] for n in SMALL], 1))
    br, bi = (a[f"ev_ssm_b_{x}"][0].transpose(1, 0, 2).reshape(64, 512) for x in ("re", "im"))
    cr, ci = (a[f"ev_ssm_c_{x}"][0].transpose(2, 0, 1).reshape(64, 512) for x in ("re", "im"))
    out["ssmw"] = np.ascontiguousarray(np.tile(np.concatenate([br, bi, cr, ci], 1), (2, 1)))
    out["x"] = np.ascontiguousarray(a["x"][0])
    out["pT"] = np.ascontiguousarray(a["p_2"][0, 0].T.reshape(2, 128, 1024).transpose(1, 0, 2).reshape(128, 2048))
    out["rb"] = np.ascontiguousarray(a["rel_bias"])
    out["lnp"] = np.ascontiguousarray(np.stack([a["ln_emb_g_2"], a["ln_emb_b_2"], a["ln1_g_2"][0], a["ln1_b_2"][0],
                                                a["ln2_g_2"][0], a["ln2_b_2"][0], a["b_out_2"][0]]))
    out["ohA"], out["ohB"] = onehots()
    return out


def bucket(n):
    if n < 16:
        return n
    b = 16
    while b < 31 and n ** 8 >= 2 ** (4 * 8 + 3 * (b - 15)):
        b += 1
    return b


def onehots():
    A_ = np.zeros((33, STRIP_A), np.float32)
    B_ = np.zeros((33, STRIP_B), np.float32)
    for x in range(STRIP_A):
        dist = 255 - x
        A_[bucket(dist) if 0 <= dist < 128 else 32, x] = 1
    for x in range(STRIP_B):
        dist = 1023 - x
        B_[bucket(dist) if dist >= 0 else 32, x] = 1
    return A_, B_


SHAPES = {"x": (1024, 1024), "ssmw": (128, 2048), "small": (128, SM_COLS), "rb": (32, 8), "ohA": (33, STRIP_A),
          "ohB": (33, STRIP_B), "pT": (128, 2048), "lnp": (7, 1024)}
SHAPES["w"] = (128 * CH_COLS,)
SCRATCH = {"gscr": (1024, 1024), "zscr": (1024, 1024), "cvscr": (1024, 1024), "cgscr": (1024, 1024), "strip": (8, STRIP_A + STRIP_B), "uscr": (512, 8, 128), "yscr": (512, 8, 128), "hscr": (1024, 1024)}


def drams(nc, names):
    d = {n: nc.dram_tensor(f"in_{n}", SHAPES[n], F32, kind="ExternalInput").ap() for n in names}
    for n, s in SCRATCH.items():
        d[n] = nc.dram_tensor(f"scr_{n}", s, F32, kind="Internal").ap()
    return d


def build(nc, d, out):
    k = K(nc, d, EVEN_P + ODD_P + SEC_P)
    k.setup()
    tH = even(k)
    tH = odd(k, tH)
    second(k, tH, out)


def kernel(**inputs):
    import concourse.bacc as _bacc
    from concourse.bass_utils import run_bass_kernel_spmd as _run

    arrays = {f"in_{n}": v for n, v in host(inputs).items()}
    nc = _bacc.Bacc("TRN2", target_bir_lowering=False, num_devices=1)
    d = drams(nc, list(SHAPES))
    out = nc.dram_tensor("out_0_dram", (1024, 1024), F32, kind="ExternalOutput").ap()
    build(nc, d, out)
    r = _run(nc, [arrays], core_ids=[0])
    return np.asarray(r.results[0]["out_0_dram"]).reshape(1, 1024, 1024)
```
